# Optimizing a Trainium2 kernel written in Bass

```python
import jax, jax.numpy as jnp
from jax import lax
import numpy as np

D_MODEL = 1024
BATCH = 1
SEQ = 512
DEPTH = 1

N_META = 16
ATTN_HEADS = 8
ATTN_HEAD_DIM = 64
ATTN_WIDTH = ATTN_HEADS * ATTN_HEAD_DIM
IDX_HEADS = 8
IDX_HEAD_DIM = 64
IDX_SCALE = (IDX_HEADS ** -0.5) * (IDX_HEAD_DIM ** -0.5)
ATTN_SCALE = ATTN_HEAD_DIM ** -0.5
TOPK_MAX = 256
Q_BLOCK = 128
HGRN_HEADS = 4
HGRN_KEY_DIM = 128
HGRN_VAL_DIM = 128
HGRN_WIDTH = HGRN_HEADS * HGRN_VAL_DIM
CHUNK = 64
MIX_WIDTH = ATTN_WIDTH + HGRN_WIDTH
IN_WIDTH = 4 * ATTN_WIDTH + IDX_HEADS * IDX_HEAD_DIM + IDX_HEAD_DIM + IDX_HEADS + 4 * HGRN_WIDTH
ROPE_THETA = 500000.0
ROPE_FRACTION = 4
EPS = 1e-6

kernel_name = "hymba_dsa_hgrn2_hybrid"

def rms_norm(x, g):
    xf = x.astype(jnp.float32)
    y = xf * lax.rsqrt(jnp.mean(xf * xf, axis=-1, keepdims=True) + EPS)
    return (y * g.astype(jnp.float32)).astype(x.dtype)

def layer_norm(x, g, b):
    xf = x.astype(jnp.float32)
    mu = jnp.mean(xf, axis=-1, keepdims=True)
    var = jnp.mean((xf - mu) ** 2, axis=-1, keepdims=True)
    y = (xf - mu) * lax.rsqrt(var + EPS)
    return (y * g.astype(jnp.float32) + b.astype(jnp.float32)).astype(x.dtype)

def rope_tables(T, head_dim):
    r = head_dim // ROPE_FRACTION
    half = r // 2
    inv = ROPE_THETA ** (-jnp.arange(half, dtype=jnp.float32) * 2.0 / r)
    ang = jnp.arange(T, dtype=jnp.float32)[:, None] * inv[None, :]
    return jnp.cos(ang)[:, None, :], jnp.sin(ang)[:, None, :]

def partial_rope(x, cos, sin):
    d = x.shape[-1]
    r = d // ROPE_FRACTION
    half = r // 2
    x1 = x[..., :half].astype(jnp.float32)
    x2 = x[..., half:r].astype(jnp.float32)
    rot = jnp.concatenate([x1 * cos - x2 * sin, x2 * cos + x1 * sin], axis=-1)
    return jnp.concatenate([rot.astype(x.dtype), x[..., r:]], axis=-1)

def split_columns(proj):
    sizes = [ATTN_WIDTH] * 4 + [IDX_HEADS * IDX_HEAD_DIM, IDX_HEAD_DIM, IDX_HEADS] + [HGRN_WIDTH] * 4
    points = np.cumsum(sizes)[:-1].tolist()
    return jnp.split(proj, points, axis=-1)

def sparse_attention(aq, ak, av, iq, ik, iw, idx_k_g, idx_k_b):
    B, T, _ = aq.shape
    S = T - N_META
    cos, sin = rope_tables(T, ATTN_HEAD_DIM)
    q = partial_rope(aq.reshape(B, T, ATTN_HEADS, ATTN_HEAD_DIM), cos, sin)
    k = partial_rope(ak.reshape(B, T, ATTN_HEADS, ATTN_HEAD_DIM), cos, sin)
    v = av.reshape(B, T, ATTN_HEADS, ATTN_HEAD_DIM)
    icos, isin = rope_tables(T, IDX_HEAD_DIM)
    qi = partial_rope(iq.reshape(B, T, IDX_HEADS, IDX_HEAD_DIM), icos, isin)
    ki = partial_rope(layer_norm(ik, idx_k_g, idx_k_b)[:, :, None, :], icos, isin)[:, :, 0, :]

    q_m, k_m, v_m = q[:, :N_META], k[:, :N_META], v[:, :N_META]
    s_m = jnp.einsum('bqhd,bkhd->bhqk', q_m, k_m).astype(jnp.float32) * ATTN_SCALE
    meta_causal = jnp.tril(jnp.ones((N_META, N_META), dtype=bool))
    s_m = jnp.where(meta_causal[None, None], s_m, -jnp.inf)
    p_m = jax.nn.softmax(s_m, axis=-1).astype(v.dtype)
    o_m = jnp.einsum('bhqk,bkhd->bqhd', p_m, v_m)

    q_r, k_r, v_r = q[:, N_META:], k[:, N_META:], v[:, N_META:]
    qi_r, ki_r, iw_r = qi[:, N_META:], ki[:, N_META:], iw[:, N_META:]
    n_blocks = S // Q_BLOCK
    topk = min(TOPK_MAX, S // 4)
    key_pos = jnp.arange(S)

    def to_blocks(a):
        return jnp.moveaxis(a.reshape((B, n_blocks, Q_BLOCK) + a.shape[2:]), 1, 0)

    def block_fn(args):
        blk, qb, qib, wb = args
        r = blk * Q_BLOCK + jnp.arange(Q_BLOCK)
        rel = jax.nn.relu(jnp.einsum('bqhd,bsd->bqhs', qib, ki_r))
        score = jnp.einsum('bqhs,bqh->bqs', rel, wb).astype(jnp.float32) * IDX_SCALE
        admissible = key_pos[None, :] <= r[:, None]
        score = jnp.where(admissible[None], score, -jnp.inf)
        _, sel = lax.top_k(score, topk)
        valid = sel <= r[None, :, None]
        k_sel = jax.vmap(lambda kb, ib: kb[ib])(k_r, sel)
        v_sel = jax.vmap(lambda vb, ib: vb[ib])(v_r, sel)
        s_sel = jnp.einsum('bqhd,bqkhd->bhqk', qb, k_sel).astype(jnp.float32) * ATTN_SCALE
        s_sel = jnp.where(valid[:, None], s_sel, -jnp.inf)
        s_meta = jnp.einsum('bqhd,bmhd->bhqm', qb, k_m).astype(jnp.float32) * ATTN_SCALE
        p = jax.nn.softmax(jnp.concatenate([s_meta, s_sel], axis=-1), axis=-1).astype(v.dtype)
        return (jnp.einsum('bhqm,bmhd->bqhd', p[..., :N_META], v_m)
                + jnp.einsum('bhqk,bqkhd->bqhd', p[..., N_META:], v_sel))

    o_r = lax.map(block_fn, (jnp.arange(n_blocks), to_blocks(q_r), to_blocks(qi_r), to_blocks(iw_r)))
    o_r = jnp.moveaxis(o_r, 0, 1).reshape(B, S, ATTN_HEADS, ATTN_HEAD_DIM)
    return jnp.concatenate([o_m, o_r], axis=1).reshape(B, T, ATTN_WIDTH)

def hgrn2(hq, hf, hi, lower_bound):
    B, T, _ = hq.shape
    f32 = jnp.float32
    q = jax.nn.silu(hq.astype(f32)).reshape(B, T, HGRN_HEADS, HGRN_KEY_DIM)
    f = lower_bound + (1.0 - lower_bound) * jax.nn.sigmoid(hf.astype(f32))
    log_f = jnp.log(f).reshape(B, T, HGRN_HEADS, HGRN_KEY_DIM)
    k = (1.0 - f).reshape(B, T, HGRN_HEADS, HGRN_KEY_DIM)
    v = hi.astype(f32).reshape(B, T, HGRN_HEADS, HGRN_VAL_DIM)
    pad = (-N_META) % CHUNK
    padw = ((0, 0), (pad, 0), (0, 0), (0, 0))
    q, log_f, k, v = [jnp.pad(a, padw) for a in (q, log_f, k, v)]
    Tp = T + pad
    n_chunks = Tp // CHUNK

    def chunks(a):
        return a.reshape(B, n_chunks, CHUNK, HGRN_HEADS, a.shape[-1]).transpose(1, 0, 3, 2, 4)

    causal = jnp.tril(jnp.ones((CHUNK, CHUNK), dtype=bool))[None, None, :, :, None]

    def step(state, xs):
        qc, kc, vc, gc = xs
        b = jnp.cumsum(gc, axis=2)
        diff = b[:, :, :, None, :] - b[:, :, None, :, :]
        decay = jnp.exp(jnp.where(causal, diff, -jnp.inf))
        a = jnp.einsum('bhtd,bhsd,bhtsd->bhts', qc, kc, decay)
        o = jnp.einsum('bhts,bhsv->bhtv', a, vc) + jnp.einsum('bhtd,bhdv->bhtv', qc * jnp.exp(b), state)
        b_last = b[:, :, -1]
        state = (jnp.exp(b_last)[..., None] * state
                 + jnp.einsum('bhsd,bhsv->bhdv', kc * jnp.exp(b_last[:, :, None, :] - b), vc))
        return state, o

    s0 = jnp.zeros((B, HGRN_HEADS, HGRN_KEY_DIM, HGRN_VAL_DIM), f32)
    _, o = lax.scan(step, s0, (chunks(q), chunks(k), chunks(v), chunks(log_f)))
    o = o.transpose(1, 0, 3, 2, 4).reshape(B, Tp, HGRN_HEADS, HGRN_VAL_DIM)
    return o[:, pad:].astype(hq.dtype)

def hybrid_mixer(h, w_in, idx_k_g, idx_k_b, attn_norm_g, lower_bound, hgrn_norm_g, w_out):
    B, T, _ = h.shape
    proj = jnp.einsum('btd,de->bte', h, w_in)
    aq, ak, av, ag, iq, ik, iw, hq, hf, hi, hg = split_columns(proj)
    o_attn = sparse_attention(aq, ak, av, iq, ik, iw, idx_k_g, idx_k_b)
    o_attn = rms_norm(o_attn, attn_norm_g) * jax.nn.silu(ag)
    o_hgrn = rms_norm(hgrn2(hq, hf, hi, lower_bound), hgrn_norm_g).reshape(B, T, HGRN_WIDTH)
    o_hgrn = o_hgrn * jax.nn.silu(hg)
    mixed = jnp.concatenate([o_attn, o_hgrn], axis=-1)
    return jnp.einsum('bte,ed->btd', mixed, w_out)

def setup_inputs(seed: int = 0) -> dict:
    key = jax.random.key(seed)
    ks = jax.random.split(key, 12)
    f32 = jnp.float32
    return {
        "x": jax.random.normal(ks[0], (BATCH, SEQ, D_MODEL), f32),
        "meta_tokens": jax.random.normal(ks[1], (N_META, D_MODEL), f32),
        "mix_norm": 1.0 + 0.05 * jax.random.normal(ks[2], (DEPTH, D_MODEL), f32),
        "w_in": jax.random.normal(ks[3], (DEPTH, D_MODEL, IN_WIDTH), f32) * D_MODEL ** -0.5,
        "idx_k_norm_g": 1.0 + 0.05 * jax.random.normal(ks[4], (DEPTH, IDX_HEAD_DIM), f32),
        "idx_k_norm_b": 0.02 * jax.random.normal(ks[5], (DEPTH, IDX_HEAD_DIM), f32),
        "attn_out_norm": 1.0 + 0.05 * jax.random.normal(ks[6], (DEPTH, ATTN_WIDTH), f32),
        "hgrn_lb_logits": 0.5 * jax.random.normal(ks[7], (DEPTH + 1, HGRN_WIDTH), f32),
        "hgrn_out_norm": 1.0 + 0.05 * jax.random.normal(ks[8], (DEPTH, HGRN_VAL_DIM), f32),
        "w_out": jax.random.normal(ks[9], (DEPTH, MIX_WIDTH, D_MODEL), f32) * MIX_WIDTH ** -0.5,
        "final_norm": 1.0 + 0.05 * jax.random.normal(ks[10], (D_MODEL,), f32),
    }

def reference(x, meta_tokens, mix_norm, w_in, idx_k_norm_g, idx_k_norm_b, attn_out_norm,
              hgrn_lb_logits, hgrn_out_norm, w_out, final_norm):
    B = x.shape[0]
    meta = jnp.broadcast_to(meta_tokens.astype(x.dtype)[None], (B, N_META, D_MODEL))
    h = jnp.concatenate([meta, x], axis=1)
    lower_bounds = jnp.cumsum(jax.nn.softmax(hgrn_lb_logits.astype(jnp.float32), axis=0), axis=0)
    for l in range(DEPTH):
        h = h + hybrid_mixer(rms_norm(h, mix_norm[l]), w_in[l], idx_k_norm_g[l], idx_k_norm_b[l],
                             attn_out_norm[l], lower_bounds[l], hgrn_out_norm[l], w_out[l])
    y = rms_norm(h, final_norm)
    return y[:, N_META:]


_drawn_inputs = setup_inputs


def setup_inputs(seed=0):
    import zlib

    import numpy as np

    out = dict(_drawn_inputs(seed))
    spreads = {}
    factors = {'attn_out_norm': 3.068, 'hgrn_lb_logits': 2.737, 'hgrn_out_norm': 2.949}
    for name, (base, spread) in spreads.items():
        noise = np.random.default_rng([zlib.crc32(name.encode()), seed]).standard_normal(out[name].shape)
        drawn = base * np.exp(spread * noise) if base else spread * noise
        out[name] = __import__('jax').numpy.asarray(drawn.astype(out[name].dtype))
    for name, factor in factors.items():
        out[name] = (out[name] * factor).astype(out[name].dtype)
    return out
```

```python
from contextlib import ExitStack

import numpy as np

import concourse.bass as bass
from concourse import mybir

ACT = mybir.ActivationFunctionType
ALU = mybir.AluOpType
AX = mybir.AxisListType
F32 = mybir.dt.float32
F32R = mybir.dt.float32r
U8 = mybir.dt.uint8

P = 128
SEQ, D, NMETA = 512, 1024, 16
HEADS, HD = 8, 64
AW = HEADS * HD
GH, GK = 4, 128
TILES = SEQ // P
META = TILES
KC = D // P
QUARTERS = 4
KQ = KC // QUARTERS
TOPK = min(256, SEQ // 4)
RAW, RING = 3, 6
LEVELS = 7
INF_LEVEL = LEVELS
EPS = 1e-6
ATTN_SCALE = HD ** -0.5
IDX_SCALE = (8 ** -0.5) * (64 ** -0.5)
NEG = -1.0e30
TAKEN = -3.0e38
IKW = 72

GROUPS = {
    "hf": (3144, 512, [0, 1, 2, 3, META]),
    "hi": (3656, 512, [META, 0, 1, 2, 3]),
    "hq": (2632, 512, [0, 1, 2, 3]),
    "hg": (4168, 512, [0, 1, 2, 3]),
    "ikw": (2560, IKW, [0]),
    "iq": (2048, 512, [1, 2, 3]),
    "ak": (512, 512, [META, 0, 1, 2, 3]),
    "av": (1024, 512, [META, 0, 1, 2, 3]),
    "aq": (0, 512, [0, 1, 2, 3]),
    "ag": (1536, 512, [0, 1, 2, 3]),
    "o0": (0, 512, [0, 1, 2, 3]),
    "o1": (512, 512, [0, 1, 2, 3]),
}
ORDER = list(GROUPS)


def level_tables():
    u, p = np.meshgrid(np.arange(P), np.arange(P), indexing="ij")
    sums = np.zeros((P, LEVELS + 1, P), np.float32)
    for l in range(LEVELS):
        m = 1 << l
        mid = (p // (2 * m)) * 2 * m + m
        key = p < mid
        sums[:, l] = np.where(key, (u > p) & (u < mid), (u >= mid) & (u <= p))
    sums[:, INF_LEVEL] = u <= p
    after = (u > p).astype(np.float32)
    s, t = u, p
    level = np.full((P, P), -1)
    for l in range(LEVELS):
        m = 1 << l
        mid = (s // (2 * m)) * 2 * m + m
        level[(s // (2 * m) == t // (2 * m)) & (s < mid) & (t >= mid)] = l
    pieces = [level == l for l in (4, 3, 2, 1, 0)] + [s == t]
    kept = np.stack(pieces, 1).astype(np.float32)
    return sums, after, kept


PIECES = 7
BLOCKS = [(0, 64, 64, 128), (0, 32, 32, 64), (64, 96, 96, 128)]
IKW_TURNED = IKW
CONSTS = 8


def rope_tables():
    half = HD // 4 // 2
    inv = np.float32(500000.0) ** (-np.arange(half, dtype=np.float32) * np.float32(2.0) / np.float32(2 * half))
    pos = np.zeros((P, TILES + 1), np.float32)
    for t in range(TILES):
        pos[:, t] = NMETA + t * P + np.arange(P)
    pos[:NMETA, META] = np.arange(NMETA)
    ang = (pos[:, :, None] * inv.astype(np.float32)).astype(np.float32)
    cos, sin = np.cos(ang.astype(np.float64)), np.sin(ang.astype(np.float64))
    return (np.concatenate([cos, cos], 2).astype(np.float32), np.concatenate([-sin, sin], 2).astype(np.float32))


def schedule():
    s = []

    def proj(g, i):
        s.append(("proj", g, GROUPS[g][2][i]))

    def weights(g, *qs):
        s.extend(("weights", g, q) for q in qs)

    def group(g, between=None):
        units = GROUPS[g][2]
        nxt = ORDER[ORDER.index(g) + 1] if g != ORDER[-1] else None
        between = between or {}
        for i in range(len(units)):
            if i == max(0, len(units) - 2) and nxt:
                weights(nxt, 0, 1)
            proj(g, i)
            if i == len(units) - 1 and nxt:
                weights(nxt, 2, 3)
            s.extend(between.get(i, []))

    s += [("norm", 0), ("norm", 1), ("hT", 0, 0)]
    weights("hf", 0)
    s += [("hT", 0, 1)]
    weights("hf", 1, 2, 3)
    s += [("norm", 2), ("hT", 1, 0), ("hT", 1, 1)]
    group("hf", {0: [("norm", 3), ("hT", 2, 0), ("hT", 2, 1)],
                 1: [("norm", META), ("hT", 3, 0), ("hT", 3, 1)],
                 2: [("hT", META, 0), ("hT", META, 1)]})
    group("hi")
    def decays(t, hp):
        return [("decay", t, 2 * hp), ("decay", t, 2 * hp + 1)]

    def mid(t):
        return [("pieces", t, 0)] + decays(t, 1) + [("gated", t, 1)]

    def end(t):
        out = [("pieces", t, 1)]
        if t < TILES - 1:
            out += [("suffix", t), ("kT", t + 1)] + decays(t + 1, 0)
        out += [("out", t)]
        if t < TILES - 1:
            out += [("state", t)]
        out += [("mixH", t)]
        if t < TILES - 1:
            out += [("gated", t + 1, 0)]
        return out

    group("hq", {0: [("suffix", META), ("kT", 0)], 1: [("state", META)], 3: decays(0, 0) + [("gated", 0, 0)]})
    group("hg", {0: mid(0), 1: end(0), 2: mid(1), 3: end(1)})
    group("ikw", {0: [("ikT",)] + mid(2)})
    index = lambda b: [("index", b, h) for h in range(8)]
    top = [("topk", r) for r in range(TOPK // 8)]
    group("iq", {0: [("kiT",)] + end(2),
                 1: [("ropeT", "iq", 1)] + mid(3),
                 2: [("ropeT", "iq", 2)] + end(3)})
    group("ak", {0: [("ropeT", "iq", 3)] + index(1)[0:4], 1: [("ropeT", "ak", META)] + index(1)[4:],
                 2: [("ropeT", "ak", 0)] + index(2)[0:4], 3: [("ropeT", "ak", 1)] + index(2)[4:],
                 4: [("ropeT", "ak", 2)] + index(3)[0:4]})
    group("av", {0: [("ropeT", "ak", 3)] + index(3)[4:], 1: top[0:1], 2: top[1:3], 3: top[3:4], 4: top[4:6]})
    group("aq", {0: top[6:7], 1: [("ropeT", "aq", 0)] + top[7:9], 2: [("ropeT", "aq", 1)] + top[9:10],
                 3: [("ropeT", "aq", 2)] + top[10:12]})

    def heads(b):
        out = [("meta", b), ("score", b, 0), ("score", b, 1), ("score", b, 2)]
        for h in range(HEADS):
            out += [("probT", b, h)]
            if h + 3 < HEADS:
                out += [("score", b, h + 3)]
            if h + 3 == HEADS:
                out += [("pmeta", b)]
            if h:
                out += [("pv", b, h - 1)]
        return out + [("pv", b, HEADS - 1), ("metaT", b), ("attn", b)]

    group("ag", {0: [("ropeT", "aq", 3)] + top[12:13], 1: top[13:14] + heads(0)[0:14], 2: top[14:15] + heads(0)[14:],
                 3: top[15:16] + [("biases",)]})
    mixT = lambda t: [("mixT", t, 0), ("mixT", t, 1)]
    h1, h2, h3 = heads(1), heads(2), heads(3)
    s += h1[0:16] + mixT(0) + h1[16:]
    group("o0", {0: h2[0:16] + mixT(1) + h2[16:], 1: h3[0:16] + mixT(2) + h3[16:],
                 2: mixT(3)})
    group("o1", {1: [("final", 0)], 2: [("final", 1)], 3: [("final", 2), ("final", 3)]})
    return s


SCHEDULE = schedule()


class Order:

    def __init__(self, keys):
        self.keys = list(keys)
        self.n = {k: i for i, k in enumerate(self.keys)}
        assert len(self.n) == len(self.keys), [k for k in self.keys if self.keys.count(k) > 1][:5]

    def at(self, key):
        return self.n[key] + 1


class Banks:

    def __init__(self, full, free, turns):
        self.full, self.free = full, free
        self.order = Order([k for k, _ in turns])
        self.bank = dict(turns)
        seen = {}
        self.turn = {}
        for k, b in turns:
            self.turn[k] = seen.get(b, 0)
            seen[b] = self.turn[k] + 1

    def wait_free(self, eng, key):
        if self.turn[key]:
            eng.wait_ge(self.free[self.bank[key]], self.turn[key])

    def wait_full(self, eng, key):
        eng.wait_ge(self.full, self.order.at(key))

    def wait_freed(self, eng, key):
        eng.wait_ge(self.free[self.bank[key]], self.turn[key] + 1)

    def freed(self, key):
        return self.free[self.bank[key]]


def units():
    return [s[1:] for s in SCHEDULE if s[0] == "proj"]


def hymba_layer(nc, x, meta_tokens, mix_norm, w_in, idx_g, idx_b, attn_g, lb_logits, hgrn_g, w_out,
                final_g, t_ident, t_cos, t_sin, t_sums, t_after, t_kept, t_causal, out):
    with ExitStack() as ctx:
        def sb(name, shape, dt=F32, where=ctx):
            return where.enter_context(nc.sbuf_tensor(name, shape, dt))

        def sem(name):
            return ctx.enter_context(nc.semaphore(name))

        hT_hi = sb("hT_hi", [P, KC, SEQ + NMETA], F32R)
        hT_lo = sb("hT_lo", [P, KC, SEQ + NMETA], F32R)
        w_raw = sb("w_raw", [P, RAW, KQ, 512])
        w_hi = sb("w_hi", [P, RING, KQ, 512], F32R)
        w_lo = sb("w_lo", [P, RING, KQ, 512], F32R)
        ident = sb("ident", [P, P])
        cos = sb("cos", [P, TILES + 1, 16])
        sin = sb("sin", [P, TILES + 1, 16])
        sums = sb("sums", [P, LEVELS + 1, P], F32R)
        after = sb("after", [P, P], F32R)
        kept = sb("kept", [P, PIECES - 1, P], U8)
        bias = [sb(f"bias{b}", [P, (b + 1) * P]) for b in range(TILES)]
        rows = sb("rows", [P, 2, 512])
        temp = sb("temp", [P, 2, 512])
        mixH = sb("mixH", [P, TILES, 512])
        small = sb("small", [P, 104])
        gcol = sb("gcol", [P, KC])
        idxw = sb("idxw", [P, TILES, 8])
        mhalf = small[:, 0:8]
        sq_x, rs_x = small[:, 8:13], small[:, 13:18]
        ik_mean, ik_var, ik_rs = small[:, 18:22], small[:, 22:26], small[:, 26:30]
        ms_h, rs_h = small[:, 30:34], small[:, 34:38]
        mmax, pmax, nmax = small[:, 38:46], small[:, 46:54], small[:, 54:62]
        psums, prec = small[:, 62:70], small[:, 70:78]
        ms_a, rs_a = small[:, 78:79], small[:, 79:80]
        msum = small[:, 88:96]
        ms_f, rs_f = small[:, 80:84], small[:, 84:88]
        top8 = sb("top8", [P, TILES, 8])
        decay_end = sb("decay_end", [P, 2, GH])
        o_row = sb("o_row", [P, 512])
        junk = sb("junk", [P, P])
        swapped = sb("swapped", [P, P])

        with ExitStack() as r1:
            x_t = sb("x_t", [P, 3, D], where=r1)
            gb = sb("gb", [P, D], where=r1)
        with ExitStack() as r1:
            qiT = sb("qiT", [P, 4, 3 * P], where=r1)
            kiT = sb("kiT", [P, SEQ], where=r1)
            rel = sb("rel", [P, 2, SEQ], where=r1)
            ik_row = sb("ik_row", [P, TILES, IKW], where=r1)
            ik_two = sb("ik_two", [P, TILES, 2, 64], where=r1)
            idx_gb = sb("idx_gb", [P, 2, 64], where=r1)
            ikT = rel[:, 0, :]
        with ExitStack() as r1:
            y = sb("y", [P, TILES, D], where=r1)
        sb("region1", [P, 16 * 1024 // 4])

        with ExitStack() as r2:
            g_hi = sb("g_hi", [P, TILES + 1, 512], F32R, where=r2)
            g_lo = sb("g_lo", [P, TILES + 1, 512], F32R, where=r2)
            hk = sb("hk", [P, TILES + 1, 512], where=r2)
            hv = sb("hv", [P, TILES + 1, 512], where=r2)
            hqT = sb("hqT", [P, GH, SEQ], where=r2)
            E = sb("E", [P, LEVELS + 1, 2, P], where=r2)
            q_inf = sb("q_inf", [P, GH, P], where=r2)
            A = sb("A", [P, GH, P], where=r2)
            S = sb("S", [P, GH, GK], where=r2)
            hkT = sb("hkT", [P, GH, P], where=r2)
            k_end = sb("k_end", [P, 512], where=r2)
        with ExitStack() as r2:
            kT = sb("kT", [P, 4, SEQ], where=r2)
            kmT = sb("kmT", [P, 4, 2 * NMETA], where=r2)
            mixA = sb("mixA", [P, TILES, 512], where=r2)
            V = sb("V", [P, TILES, 512], where=r2)
            V_meta = sb("V_meta", [P, 512], where=r2)
            v_row = sb("v_row", [NMETA, 512], where=r2)
            qT = sb("qT", [P, 4, SEQ], where=r2)
            prob = sb("prob", [P, HEADS, SEQ], where=r2)
            pm = sb("pm", [P, P], where=r2)
            probT = sb("probT", [P, 2, SEQ], where=r2)
            fb = sb("fb", [P, D], where=r2)
            pmT = sb("pmT", [P, P], where=r2)
        sb("region2", [P, 66 * 1024 // 4])

        lb, half_span, logits = mixH[:, 0, :], mixH[:, 1, :], mixH[:, 2:4, :]
        middle = lb
        attn_row = rows[:, 0, :]

        bank = [ctx.enter_context(nc.psum_tensor(f"bank{i}", [P, 512], F32)) for i in range(8)]

        s_const = sem("s_const")
        s_xin = [sem(f"s_xin{t}") for t in range(TILES + 1)]
        s_gb, s_logits, s_idxg, s_gcol = sem("s_gb"), sem("s_logits"), sem("s_idxg"), sem("s_gcol")
        s_raw = [sem(f"s_raw{i}") for i in range(RAW)]
        s_whi, s_wlo_dve, s_wlo_pool, s_wused = sem("s_whi"), sem("s_wlo_dve"), sem("s_wlo_pool"), sem("s_wused")
        s_tab = sem("s_tab")
        s_sq, s_rstd, s_xn = sem("s_sq"), sem("s_rstd"), sem("s_xn")
        s_hhi, s_hlo = sem("s_hhi"), sem("s_hlo")
        s_mhalf, s_lb, s_lbexp = sem("s_mhalf"), sem("s_lb"), sem("s_lbexp")
        s_tanh, s_pv, s_pmsub, s_pmexp, s_iqw = sem("s_tanh"), sem("s_pv"), sem("s_pmsub"), sem("s_pmexp"), sem("s_iqw")
        s_fk, s_ghi, s_glo = sem("s_fk"), sem("s_ghi"), sem("s_glo")
        s_silu = sem("s_silu")
        s_rope = sem("s_rope")
        s_ropeT = sem("s_ropeT")
        s_ik, s_ikvar, s_ikrs, s_kiT, s_iktwo = sem("s_ik"), sem("s_ikvar"), sem("s_ikrs"), sem("s_kiT"), sem("s_iktwo")
        s_rel, s_acc = sem("s_rel"), sem("s_acc")
        s_hkT, s_E, s_X, s_A = sem("s_hkT"), sem("s_E"), sem("s_X"), sem("s_A")
        s_kexp, s_kend, s_S = sem("s_kexp"), sem("s_kend"), sem("s_S")
        s_o, s_osq, s_ors, s_mixH = sem("s_o"), sem("s_osq"), sem("s_ors"), sem("s_mixH")
        s_vm, s_vrow, s_vzero = sem("s_vm"), sem("s_vrow"), sem("s_vzero")
        s_pmeta, s_nmax, s_exp, s_pT, s_pmT = sem("s_pmeta"), sem("s_nmax"), sem("s_exp"), sem("s_pT"), sem("s_pmT")
        s_asq, s_ars, s_mixA = sem("s_asq"), sem("s_ars"), sem("s_mixA")
        s_mhi, s_mlo = sem("s_mhi"), sem("s_mlo")
        s_xres = [sem(f"s_xres{t}") for t in range(TILES)]
        s_fb = sem("s_fb")
        s_y, s_ysq, s_yrs, s_fin = sem("s_y"), sem("s_ysq"), sem("s_yrs"), sem("s_fin")
        s_out = sem("s_out")
        s_a, s_v, s_p = sem("s_a"), sem("s_v"), sem("s_p")

        full = {n: sem(f"{n}_full") for n in ("pj", "tr", "sd", "mi")}
        free = {n: {b: sem(f"{n}_free{b}") for b in bs}
                for n, bs in (("pj", (0, 1)), ("tr", (2, 3)), ("sd", (4, 5)), ("mi", (6, 7)))}

        def of(*kinds):
            return [s for s in SCHEDULE if s[0] in kinds]

        pj = Banks(full["pj"], free["pj"], [(u, i % 2) for i, u in enumerate(units())])
        tr_keys = of("hT", "kT", "ikT", "kiT", "ropeT", "probT", "metaT", "mixT")
        tr = Banks(full["tr"], free["tr"], [(k, 2 + i % 2) for i, k in enumerate(tr_keys)])
        sd_turns = []
        for s in SCHEDULE:
            if s[0] in ("index", "score"):
                sd_turns.append((s, 4 + s[2] % 2))
            if s[0] == "decay":
                sd_turns += [(s + (0,), 4), (s + (1,), 5)]
        sd = Banks(full["sd"], free["sd"], sd_turns)
        mi_turns = []
        for s in SCHEDULE:
            if s[0] == "pieces":
                mi_turns += [(s + (j,), 6 + j % 2) for j in range(PIECES)]
            if s[0] in ("suffix", "meta"):
                mi_turns.append((s, 6))
            if s[0] == "state":
                mi_turns.append((s, 6))
            if s[0] in ("out", "attn"):
                mi_turns.append((s, 7))
        mi = Banks(full["mi"], free["mi"], mi_turns)

        quarters = Order([s[1:] for s in of("weights")])

        def lo_on_pool(n):
            g = quarters.keys[n][0]
            return g not in ("hf", "o0", "o1")

        lo_pool = Order([k for i, k in enumerate(quarters.keys) if lo_on_pool(i)])
        lo_dve = Order([k for i, k in enumerate(quarters.keys) if not lo_on_pool(i)])
        used = Order([k for k in quarters.keys if k[1] != QUARTERS - 1])

        def wait_lo(eng, key):
            if key in lo_pool.n:
                eng.wait_ge(s_wlo_pool, lo_pool.at(key))
            else:
                eng.wait_ge(s_wlo_dve, lo_dve.at(key))

        def wait_slot_used(eng, n):
            if n >= RING:
                g, q = quarters.keys[n - RING]
                if q == QUARTERS - 1:
                    pj.wait_full(eng, (g, GROUPS[g][2][-1]))
                else:
                    eng.wait_ge(s_wused, used.at((g, q)))

        norms = Order([s[1] for s in of("norm")])
        hTs = Order(of("hT"))
        ropes = Order([u for u in units() if u[0] in ("iq", "ak", "aq")])
        ropeTs = Order([s[1:] for s in of("ropeT")])
        silus = Order([u for u in units() if u[0] in ("hq", "hg", "ag")])
        evacs = Order([u for u in units() if u[0] not in ("o0", "o1")])
        hfs = Order(GROUPS["hf"][2])
        temps = Order([u for u in units() if u[0] in ("hf", "hq", "hg", "ag")])
        rels = Order([s[1:] for s in of("index")])
        decays = Order([s[1:] for s in of("decay")])
        gateds = Order([s[1:] for s in of("gated")])
        kept_pieces = Order([s[1:] + (j,) for s in of("pieces") for j in range(PIECES)])
        suffixes = Order([s[1] for s in of("suffix")])
        states = Order([s[1] for s in of("state")])
        outs = Order([s[1] for s in of("out")])
        mixHs = Order([s[1] for s in of("mixH")])
        kTs = Order([s[1] for s in of("kT")])
        pmetas = Order([s[1] for s in of("pmeta")])
        topks = Order([s[1] for s in of("topk")])
        ropes_iw = None
        scores = Order([s[1:] for s in of("score")])
        probTs = Order([s[1:] for s in of("probT")])
        attns = Order([s[1] for s in of("attn")])
        mixTs = Order([s[1:] for s in of("mixT")])
        finals = Order([s[1] for s in of("final")])
        yunits = Order([u for u in units() if u[0] in ("o0", "o1")])

        def rows_of(t):
            return NMETA if t == META else P

        def cols_of(t):
            return slice(SEQ, SEQ + NMETA) if t == META else slice(t * P, (t + 1) * P)

        def temp_of(u):
            return temp[0:(rows_of(u[1]) if u[0] == "hf" else P), temps.n[u] % 2, :]

        def f_of(t):
            if t == META:
                return k_end[0:NMETA, :]
            return E[:, :, :, :].rearrange("p l h t -> p (l h t)")[:, t * 512:(t + 1) * 512]

        def wait_temp(eng, u):
            n = temps.n[u]
            if n < 2:
                return
            old = temps.keys[n - 2]
            if old[0] == "hf":
                eng.wait_ge(s_fk, hfs.at(old[1]))
            else:
                pj.wait_freed(eng, old)

        def heads_of(ap, n=HEADS):
            return ap.rearrange("p (h d) -> p h d", h=n)

        block = ctx.enter_context(nc.Block())

        @block.sync
        def _(sp):
            def load_x(t):
                r = rows_of(t)
                n = norms.n[t]
                if n >= 3:
                    tr.wait_full(sp, ("hT", norms.keys[n - 3], 1))
                src = meta_tokens if t == META else x[0, t * P:(t + 1) * P, :]
                sp.dma_start(x_t[0:r, n % 3, :], src).then_inc(s_xin[t], 16)

            def load_w(n):
                g, q = quarters.keys[n]
                c0, width, _ = GROUPS[g]
                w = w_out[0] if g in ("o0", "o1") else w_in[0]
                src = w[q * KQ * P:(q + 1) * KQ * P, c0:c0 + width]
                if n >= RAW:
                    wait_lo(sp, quarters.keys[n - RAW])
                sp.dma_start(w_raw[:, n % RAW, :, 0:width], src.rearrange("(k p) c -> p k c", p=P))\
                    .then_inc(s_raw[n % RAW], 16)

            load_x(0)
            load_x(1)
            load_w(0)
            load_w(1)
            load_x(2)
            load_w(2)
            load_w(3)
            load_x(3)
            load_w(4)
            load_x(META)
            for n in range(5, len(quarters.keys)):
                load_w(n)
                if quarters.keys[n] == ("aq", 1):
                    pj.wait_freed(sp, ("av", META))
                    sp.wait_ge(s_vzero, 2)
                    for h in range(HEADS):
                        sp.dma_start(V_meta[h * NMETA:(h + 1) * NMETA, h * HD:(h + 1) * HD],
                                     v_row[:, h * HD:(h + 1) * HD]).then_inc(s_vm, 16)
                    sp.dma_start(fb[:], final_g.rearrange("(o c) -> o c", o=1).broadcast_to([P, D])).then_inc(s_fb, 16)
                if quarters.keys[n] == ("ikw", 3):
                    tr.wait_full(sp, ("hT", META, 1))
                    sp.dma_start(idx_gb[:, 0, :], idx_g[0:1, :].broadcast_to([P, 64])).then_inc(s_idxg, 16)
                    sp.dma_start(idx_gb[:, 1, :], idx_b[0:1, :].broadcast_to([P, 64])).then_inc(s_idxg, 16)
                if quarters.keys[n] == ("o0", 3):
                    sp.wait_ge(s_acc, rels.at((3, 7)))
                    for t in range(TILES):
                        sp.dma_start(y[:, t, :], x[0, t * P:(t + 1) * P, :]).then_inc(s_xres[t], 16)
            for t in range(TILES):
                sp.wait_ge(s_fin, t + 1)
                sp.dma_start(out[0, t * P:(t + 1) * P, :], y[:, t, :]).then_inc(s_out, 16)
            sp.wait_ge(s_out, 16 * TILES)

        @block.gpsimd
        def _(pool):
            steps = [0]

            def link(ins):
                steps[0] += 1
                ins.then_inc(s_p, 1)
                pool.wait_ge(s_p, steps[0])

            def rstd(dst, src, scale, done, r=P, eps=EPS):
                link(pool.tensor_scalar(dst, src, scale, eps, ALU.mult, ALU.add))
                pool.tensor_tensor(dst, dst, mhalf[0:r, 0:dst.shape[1]], ALU.pow).then_inc(done, 1)

            link(pool.memset(mhalf, -0.5))
            for step in SCHEDULE:
                kind = step[0]
                if kind == "proj" and step[1:] == ("hi", META):
                    for t in GROUPS["hf"][2]:
                        r = rows_of(t)
                        pool.wait_ge(s_ghi, hfs.at(t))
                        pool.tensor_tensor(g_lo[0:r, t, :], f_of(t), g_hi[0:r, t, :].bitcast(F32),
                                           ALU.subtract).then_inc(s_glo, 1)
                if kind == "norm":
                    t = step[1]
                    r = rows_of(t)
                    pool.wait_ge(s_sq, norms.at(t))
                    rstd(rs_x[0:r, t:t + 1], sq_x[0:r, t:t + 1], 1.0 / D, s_rstd, r)
                elif kind == "weights" and step[1:] in lo_pool.n:
                    n = quarters.n[step[1:]]
                    width = GROUPS[step[1]][1]
                    pool.wait_ge(s_whi, n + 1)
                    pool.tensor_tensor(w_lo[:, n % RING, :, 0:width], w_raw[:, n % RAW, :, 0:width],
                                       w_hi[:, n % RING, :, 0:width].bitcast(F32), ALU.subtract)\
                        .then_inc(s_wlo_pool, 1)
                elif kind == "ikT":
                    pool.wait_ge(s_ikvar, 1)
                    rstd(ik_rs, ik_var, 1.0 / 64, s_ikrs)
                elif kind == "mixH":
                    pool.wait_ge(s_osq, mixHs.at(step[1]))
                    rstd(rs_h, ms_h, 1.0 / GK, s_ors)
                elif kind == "proj" and step[1:] == ("ak", META):
                    sd.wait_full(pool, ("decay", 3, 3, 1))
                    pool.memset(kmT[:, :, :], 0.0).then_inc(s_vzero, 1)
                    tr.wait_full(pool, ("kT", 3))
                    pool.wait_ge(s_X, gateds.at((3, 1)))
                    pool.wait_ge(s_kend, suffixes.at(2))
                    mi.wait_full(pool, ("out", 3))
                    pool.memset(V_meta[:, :], 0.0).then_inc(s_vzero, 1)
                elif kind == "attn":
                    pool.wait_ge(s_asq, attns.at(step[1]))
                    rstd(rs_a, ms_a, 4.0 / AW, s_ars, eps=4.0 * EPS)
                elif kind == "final":
                    t = step[1]
                    pool.wait_ge(s_ysq, finals.at(t))
                    rstd(rs_f[:, t:t + 1], ms_f[:, t:t + 1], 1.0 / D, s_yrs)

        @block.scalar
        def _(act):
            steps = [0]

            def link(ins):
                steps[0] += 1
                ins.then_inc(s_a, 1)
                act.wait_ge(s_a, steps[0])

            act.dma_start(ident[:], t_ident).then_inc(s_const, 16)
            act.dma_start(gb[:], mix_norm[0:1, :].broadcast_to([P, D])).then_inc(s_gb, 16)
            act.dma_start(logits, lb_logits.rearrange("(o a) c -> o a c", o=1).broadcast_to([P, 2, 512]))\
                .then_inc(s_logits, 16)
            act.dma_start(E[:, :, :, :].rearrange("p l h t -> p (l h t)")[:, 0:1024], t_sums).then_inc(s_const, 16)
            act.dma_start(A[:, 0, :], t_after).then_inc(s_const, 16)
            act.dma_start(hqT[:, 0, :].rearrange("p (o t) -> p o t", t=P), t_kept[:, 0:4, :]).then_inc(s_const, 16)
            act.dma_start(hqT[:, 1, 0:2 * P].rearrange("p (o t) -> p o t", t=P), t_kept[:, 4:6, :]).then_inc(s_const, 16)
            act.dma_start(cos[:], t_cos).then_inc(s_const, 16)
            act.dma_start(sin[:], t_sin).then_inc(s_const, 16)
            act.dma_start(bias[0][:], t_causal).then_inc(s_const, 16)
            act.dma_start(gcol[:, 0:4], attn_g.rearrange("o (k p) -> p (o k)", p=P), allow_slow_non_contiguous=True).then_inc(s_gcol, 16)
            for k in range(4, 8):
                act.dma_start(gcol[:, k:k + 1], hgrn_g.rearrange("o (k p) -> p (o k)", p=P), allow_slow_non_contiguous=True).then_inc(s_gcol, 16)

            def weights_hi(g, q):
                n = quarters.n[(g, q)]
                width = GROUPS[g][1]
                wait_slot_used(act, n)
                act.wait_ge(s_raw[n % RAW], 16 * (n // RAW + 1))
                if g in ("o0", "o1"):
                    act.wait_ge(s_gcol, 80)
                    for j in range(KQ):
                        k = q * KQ + j
                        ins = act.activation(w_hi[:, n % RING, j, :], w_raw[:, n % RAW, j, :], ACT.Copy,
                                             scale=gcol[:, k:k + 1])
                else:
                    ins = act.activation(w_hi[:, n % RING, :, 0:width], w_raw[:, n % RAW, :, 0:width], ACT.Copy)
                ins.then_inc(s_whi, 1)

            def unit(g, t):
                u = (g, t)
                src = bank[pj.bank[u]]
                r = P if g == "hq" else rows_of(t)
                if g in ("o0", "o1"):
                    return
                if g in ("hf", "hq", "hg", "ag"):
                    wait_temp(act, u)
                    pj.wait_full(act, u)
                    ins = act.activation(temp_of(u), src[0:r, :], ACT.Tanh, scale=0.5)
                    ins.then_inc(pj.freed(u) if g == "hf" else s_tanh, 1)
                elif g == "hi":
                    pj.wait_full(act, u)
                    act.activation(hv[0:r, t, :], src[0:r, :], ACT.Copy).then_inc(pj.freed(u), 1)
                elif g == "av":
                    pj.wait_full(act, u)
                    act.wait_ge(s_mixH, 4)
                    dst = v_row[:, :] if t == META else V[:, t, :]
                    act.activation(dst, src[0:r, :], ACT.Copy).then_inc(pj.freed(u), 1)
                elif g == "ikw":
                    pj.wait_full(act, u)
                    act.activation(ikT[0:IKW, :], src[0:IKW, :], ACT.Copy).then_inc(pj.freed(u), 1)
                else:
                    n = ropes.n[u]
                    if n >= 2:
                        tr.wait_full(act, ("ropeT",) + ropes.keys[n - 2])
                    pj.wait_full(act, u)
                    act.activation(rows[0:r, n % 2, :], src[0:r, :], ACT.Copy).then_inc(pj.freed(u), 1)

            def log_gates():
                for t in GROUPS["hf"][2]:
                    r = rows_of(t)
                    act.wait_ge(s_fk, hfs.at(t))
                    link(act.activation(f_of(t), f_of(t), ACT.Ln))
                    act.activation(g_hi[0:r, t, :], f_of(t), ACT.Copy).then_inc(s_ghi, 1)

            act.wait_ge(s_const, 16 * CONSTS)
            act.activation(sums[:, :, :].rearrange("p l t -> p (l t)"),
                           E[:, :, :, :].rearrange("p l h t -> p (l h t)")[:, 0:1024], ACT.Copy).then_inc(s_tab, 1)
            act.activation(after[:], A[:, 0, :], ACT.Copy).then_inc(s_tab, 1)
            for step in SCHEDULE:
                kind = step[0]
                if kind == "norm":
                    t = step[1]
                    r = rows_of(t)
                    act.wait_ge(s_xin[t], 16)
                    if norms.n[t]:
                        act.wait_ge(s_sq, norms.n[t])
                    act.activation(rows[0:r, :, :].rearrange("p a b -> p (a b)"), x_t[0:r, norms.n[t] % 3, :],
                                   ACT.Square, accum_out=sq_x[0:r, t:t + 1]).then_inc(s_sq, 1)
                    if norms.n[t] == 0:
                        act.wait_ge(s_lbexp, 1)
                        act.activation(logits, logits, ACT.Exp).then_inc(s_lb, 1)
                elif kind == "hT":
                    _, t, half = step
                    r = rows_of(t)
                    b = bank[tr.bank[step]]
                    tr.wait_full(act, step)
                    act.activation(hT_hi[:, 4 * half:4 * half + 4, cols_of(t)],
                                   b[:, :].rearrange("p (k t) -> p k t", k=4)[:, :, 0:r], ACT.Copy).then_inc(s_hhi, 1)
                elif kind == "weights":
                    weights_hi(*step[1:])
                elif kind == "proj":
                    unit(*step[1:])
                    if step[1:] == ("hi", META):
                        log_gates()
                elif kind == "ikT":
                    tr.wait_full(act, step)
                    act.activation(ik_row[:, :, :], bank[tr.bank[step]][:, 0:TILES * IKW]
                                   .rearrange("p (t c) -> p t c", t=TILES), ACT.Copy).then_inc(tr.freed(step), 1)
                elif kind == "kiT":
                    tr.wait_full(act, step)
                    act.activation(kiT[:, :], bank[tr.bank[step]][:, :], ACT.Copy).then_inc(tr.freed(step), 1)
                elif kind == "ropeT":
                    _, g, t = step
                    b4 = bank[tr.bank[step]][:, :].rearrange("p (j t) -> p j t", j=4)
                    tr.wait_full(act, step)
                    if g == "iq":
                        ins = act.activation(qiT[:, :, (t - 1) * P:t * P], b4, ACT.Copy)
                    elif g == "aq":
                        ins = act.activation(qT[:, :, t * P:(t + 1) * P], b4, ACT.Copy)
                    elif t == META:
                        act.wait_ge(s_vzero, 2)
                        act.activation(kmT[0:HD, :, 0:NMETA], b4[0:HD, :, 0:NMETA], ACT.Copy)
                        ins = act.activation(kmT[HD:P, :, NMETA:2 * NMETA], b4[HD:P, :, 0:NMETA], ACT.Copy)
                    else:
                        ins = act.activation(kT[:, :, t * P:(t + 1) * P], b4, ACT.Copy)
                    ins.then_inc(tr.freed(step), 1)
                elif kind == "index":
                    _, b, h = step
                    n = rels.n[(b, h)]
                    if n >= 2:
                        act.wait_ge(s_acc, n - 1)
                    sd.wait_full(act, step)
                    w = (b + 1) * P
                    act.activation(rel[:, n % 2, 0:w], bank[sd.bank[step]][:, 0:w], ACT.Relu)\
                        .then_inc(sd.freed(step), 1)
                elif kind == "kT":
                    t = step[1]
                    tr.wait_full(act, step)
                    if kTs.n[t]:
                        mi.wait_full(act, ("pieces", kTs.keys[kTs.n[t] - 1], 1, PIECES - 1))
                        act.wait_ge(s_X, gateds.at((kTs.keys[kTs.n[t] - 1], 1)))
                    act.activation(hkT[:, :, :], bank[tr.bank[step]][:, :].rearrange("p (h t) -> p h t", h=GH),
                                   ACT.Copy).then_inc(tr.freed(step), 1)
                elif kind == "decay":
                    _, t, h = step
                    n = decays.n[(t, h)]
                    if h % 2 == 0 and n >= 2:
                        prev = decays.keys[n - 1]
                        mi.wait_full(act, ("pieces", prev[0], prev[1] // 2, PIECES - 1))
                    for half in range(2):
                        key = step + (half,)
                        sd.wait_full(act, key)
                        act.activation(E[:, 4 * half:4 * half + 4, h % 2, :],
                                       bank[sd.bank[key]][:, :].rearrange("p (l t) -> p l t", l=4), ACT.Exp)\
                            .then_inc(sd.freed(key), 1)
                elif kind == "suffix":
                    t = step[1]
                    r = rows_of(t)
                    mi.wait_full(act, step)
                    if suffixes.n[t]:
                        mi.wait_full(act, ("state", suffixes.keys[suffixes.n[t] - 1]))
                    act.activation(k_end[0:r, :], bank[6][0:r, :], ACT.Exp).then_inc(mi.freed(step), 1)
                elif kind == "out":
                    t = step[1]
                    mi.wait_full(act, step)
                    if outs.n[t]:
                        act.wait_ge(s_mixH, mixHs.at(outs.keys[outs.n[t] - 1]))
                    act.activation(o_row[:, :], bank[7][:, :], ACT.Copy, scale=0.5).then_inc(mi.freed(step), 1)
                    mi.wait_freed(act, step)
                    for h in range(GH):
                        link(act.activation(junk[:, :], o_row[:, h * GK:(h + 1) * GK], ACT.Square,
                                            accum_out=ms_h[:, h:h + 1])) if h < GH - 1 else \
                            act.activation(junk[:, :], o_row[:, h * GK:(h + 1) * GK], ACT.Square,
                                           accum_out=ms_h[:, h:h + 1]).then_inc(s_osq, 1)
                elif kind == "meta":
                    b = step[1]
                    mi.wait_full(act, step)
                    if b:
                        tr.wait_full(act, ("metaT", b - 1))
                    else:
                        act.wait_ge(s_mixH, 4)
                    act.activation(pm[:, :], bank[6][:, 0:P], ACT.Copy).then_inc(mi.freed(step), 1)
                elif kind == "pmeta":
                    act.wait_ge(s_pmsub, pmetas.at(step[1]))
                    act.activation(pm[:, :], pm[:, :], ACT.Exp, scale=ATTN_SCALE).then_inc(s_pmexp, 1)
                elif kind == "score":
                    _, b, h = step
                    w = (b + 1) * P
                    act.wait_ge(s_nmax, scores.at((b, h)))
                    act.activation(prob[:, h, 0:w], prob[:, h, 0:w], ACT.Exp, bias=nmax[:, h:h + 1],
                                   scale=ATTN_SCALE, accum_out=psums[:, h:h + 1]).then_inc(s_exp, 1)
                elif kind == "probT":
                    _, b, h = step
                    n = probTs.n[(b, h)]
                    w = (b + 1) * P
                    tr.wait_full(act, step)
                    if n >= 2:
                        act.wait_ge(s_pv, n - 1)
                    act.activation(probT[:, n % 2, 0:w], bank[tr.bank[step]][:, 0:w], ACT.Copy)\
                        .then_inc(tr.freed(step), 1)
                elif kind == "metaT":
                    tr.wait_full(act, step)
                    if step[1]:
                        mi.wait_full(act, ("attn", step[1] - 1))
                    act.activation(pmT[:, :], bank[tr.bank[step]][:, 0:P], ACT.Copy).then_inc(tr.freed(step), 1)
                elif kind == "attn":
                    mi.wait_freed(act, step)
                    act.activation(rows[:, 1, :], attn_row, ACT.Square, accum_out=ms_a).then_inc(s_asq, 1)
                elif kind == "mixT":
                    _, t, half = step
                    tr.wait_full(act, step)
                    act.activation(hT_hi[:, 4 * half:4 * half + 4, cols_of(t)],
                                   bank[tr.bank[step]][:, :].rearrange("p (k t) -> p k t", k=4), ACT.Copy)\
                        .then_inc(s_mhi, 1)
                elif kind == "final":
                    t = step[1]
                    pj.wait_freed(act, ("o1", t))
                    if finals.n[t]:
                        act.wait_ge(s_ysq, finals.n[t])
                    act.activation(rows[:, :, :].rearrange("p a b -> p (a b)"), y[:, t, :], ACT.Square,
                                   accum_out=ms_f[:, t:t + 1]).then_inc(s_ysq, 1)

        @block.vector
        def _(dve):
            steps = [0]

            def mark(ins):
                steps[0] += 1
                ins.then_inc(s_v, 1)
                return steps[0]

            def link(ins):
                dve.wait_ge(s_v, mark(ins))

            def over_heads(ap, n=HEADS, d=HD):
                return ap.rearrange("p (h o) -> p h o", o=1).broadcast_to([P, n, d])

            def rope(rot, rot_swapped, c, sn, tmp):
                mark(dve.tensor_tensor(tmp, rot_swapped, sn, ALU.mult))
                dve.wait_ge(s_v, steps[0])
                link(dve.tensor_tensor(rot, rot, c, ALU.mult))
                return dve.tensor_tensor(rot, rot, tmp, ALU.add)

            def silu(u, dst):
                z = temp_of(u)
                dve.wait_ge(s_tanh, silus.at(u))
                dve.scalar_tensor_tensor(out=dst, in0=z, scalar=1.0, in1=bank[pj.bank[u]][:, :], op0=ALU.add,
                                         op1=ALU.mult).then_inc(pj.freed(u), 1)

            dve.wait_ge(s_logits, 16)
            link(dve.tensor_tensor(lb, logits[:, 0, :], logits[:, 1, :], ALU.max))
            link(dve.tensor_tensor(logits[:, 0, :], logits[:, 0, :], lb, ALU.subtract))
            dve.tensor_tensor(logits[:, 1, :], logits[:, 1, :], lb, ALU.subtract).then_inc(s_lbexp, 1)
            dve.wait_ge(s_gb, 16)

            def floors():
                dve.wait_ge(s_lb, 1)
                link(dve.tensor_tensor(half_span, logits[:, 0, :], logits[:, 1, :], ALU.add))
                link(dve.reciprocal(half_span, half_span))
                link(dve.tensor_tensor(lb, logits[:, 0, :], half_span, ALU.mult))
                link(dve.tensor_scalar(half_span, lb, -0.5, 0.5, ALU.mult, ALU.add))
                link(dve.tensor_tensor(middle, lb, half_span, ALU.add))
                dve.wait_ge(s_tab, 2)
                link(dve.memset(A[:, :, :], 0.0))
                dve.wait_ge(s_const, 16 * CONSTS)
                masks = hqT[:, 0:2, :].rearrange("p a b -> p (a b)")[:, 0:(PIECES - 1) * P]
                link(dve.tensor_copy(kept[:, :, :].rearrange("p j t -> p (j t)"), masks))

            last_round = {}
            for step in SCHEDULE:
                kind = step[0]
                if kind == "norm":
                    t = step[1]
                    r = rows_of(t)
                    xt = x_t[0:r, norms.n[t] % 3, :]
                    dve.wait_ge(s_rstd, norms.at(t))
                    dve.scalar_tensor_tensor(out=xt, in0=xt, scalar=rs_x[0:r, t:t + 1], in1=gb[0:r, :],
                                             op0=ALU.mult, op1=ALU.mult).then_inc(s_xn, 1)
                    if norms.n[t] == 1:
                        floors()
                elif kind == "hT" or kind == "mixT":
                    _, t, half = step
                    r = rows_of(t)
                    if kind == "hT":
                        dve.wait_ge(s_hhi, hTs.at(step))
                    else:
                        dve.wait_ge(s_mhi, mixTs.at(step[1:]))
                    at = (slice(None), slice(4 * half, 4 * half + 4), cols_of(t))
                    dve.tensor_tensor(hT_lo[at], bank[tr.bank[step]][:, :].rearrange("p (k t) -> p k t", k=4)[:, :, 0:r],
                                      hT_hi[at].bitcast(F32), ALU.subtract).then_inc(tr.freed(step), 1)
                elif kind == "weights" and step[1:] in lo_dve.n:
                    g, q = step[1:]
                    n = quarters.n[(g, q)]
                    dve.wait_ge(s_whi, n + 1)
                    for j in range(KQ):
                        raw, hi = w_raw[:, n % RAW, j, :], w_hi[:, n % RING, j, :].bitcast(F32)
                        if g == "hf":
                            ins = dve.tensor_tensor(w_lo[:, n % RING, j, :], raw, hi, ALU.subtract)
                        else:
                            k = q * KQ + j
                            ins = dve.scalar_tensor_tensor(out=w_lo[:, n % RING, j, :], in0=raw,
                                                           scalar=gcol[:, k:k + 1], in1=hi,
                                                           op0=ALU.mult, op1=ALU.subtract)
                    ins.then_inc(s_wlo_dve, 1)
                elif kind == "proj":
                    g, t = u = step[1:]
                    if g == "hf":
                        r = rows_of(t)
                        z = temp_of(u)
                        pj.wait_freed(dve, u)
                        link(dve.tensor_tensor(z, z, half_span[0:r, :], ALU.mult))
                        link(dve.tensor_tensor(f_of(t), z, middle[0:r, :], ALU.add))
                        dve.tensor_scalar(hk[0:r, t, :], f_of(t), -1.0, 1.0, ALU.mult, ALU.add).then_inc(s_fk, 1)
                    elif g == "hq":
                        silu(u, hqT[:, t, :])
                    elif g == "hg":
                        silu(u, mixH[:, t, :])
                    elif g == "ag":
                        silu(u, mixA[:, t, :])
                    elif g in ("iq", "ak", "aq"):
                        r = rows_of(t)
                        pj.wait_freed(dve, u)
                        v = rows[0:r, ropes.n[u] % 2, :].rearrange("p (h a two k) -> p h a two k", h=HEADS, a=4, two=2)
                        rot, rev = v[:, :, 0, :, :], v[:, :, 0, ::-1, :]
                        shape = [r, HEADS, 2, 8]
                        c = cos[0:r, t, :].rearrange("p (o two k) -> p o two k", o=1, two=2).broadcast_to(shape)
                        sn = sin[0:r, t, :].rearrange("p (o two k) -> p o two k", o=1, two=2).broadcast_to(shape)
                        tmp = swapped[0:r, :].rearrange("p (h two k) -> p h two k", h=HEADS, two=2)
                        rope(rot, rev, c, sn, tmp).then_inc(s_rope, 1)
                    elif g in ("o0", "o1"):
                        half = int(g == "o1")
                        pj.wait_full(dve, u)
                        if not half:
                            dve.wait_ge(s_xres[t], 16)
                        yt = y[:, t, half * 512:(half + 1) * 512]
                        dve.tensor_tensor(yt, yt, bank[pj.bank[u]][:, :], ALU.add).then_inc(pj.freed(u), 1)
                elif kind == "ikT":
                    tr.wait_freed(dve, step)
                    key, two, sq = ik_row[:, :, 0:64], ik_two[:, :, 0, :], ik_two[:, :, 1, :]
                    per_tile = [P, TILES, 64]
                    link(dve.tensor_reduce(ik_mean, key, AX.X, ALU.add))
                    link(dve.tensor_scalar(ik_mean, ik_mean, 1.0 / 64, None, ALU.mult))
                    link(dve.tensor_tensor(two, key, over_heads(ik_mean, TILES, 64), ALU.subtract))
                    link(dve.tensor_tensor(sq, two, two, ALU.mult))
                    dve.tensor_reduce(ik_var, sq, AX.X, ALU.add).then_inc(s_ikvar, 1)
                    link(dve.tensor_scalar(idxw[:, :, :], ik_row[:, :, 64:72], IDX_SCALE, None, ALU.mult))
                    dve.wait_ge(s_ikrs, 1)
                    dve.wait_ge(s_idxg, 32)
                    gain = idx_gb[:, 0:1, :].broadcast_to(per_tile)
                    shift = idx_gb[:, 1:2, :].broadcast_to(per_tile)
                    link(dve.tensor_tensor(two, two, over_heads(ik_rs, TILES, 64), ALU.mult))
                    link(dve.tensor_tensor(two, two, gain, ALU.mult))
                    link(dve.tensor_tensor(two, two, shift, ALU.add))
                    v = two.rearrange("p t (a two k) -> p t a two k", a=4, two=2)
                    as_pairs = lambda ap: ap.rearrange("p t (two k) -> p t two k", two=2)
                    link(rope(v[:, :, 0, :, :], v[:, :, 0, ::-1, :], as_pairs(cos[:, 0:TILES, :]),
                              as_pairs(sin[:, 0:TILES, :]),
                              swapped[:, 0:64].rearrange("p (t two k) -> p t two k", t=TILES, two=2)))
                    dve.tensor_copy(sq, two).then_inc(s_iktwo, 1)
                elif kind == "index":
                    _, b, h = step
                    n = rels.n[(b, h)]
                    w = (b + 1) * P
                    wgt = idxw[:, b, h:h + 1]
                    sd.wait_freed(dve, step)
                    if h == 0:
                        dve.tensor_scalar(bias[b][:, :], rel[:, n % 2, 0:w], wgt, None, ALU.mult).then_inc(s_acc, 1)
                    else:
                        dve.wait_ge(s_acc, n)
                        dve.scalar_tensor_tensor(out=bias[b][:, :], in0=rel[:, n % 2, 0:w], scalar=wgt, in1=bias[b][:, :],
                                                 op0=ALU.mult, op1=ALU.add).then_inc(s_acc, 1)
                    if h == 7:
                        dve.wait_ge(s_acc, n + 1)
                        diag = bias[b][:, b * P:w]
                        last_round[b] = mark(dve.tensor_tensor(diag, diag, bias[0][:, :], ALU.add))
                elif kind == "topk":
                    found = {}
                    for b in range(1, TILES):
                        dve.wait_ge(s_v, last_round[b])
                        found[b] = mark(dve.max(top8[:, b, :], bias[b][:, :]))
                    for b in range(1, TILES):
                        dve.wait_ge(s_v, found[b])
                        last_round[b] = mark(dve.match_replace(bias[b][:, :], top8[:, b, :], bias[b][:, :], TAKEN))
                elif kind == "biases":
                    for b in range(1, TILES):
                        dve.wait_ge(s_v, last_round[b])
                        last_round[b] = mark(dve.tensor_scalar(bias[b][:, :], bias[b][:, :], 0.5 * TAKEN, NEG,
                                                               ALU.is_gt, ALU.mult))
                elif kind == "gated":
                    _, t, hp = step
                    for half in range(2):
                        sd.wait_freed(dve, ("decay", t, 2 * hp + 1, half))
                    tr.wait_freed(dve, ("kT", t))
                    pair = slice(2 * hp, 2 * hp + 2)
                    keys, queries = hkT[:, pair, :], hqT[:, pair, t * P:(t + 1) * P]
                    for l in range(LEVELS):
                        def halves(ap):
                            return ap.rearrange("p h (b two m) -> p h b two m", two=2, m=1 << l)
                        e = halves(E[:, l, :, :])
                        for side, z in ((0, keys), (1, queries)):
                            dve.tensor_tensor(e[:, :, :, side, :], e[:, :, :, side, :], halves(z)[:, :, :, side, :],
                                              ALU.mult)
                    if hp == 0 and t:
                        mi.wait_full(dve, ("out", t - 1))
                    dve.tensor_copy(decay_end[:, t % 2, pair], E[:, INF_LEVEL, :, P - 1])
                    dve.tensor_tensor(q_inf[:, pair, :], E[:, INF_LEVEL, :, :], queries, ALU.mult).then_inc(s_X, 1)
                elif kind == "pieces":
                    _, t, hp = step
                    pair = slice(2 * hp, 2 * hp + 2)
                    if hp == 0 and t:
                        mi.wait_full(dve, ("out", t - 1))
                    for j in range(PIECES):
                        key = step + (j,)
                        src = bank[mi.bank[key]][:, 0:2 * P].rearrange("p (h t) -> p h t", h=2)
                        mi.wait_full(dve, key)
                        if j == 0:
                            for s0, s1, t0, t1 in BLOCKS:
                                ins = dve.tensor_copy(A[s0:s1, pair, t0:t1], src[s0:s1, :, t0:t1])
                        else:
                            mi.wait_freed(dve, step + (j - 1,))
                            ins = dve.copy_predicated(A[:, pair, :], kept[:, j - 1:j, :].broadcast_to([P, 2, P]), src)
                        ins.then_inc(mi.freed(key), 1)
                elif kind == "suffix":
                    t = step[1]
                    r = rows_of(t)
                    mi.wait_freed(dve, step)
                    dve.tensor_tensor(k_end[0:r, :], k_end[0:r, :], hk[0:r, t, :], ALU.mult).then_inc(s_kend, 1)
                elif kind == "state":
                    t = step[1]
                    mi.wait_full(dve, step)
                    if t == META:
                        dve.tensor_copy(S[:, :, :], bank[6][:, :].rearrange("p (h v) -> p h v", h=GH))\
                            .then_inc(mi.freed(step), 1)
                    else:
                        mi.wait_full(dve, ("out", t))
                        for h in range(GH):
                            ins = dve.scalar_tensor_tensor(out=S[:, h, :], in0=S[:, h, :],
                                                           scalar=decay_end[:, t % 2, h:h + 1],
                                                           in1=bank[6][:, h * GK:(h + 1) * GK],
                                                           op0=ALU.mult, op1=ALU.add)
                        ins.then_inc(mi.freed(step), 1)
                elif kind == "mixH":
                    t = step[1]
                    dve.wait_ge(s_ors, mixHs.at(t))
                    o4 = o_row[:, :].rearrange("p (h v) -> p h v", h=GH)
                    link(dve.tensor_tensor(o4, o4, over_heads(rs_h, GH, GK), ALU.mult))
                    dve.scalar_tensor_tensor(out=mixH[:, t, :], in0=mixH[:, t, :], scalar=0.5, in1=o_row[:, :],
                                             op0=ALU.mult, op1=ALU.mult).then_inc(s_mixH, 1)
                elif kind == "meta":
                    mi.wait_freed(dve, step)
                    link(dve.tensor_reduce(mmax, pm[:, :].rearrange("p (h m) -> p h m", h=HEADS), AX.X, ALU.max))
                elif kind == "score":
                    _, b, h = step
                    w = (b + 1) * P
                    sd.wait_full(dve, step)
                    if b:
                        tr.wait_full(dve, ("probT", b - 1, h))
                    dve.tensor_tensor_reduce(prob[:, h, 0:w], bank[sd.bank[step]][:, 0:w], bias[b][:, :], 1.0,
                                             mmax[:, h:h + 1], ALU.add, ALU.max, pmax[:, h:h + 1])\
                        .then_inc(sd.freed(step), 1)
                    sd.wait_freed(dve, step)
                    dve.tensor_scalar(nmax[:, h:h + 1], pmax[:, h:h + 1], -ATTN_SCALE, None, ALU.mult)\
                        .then_inc(s_nmax, 1)
                elif kind == "pmeta":
                    pm3 = pm[:, :].rearrange("p (h m) -> p h m", h=HEADS)
                    dve.tensor_tensor(pm3, pm3, over_heads(pmax, HEADS, NMETA), ALU.subtract).then_inc(s_pmsub, 1)
                elif kind == "metaT":
                    b = step[1]
                    dve.wait_ge(s_pmexp, pmetas.at(b))
                    dve.wait_ge(s_exp, scores.at((b, HEADS - 1)))
                    link(dve.tensor_reduce(msum, pm[:, :].rearrange("p (h m) -> p h m", h=HEADS), AX.X, ALU.add))
                    link(dve.tensor_tensor(msum, msum, psums, ALU.add))
                    link(dve.reciprocal(prec, msum))
                elif kind == "attn":
                    b = step[1]
                    mi.wait_full(dve, step)
                    dve.tensor_tensor(attn_row.rearrange("p (h d) -> p h d", h=HEADS),
                                      bank[7][:, :].rearrange("p (h d) -> p h d", h=HEADS), over_heads(prec), ALU.mult)\
                        .then_inc(mi.freed(step), 1)
                    dve.wait_ge(s_ars, attns.at(b))
                    dve.scalar_tensor_tensor(out=mixA[:, b, :], in0=attn_row, scalar=rs_a, in1=mixA[:, b, :],
                                             op0=ALU.mult, op1=ALU.mult).then_inc(s_mixA, 1)
                elif kind == "final":
                    t = step[1]
                    dve.wait_ge(s_yrs, finals.at(t))
                    dve.wait_ge(s_fb, 16)
                    dve.scalar_tensor_tensor(out=y[:, t, :], in0=y[:, t, :], scalar=rs_f[:, t:t + 1], in1=fb[:, :],
                                             op0=ALU.mult, op1=ALU.mult).then_inc(s_fin, 1)

        @block.tensor
        def _(pe):
            pe.wait_ge(s_const, 16 * CONSTS)
            ready = set()

            def transposes(step, sources, width=P):
                b = bank[tr.bank[step]]
                tr.wait_free(pe, step)
                for i, src in enumerate(sources):
                    r, c = src.shape
                    ins = pe.transpose(b[0:c, width * i:width * i + r], src, ident[0:r, 0:r])
                ins.then_inc(full["tr"], 1)

            def project(u):
                g, t = u
                r = P if g == "hq" else rows_of(t)
                width = GROUPS[g][1]
                n0 = quarters.n[(g, 0)]
                cols = slice(0, SEQ) if g in ("hq", "ikw") else cols_of(t)
                b = bank[pj.bank[u]]
                if g in ("o0", "o1"):
                    for half in range(2):
                        tr.wait_freed(pe, ("mixT", t, half))
                else:
                    for tt in ([0, 1, 2, 3] if g in ("hq", "ikw") else [t]):
                        for half in range(2):
                            tr.wait_freed(pe, ("hT", tt, half))
                pj.wait_free(pe, u)
                last_unit = u[1] == GROUPS[g][2][-1]
                for k in range(KC):
                    q, j = divmod(k, KQ)
                    slot = (n0 + q) % RING
                    if (g, q) not in ready:
                        wait_lo(pe, (g, q))
                        ready.add((g, q))
                    h_hi, h_lo = hT_hi[:, k, cols], hT_lo[:, k, cols]
                    m_hi, m_lo = w_hi[:, slot, j, 0:width], w_lo[:, slot, j, 0:width]
                    if g == "hq":
                        c = slice(t * P, (t + 1) * P)
                        pairs = [(m_hi[:, c], h_hi), (m_hi[:, c], h_lo), (m_lo[:, c], h_hi)]
                    elif g == "ikw":
                        pairs = [(m_hi, h_hi), (m_hi, h_lo), (m_lo, h_hi)]
                    else:
                        pairs = [(h_hi, m_hi), (h_hi, m_lo), (h_lo, m_hi)]
                    dst = b[0:IKW, :] if g == "ikw" else b[0:r, 0:512]
                    for i, (a, m) in enumerate(pairs):
                        ins = pe.matmul(dst, a, m, start=(k == 0 and i == 0), stop=(k == KC - 1 and i == 2))
                    if k == KC - 1:
                        ins.then_inc(full["pj"], 1)
                    elif last_unit and j == KQ - 1:
                        ins.then_inc(s_wused, 1)

            for step in SCHEDULE:
                kind = step[0]
                if kind == "hT":
                    _, t, half = step
                    r = rows_of(t)
                    pe.wait_ge(s_xn, norms.at(t))
                    transposes(step, [x_t[0:r, norms.n[t] % 3, k * P:(k + 1) * P] for k in range(4 * half, 4 * half + 4)])
                elif kind == "proj":
                    project(step[1:])
                elif kind == "ikT":
                    pj.wait_freed(pe, ("ikw", 0))
                    transposes(step, [ikT[0:IKW, t * P:(t + 1) * P] for t in range(TILES)], IKW_TURNED)
                elif kind == "kiT":
                    pe.wait_ge(s_iktwo, 1)
                    transposes(step, [ik_two[:, t, :, :].rearrange("p two d -> p (two d)") for t in range(TILES)])
                elif kind == "ropeT":
                    _, g, t = step
                    r = rows_of(t)
                    pe.wait_ge(s_rope, ropes.at((g, t)))
                    transposes(step, [rows[0:r, ropes.n[(g, t)] % 2, j * P:(j + 1) * P] for j in range(4)])
                elif kind == "kT":
                    t = step[1]
                    pe.wait_ge(s_fk, hfs.at(t))
                    transposes(step, [hk[:, t, j * P:(j + 1) * P] for j in range(4)])
                elif kind == "index":
                    _, b, h = step
                    sd.wait_free(pe, step)
                    tr.wait_freed(pe, ("ropeT", "iq", b))
                    tr.wait_freed(pe, ("kiT",))
                    lanes = slice(64 * (h % 2), 64 * (h % 2) + 64)
                    w = (b + 1) * P
                    pe.matmul(bank[sd.bank[step]][:, 0:w], qiT[lanes, h // 2, (b - 1) * P:b * P], kiT[lanes, 0:w],
                              start=True, stop=True).then_inc(full["sd"], 1)
                elif kind == "decay":
                    _, t, h = step
                    pe.wait_ge(s_glo, hfs.at(t))
                    for half in range(2):
                        key = step + (half,)
                        sd.wait_free(pe, key)
                        b = bank[sd.bank[key]]
                        m = sums[:, 4 * half:4 * half + 4, :].rearrange("p l t -> p (l t)")
                        pe.matmul(b[:, :], g_hi[:, t, h * GK:(h + 1) * GK], m, start=True, stop=False)
                        pe.matmul(b[:, :], g_lo[:, t, h * GK:(h + 1) * GK], m, start=False, stop=True)\
                            .then_inc(full["sd"], 1)
                elif kind == "suffix":
                    t = step[1]
                    r = rows_of(t)
                    pe.wait_ge(s_glo, hfs.at(t))
                    mi.wait_free(pe, step)
                    pe.matmul(bank[6][0:r, :], after[0:r, 0:r], g_hi[0:r, t, :], start=True, stop=False)
                    pe.matmul(bank[6][0:r, :], after[0:r, 0:r], g_lo[0:r, t, :], start=False, stop=True)\
                        .then_inc(full["mi"], 1)
                elif kind == "state":
                    t = step[1]
                    r = rows_of(t)
                    pe.wait_ge(s_kend, suffixes.at(t))
                    pj.wait_freed(pe, ("hi", t))
                    mi.wait_free(pe, step)
                    for h in range(GH):
                        c = slice(h * GK, (h + 1) * GK)
                        ins = pe.matmul(bank[6][:, c], k_end[0:r, c], hv[0:r, t, c], start=True, stop=True)
                    ins.then_inc(full["mi"], 1)
                elif kind == "pieces":
                    _, t, hp = step
                    pe.wait_ge(s_X, gateds.at((t, hp)))
                    for j in range(PIECES):
                        key = step + (j,)
                        b = bank[mi.bank[key]]
                        mi.wait_free(pe, key)
                        for i in range(2):
                            h = 2 * hp + i
                            if j == 0:
                                for s0, s1, t0, t1 in BLOCKS:
                                    e = E[:, 6 if s1 == 64 else 5, i, :]
                                    ins = pe.matmul(b[s0:s1, i * P + t0:i * P + t1], e[:, s0:s1], e[:, t0:t1],
                                                    start=True, stop=True)
                            elif j < PIECES - 1:
                                e = E[:, 5 - j, i, :]
                                ins = pe.matmul(b[:, i * P:(i + 1) * P], e, e, start=True, stop=True)
                            else:
                                ins = pe.matmul(b[:, i * P:(i + 1) * P], hkT[:, h, :], hqT[:, h, t * P:(t + 1) * P],
                                                start=True, stop=True)
                        ins.then_inc(full["mi"], 1)
                elif kind == "out":
                    t = step[1]
                    mi.wait_freed(pe, ("pieces", t, 1, PIECES - 1))
                    prev = states.keys[outs.n[t]]
                    mi.wait_freed(pe, ("state", prev))
                    mi.wait_free(pe, step)
                    for h in range(GH):
                        c = slice(h * GK, (h + 1) * GK)
                        pe.matmul(bank[7][:, c], A[:, h, :], hv[:, t, c], start=True, stop=False)
                        ins = pe.matmul(bank[7][:, c], q_inf[:, h, :], S[:, h, :], start=False, stop=True)
                    ins.then_inc(full["mi"], 1)
                elif kind == "meta":
                    b = step[1]
                    tr.wait_freed(pe, ("ropeT", "ak", META))
                    tr.wait_freed(pe, ("ropeT", "aq", b))
                    mi.wait_free(pe, step)
                    for j in range(4):
                        ins = pe.matmul(bank[6][:, 32 * j:32 * j + 32], qT[:, j, b * P:(b + 1) * P], kmT[:, j, :],
                                        start=True, stop=True)
                    ins.then_inc(full["mi"], 1)
                elif kind == "score":
                    _, b, h = step
                    tr.wait_freed(pe, ("ropeT", "ak", b))
                    sd.wait_free(pe, step)
                    lanes = slice(64 * (h % 2), 64 * (h % 2) + 64)
                    w = (b + 1) * P
                    pe.matmul(bank[sd.bank[step]][:, 0:w], qT[lanes, h // 2, b * P:(b + 1) * P], kT[lanes, h // 2, 0:w],
                              start=True, stop=True).then_inc(full["sd"], 1)
                elif kind == "probT":
                    _, b, h = step
                    pe.wait_ge(s_exp, scores.at((b, h)))
                    transposes(step, [prob[:, h, j * P:(j + 1) * P] for j in range(b + 1)])
                elif kind == "pv":
                    _, b, h = step
                    n = probTs.n[(b, h)]
                    tr.wait_freed(pe, ("probT", b, h))
                    if h == 0:
                        mi.wait_free(pe, ("attn", b))
                        for t in range(b + 1):
                            pj.wait_freed(pe, ("av", t))
                    c = slice(h * HD, (h + 1) * HD)
                    for j in range(b + 1):
                        ins = pe.matmul(bank[7][:, c], probT[:, n % 2, j * P:(j + 1) * P], V[:, j, c],
                                        start=(h == 0 and j == 0), stop=False, skip_group_check=True)
                    ins.then_inc(s_pv, 1)
                elif kind == "metaT":
                    b = step[1]
                    pe.wait_ge(s_pmexp, pmetas.at(b))
                    transposes(step, [pm[:, :]])
                elif kind == "attn":
                    b = step[1]
                    tr.wait_freed(pe, ("metaT", b))
                    pe.wait_ge(s_vm, 16 * HEADS)
                    pe.matmul(bank[7][:, :], pmT[:, :], V_meta[:, :], start=False, stop=True, skip_group_check=True)\
                        .then_inc(full["mi"], 1)
                elif kind == "mixT":
                    _, t, half = step
                    if half == 0:
                        pe.wait_ge(s_mixA, attns.at(t))
                    else:
                        pe.wait_ge(s_mixH, mixHs.at(t))
                    src = mixH if half else mixA
                    transposes(step, [src[:, t, j * P:(j + 1) * P] for j in range(4)])


def program(nc, arrays, out_shape):
    aps = []
    for name, a in arrays.items():
        aps.append(nc.dram_tensor(name, a.shape, mybir.dt.from_np(a.dtype), kind="ExternalInput").ap())
    aps.append(nc.dram_tensor("out_0_dram", out_shape, F32, kind="ExternalOutput").ap())
    hymba_layer(nc, *aps)


_INS = ["x", "meta_tokens", "mix_norm", "w_in", "idx_k_norm_g", "idx_k_norm_b", "attn_out_norm",
        "hgrn_lb_logits", "hgrn_out_norm", "w_out", "final_norm"]


def kernel(**inputs):
    import concourse.bacc as bacc
    from concourse.bass_utils import run_bass_kernel_spmd

    nc = bacc.Bacc("TRN2", target_bir_lowering=False, num_devices=1)
    arrays = {f"in_{n}": np.ascontiguousarray(inputs[n]) for n in _INS}
    sums, after, kept = level_tables()
    cos, sin = rope_tables()
    causal = np.where(np.arange(P)[None, :] <= np.arange(P)[:, None], 0.0, NEG).astype(np.float32)
    arrays |= {"t_ident": np.eye(P, dtype=np.float32), "t_cos": cos, "t_sin": sin,
               "t_sums": sums.reshape(P, -1), "t_after": after, "t_kept": kept, "t_causal": causal}
    program(nc, arrays, inputs["x"].shape)
    r = run_bass_kernel_spmd(nc, [arrays], core_ids=[0])
    return r.results[0]["out_0_dram"]
```

```python
from contextlib import ExitStack

import numpy as np

import concourse.bass as bass
from concourse import mybir

ACT = mybir.ActivationFunctionType
ALU = mybir.AluOpType
AX = mybir.AxisListType
F32 = mybir.dt.float32
F32R = mybir.dt.float32r
U8 = mybir.dt.uint8

P = 128
SEQ, D, NMETA = 512, 1024, 16
HEADS, HD = 8, 64
AW = HEADS * HD
GH, GK = 4, 128
TILES = SEQ // P
META = TILES
KC = D // P
QUARTERS = 4
KQ = KC // QUARTERS
TOPK = min(256, SEQ // 4)
RAW, RING, PROBS = 3, 6, 4
LEVELS = 7
TOP_OPS = 9
LAG = 5
INF_LEVEL = LEVELS
EPS = 1e-6
ATTN_SCALE = HD ** -0.5
IDX_SCALE = (8 ** -0.5) * (64 ** -0.5)
NEG = -1.0e30
TAKEN = -3.0e38
IKW = 72

GROUPS = {
    "hf": (3144, 512, [0, 1, 2, 3, META]),
    "ikw": (2560, IKW, [0]),
    "iq": (2048, 512, [1, 2, 3]),
    "hi": (3656, 512, [META, 0, 1, 2, 3]),
    "hq": (2632, 512, [0, 1, 2, 3]),
    "hg": (4168, 512, [0, 1, 2, 3]),
    "ag": (1536, 512, [0, 1, 2, 3]),
    "ak": (512, 512, [META, 0, 1, 2, 3]),
    "aq": (0, 512, [0, 1, 2, 3]),
    "av": (1024, 512, [META, 0, 1, 2, 3]),
    "o0": (0, 512, [0, 1, 2, 3]),
    "o1": (512, 512, [0, 1, 2, 3]),
}
ORDER = list(GROUPS)


def row_chunk(g, k):
    return (k + KC // 2) % KC if g in ("o0", "o1") else k


def level_tables():
    u, p = np.meshgrid(np.arange(P), np.arange(P), indexing="ij")
    sums = np.zeros((P, LEVELS + 1, P), np.float32)
    for l in range(LEVELS):
        m = 1 << l
        mid = (p // (2 * m)) * 2 * m + m
        key = p < mid
        sums[:, l] = np.where(key, (u > p) & (u < mid), (u >= mid) & (u <= p))
    sums[:, INF_LEVEL] = u <= p
    after = (u > p).astype(np.float32)
    s, t = u, p
    level = np.full((P, P), -1)
    for l in range(LEVELS):
        m = 1 << l
        mid = (s // (2 * m)) * 2 * m + m
        level[(s // (2 * m) == t // (2 * m)) & (s < mid) & (t >= mid)] = l
    pieces = [s == t] + [level == l for l in (4, 3, 2, 1, 0)]
    kept = np.stack(pieces, 1).astype(np.float32)
    return sums, after, kept


PIECES = 7
BLOCKS = [(0, 64, 64, 128), (0, 32, 32, 64), (64, 96, 96, 128)]


def rope_tables():
    half = HD // 4 // 2
    inv = np.float32(500000.0) ** (-np.arange(half, dtype=np.float32) * np.float32(2.0) / np.float32(2 * half))
    pos = np.zeros((P, TILES + 1), np.float32)
    for t in range(TILES):
        pos[:, t] = NMETA + t * P + np.arange(P)
    pos[:NMETA, META] = np.arange(NMETA)
    ang = (pos[:, :, None] * inv.astype(np.float32)).astype(np.float32)
    cos, sin = np.cos(ang.astype(np.float64)), np.sin(ang.astype(np.float64))
    return (np.concatenate([cos, cos], 2).astype(np.float32), np.concatenate([-sin, sin], 2).astype(np.float32))


def schedule():
    s = []

    def proj(g, i):
        s.append(("proj", g, GROUPS[g][2][i]))

    def weights(g, *qs):
        s.extend(("weights", g, q) for q in qs)

    def group(g, between=None):
        units = GROUPS[g][2]
        nxt = ORDER[ORDER.index(g) + 1] if g != ORDER[-1] else None
        between, last = between or {}, len(s)
        for i in range(len(units)):
            early = [q for q in range(2) if nxt and i == max(0, min(q + 1, len(units) - 2))]
            if len(units) == 1:
                weights(nxt, *early)
            if i == len(units) - 1 and nxt:
                n = len(s) - last
                s.insert(last + (n * 2 // 3 if i else n), ("weights", nxt, 2))
                s.append(("weights", nxt, 3))
            proj(g, i)
            if len(units) > 1:
                weights(nxt, *early)
            last = len(s)
            s.extend(between.get(i, []))

    def gates(t, hp, levels):
        return [("gate", t, hp, l) for l in levels]

    def turn(t, hp):
        last = (t, hp) == (TILES - 1, 1)
        nt, nhp = (t, 1) if hp == 0 else (t + 1, 0)
        out = [("piece", t, hp, 0)]
        out += [("piece", t, hp, 1), ("piece", t, hp, 2)]
        if hp == 0 and t:
            out += [("state", t - 1)]
        out += gates(t, hp, [3, 2, 1, 0, INF_LEVEL])
        if last:
            return out + [("piece", t, hp, j) for j in range(3, PIECES)] + [("out", t), ("mixH", t)]
        if hp == 1:
            out += [("suffix", t), ("kT", nt)]
        out += [("decay", nt, nhp, 1)]
        for j in range(3, PIECES):
            out += [("piece", t, hp, j)]
            if j < PIECES - 1:
                out += gates(nt, nhp, [LEVELS + 2 - j])
        out += [("decay", nt, nhp, 0)]
        if hp == 0 and t:
            out += [("mixH", t - 1)]
        if hp == 1:
            out += [("out", t)]
        return out

    def with_gate(g, t, steps):
        i = next(i for i, s in enumerate(steps) if s[0] == "gate" and s[3] == INF_LEVEL)
        return steps[:i + 1] + [("silu", g, t)] + steps[i + 1:]

    def index(b):
        return [("index", b, h) for h in range(8)]

    def attend(first, last):
        out = []
        for n in range(first, last):
            b, h = divmod(n, HEADS)
            if b < TILES:
                out.append(("probT", b, h))
            ahead, ah = divmod(n + 3, HEADS)
            if ahead < TILES:
                if ah == 0:
                    out.append(("meta", ahead))
                out.append(("score", ahead, ah))
                if ah == HEADS - 1:
                    out.append(("pmeta", ahead))
            if n:
                pb, ph = divmod(n - 1, HEADS)
                if pb < TILES:
                    out.append(("pv", pb, ph))
                if ph == HEADS - 3:
                    out.append(("metaT", pb))
                if ph == HEADS - 1:
                    out.append(("attn", pb))
                if ph == 1 and pb:
                    out.append(("mixA", pb - 1))
                if ph == 2 and pb:
                    out.append(("mixT", pb - 1, 0))
        return out

    rounds = [(kind, r, b) for r in range(TOPK // 8) for kind in ("find", "take") for b in range(1, TILES)]

    def top(n, steps=()):
        out, steps, n = [], list(steps), min(n, len(rounds))
        for i in range(n):
            out.append(rounds.pop(0))
            out += steps[len(steps) * i // n:len(steps) * (i + 1) // n]
        return out + (steps if n == 0 else [])

    s += [("norm", 0)]
    weights("hf", 0)
    s += [("hT", 0, 0), ("hT", 0, 1)]
    s += [("norm", 1)]
    weights("hf", 1, 2)
    s += [("hT", 1, 0), ("hT", 1, 1), ("norm", 2)]
    weights("hf", 3)
    s += [("floor", 0)]
    group("hf", {0: [("hT", 2, 0), ("hT", 2, 1), ("norm", 3), ("floor", 1)],
                 1: [("hT", 3, 0), ("hT", 3, 1), ("norm", META), ("gate f", 0)],
                 2: [("gate f", 1), ("hT", META, 0), ("hT", META, 1)], 3: [("gate f", 2), ("gate f", 3)],
                 4: [("gate f", META)]})
    group("ikw", {0: [("ikT",)]})
    logs = [("log", t) for t in GROUPS["hf"][2]]
    group("iq", {0: [logs[0], ("kiT",), ("ropeT", "iq", 1)],
                 1: [logs[1], ("ropeT", "iq", 2)] + index(1),
                 2: [logs[2], ("ropeT", "iq", 3)] + index(2)[0:4]})
    T = TOP_OPS
    group("hi", {0: [logs[3]] + index(2)[4:], 1: [logs[4]] + index(3)[0:4], 2: index(3)[4:], 3: top(T), 4: top(T)})
    group("hq", {0: top(T, [("suffix", META), ("kT", 0)]), 1: top(T, [("state", META)]),
                 2: top(T, [("decay", 0, 0, 1), ("decay", 0, 0, 0)]),
                 3: top(T, gates(0, 0, [6, 5, 4]))})
    group("hg", {t: with_gate("hg", t, turn(t // 2, t % 2)) for t in range(TILES)})
    group("ag", {t: with_gate("ag", t, turn(2 + t // 2, t % 2)) for t in range(TILES)})
    group("ak", {0: top(T) + [("ropeT", "ak", META)], 1: top(T) + [("ropeT", "ak", 0)],
                 2: top(T) + [("ropeT", "ak", 1)], 3: top(T) + [("ropeT", "ak", 2)], 4: top(96)})
    group("aq", {0: [("biases",), ("ropeT", "ak", 3)], 1: [("ropeT", "aq", 0)], 2: [("ropeT", "aq", 1)], 3: [("ropeT", "aq", 2)]})
    group("av", {0: [("ropeT", "aq", 3), ("meta", 0), ("score", 0, 0), ("score", 0, 1), ("score", 0, 2)],
                 1: attend(0, 7), 2: attend(7, 13) + [("mixT", 0, 1)],
                 3: attend(13, 18) + [("mixT", 1, 1)], 4: [("mixT", 2, 1)] + attend(18, 22)})
    group("o0", {0: [("mixT", 3, 1)] + attend(22, 26), 1: attend(26, 30),
                 2: attend(30, 33) + [("mixA", 3), ("mixT", 3, 0)]})
    group("o1", {1: [("final", 0)], 2: [("final", 1)], 3: [("final", 2), ("final", 3)]})
    return s


SCHEDULE = schedule()


FILL = {"meta": 4, "kiT": 8, "ropeT": 2, "out": 2, "decay": 0.5, "state": 1, "index": 1, "score": 1,
        "probT": 1, "pv": 1, "metaT": 1, "attn": 1, "mixT": 1, "ikT": 1, "suffix": 1,
        "pieces": (0.6, 0.6, 1.2, 1, 1, 1.3, 1.3)}


def fill_before(step, part):
    if step[0] == "piece":
        return FILL["pieces"][step[3]]
    return FILL.get(step[0], 0)


def tensor_order():
    order, between = [], []
    for step in SCHEDULE:
        if step[0] == "proj":
            _, g, t = step
            needs = {}
            for i, (s, _) in enumerate(between):
                if s[0] == "hT" and (s[1] == t or g in ("hq", "ikw")) or g in ("o0", "o1") and s == ("mixT", t, 1):
                    needs[0] = i + 1
                if g in ("o0", "o1") and s == ("mixT", t, 0):
                    needs[KC // 2] = min(i + 1 + LAG, len(between))
            first = needs.get(0, 0)
            order += between[:first]
            between = between[first:]
            want = np.cumsum([fill_before(*s) for s in between])
            done = 0
            for k in range(KC):
                while k and done < needs.get(k, 0) - first:
                    order.append(between[done])
                    done += 1
                order.append((step, k))
                while done < len(between) and (k == KC - 1 or want[done] * (KC - 1) <= (k + 1) * want[-1]):
                    order.append(between[done])
                    done += 1
            between = []
        else:
            between.append((step, None))
    early = [(("proj", "o1", 0), k) for k in range(KC // 2)]
    order = [o for o in order if o not in early]
    wait = order.index((("mixT", TILES - 1, 0), None))
    return order[:wait] + early + order[wait:] + between


TENSOR_ORDER = tensor_order()


class Order:

    def __init__(self, keys):
        self.keys = list(keys)
        self.n = {k: i for i, k in enumerate(self.keys)}
        assert len(self.n) == len(self.keys), [k for k in self.keys if self.keys.count(k) > 1][:5]

    def at(self, key):
        return self.n[key] + 1


class Banks:

    def __init__(self, full, free, turns):
        self.full, self.free = full, free
        self.order = Order([k for k, _ in turns])
        self.bank = dict(turns)
        seen = {}
        self.turn = {}
        for k, b in turns:
            self.turn[k] = seen.get(b, 0)
            seen[b] = self.turn[k] + 1

    def wait_free(self, eng, key):
        if self.turn[key]:
            eng.wait_ge(self.free[self.bank[key]], self.turn[key])

    def wait_full(self, eng, key):
        eng.wait_ge(self.full, self.order.at(key))

    def wait_freed(self, eng, key):
        eng.wait_ge(self.free[self.bank[key]], self.turn[key] + 1)

    def freed(self, key):
        return self.free[self.bank[key]]


def units():
    return [s[1:] for s in SCHEDULE if s[0] == "proj"]


def hymba_layer(nc, x, meta_tokens, mix_norm, w_in, idx_g, idx_b, attn_g, lb_logits, hgrn_g, w_out,
                final_g, t_ident, t_cos, t_sin, t_sums, t_after, t_kept, t_causal, out):
    with ExitStack() as ctx:
        def sb(name, shape, dt=F32, where=ctx):
            return where.enter_context(nc.sbuf_tensor(name, shape, dt))

        def sem(name):
            return ctx.enter_context(nc.semaphore(name))

        hT_hi = sb("hT_hi", [P, KC, SEQ + NMETA], F32R)
        hT_lo = sb("hT_lo", [P, KC, SEQ + NMETA], F32R)
        w_raw = sb("w_raw", [P, RAW, KQ, 512])
        w_hi = sb("w_hi", [P, RING, KQ, 512], F32R)
        w_lo = sb("w_lo", [P, RING, KQ, 512], F32R)
        ident = sb("ident", [P, P])
        cos = sb("cos", [P, TILES + 1, 16])
        sin = sb("sin", [P, TILES + 1, 16])
        sums = sb("sums", [P, LEVELS + 1, P], F32R)
        after = sb("after", [P, P], F32R)
        kept = sb("kept", [P, PIECES - 1, P], U8)
        bias = [sb(f"bias{b}", [P, (b + 1) * P]) for b in range(TILES)]
        rows = sb("rows", [P, 2, 512])
        temp = sb("temp", [P, 2, 512])
        mixH = sb("mixH", [P, TILES, 512])
        small = sb("small", [P, 128])
        idxw = sb("idxw", [P, TILES, 8])
        mhalf = small[:, 0:8]
        sq_x, rs_x = small[:, 8:13], small[:, 13:18]
        ik_mean, ik_var, ik_rs = small[:, 18:22], small[:, 22:26], small[:, 26:30]
        ms_h, rs_h = small[:, 30:34], small[:, 34:38]
        mmax, pmax, nmax, psums = ([small[:, c + 8 * i:c + 8 * i + 8] for i in range(2)] for c in (38, 54, 88, 104))
        prec, msum = small[:, 70:78], small[:, 120:128]
        ms_a, rs_a = small[:, 78:79], small[:, 79:80]
        ms_f, rs_f = small[:, 80:84], small[:, 84:88]
        top8 = sb("top8", [P, TILES, 8])
        decay_end = sb("decay_end", [P, 2, GH])
        o_row = sb("o_row", [P, 512])
        junk = sb("junk", [P, P])
        swapped = sb("swapped", [P, P])

        with ExitStack() as r1:
            x_t = sb("x_t", [P, 3, D], where=r1)
            gb = sb("gb", [P, D], where=r1)
        with ExitStack() as r1:
            qiT = sb("qiT", [P, 4, 3 * P], where=r1)
            kiT = sb("kiT", [P, SEQ], where=r1)
            rel = sb("rel", [P, 2, SEQ], where=r1)
            ik_row = sb("ik_row", [P, TILES, IKW], where=r1)
            ik_two = sb("ik_two", [P, TILES, 2, 64], where=r1)
            idx_gb = sb("idx_gb", [P, 2, 64], where=r1)
            ikT = rel[:, 0, :]
        with ExitStack() as r1:
            mixA = sb("mixA", [P, TILES, 512], where=r1)
            gain_a = sb("gain_a", [P, 512], where=r1)
            gain_h = sb("gain_h", [P, GK], where=r1)
        sb("region1", [P, 16 * 1024 // 4])

        with ExitStack() as r2:
            g_hi = sb("g_hi", [P, TILES + 1, 512], F32R, where=r2)
            g_lo = sb("g_lo", [P, TILES + 1, 512], F32R, where=r2)
            hk = sb("hk", [P, TILES + 1, 512], where=r2)
            hv = sb("hv", [P, TILES + 1, 512], where=r2)
            hqT = sb("hqT", [P, GH, SEQ], where=r2)
            E = sb("E", [P, LEVELS + 1, 2, P], where=r2)
            q_inf = sb("q_inf", [P, GH, P], where=r2)
            A = sb("A", [P, GH, P], where=r2)
            S = sb("S", [P, GH, GK], where=r2)
            hkT = sb("hkT", [P, GH, P], where=r2)
            k_end = sb("k_end", [P, 512], where=r2)
        with ExitStack() as r2:
            kT = sb("kT", [P, 4, SEQ], where=r2)
            kmT = sb("kmT", [P, 4, 2 * NMETA], where=r2)
            V = sb("V", [P, TILES, 512], where=r2)
            V_meta = sb("V_meta", [P, 512], where=r2)
            v_row = sb("v_row", [NMETA, 512], where=r2)
            qT = sb("qT", [P, 4, SEQ], where=r2)
            prob = sb("prob", [P, PROBS, SEQ], where=r2)
            pm = sb("pm", [P, 2, P], where=r2)
            probT = sb("probT", [P, 2, SEQ], where=r2)
            fb = sb("fb", [P, D], where=r2)
            pmT = sb("pmT", [P, P], where=r2)
            y = sb("y", [P, TILES, D], where=r2)
        sb("region2", [P, 66 * 1024 // 4])

        lb, half_span, logits = mixH[:, 0, :], mixH[:, 1, :], mixH[:, 2:4, :]
        middle = lb
        staged = hqT[:, :, :].rearrange("p h t -> p (h t)")
        attn_row, attn_squares = temp[:, 0, :], temp[:, 1, :]

        bank = [ctx.enter_context(nc.psum_tensor(f"bank{i}", [P, 512], F32)) for i in range(8)]

        s_ident, s_staged, s_rot, s_causal = sem("s_ident"), sem("s_staged"), sem("s_rot"), sem("s_causal")
        s_xin = [sem(f"s_xin{t}") for t in range(TILES + 1)]
        s_gb, s_logits, s_idxg, s_gains = sem("s_gb"), sem("s_logits"), sem("s_idxg"), sem("s_gains")
        s_gate = sem("s_gate")
        s_raw = [sem(f"s_raw{i}") for i in range(RAW)]
        s_whi, s_wlo_dve, s_wlo_pool, s_wused = sem("s_whi"), sem("s_wlo_dve"), sem("s_wlo_pool"), sem("s_wused")
        s_kept, s_azero = sem("s_kept"), sem("s_azero")
        s_sq, s_rstd, s_xn = sem("s_sq"), sem("s_rstd"), sem("s_xn")
        s_hhi, s_hlo = sem("s_hhi"), sem("s_hlo")
        s_mhalf, s_lb, s_lbexp = sem("s_mhalf"), sem("s_lb"), sem("s_lbexp")
        s_tanh, s_pv, s_pmsub, s_pmexp, s_iqw = sem("s_tanh"), sem("s_pv"), sem("s_pmsub"), sem("s_pmexp"), sem("s_iqw")
        s_fk, s_ghi, s_glo = sem("s_fk"), sem("s_ghi"), sem("s_glo")
        s_silu = sem("s_silu")
        s_rope = sem("s_rope")
        s_ropeT = sem("s_ropeT")
        s_ik, s_ikvar, s_ikrs, s_kiT, s_iktwo = sem("s_ik"), sem("s_ikvar"), sem("s_ikrs"), sem("s_kiT"), sem("s_iktwo")
        s_rel, s_acc = sem("s_rel"), sem("s_acc")
        s_hkT, s_E, s_X, s_A = sem("s_hkT"), sem("s_E"), sem("s_X"), sem("s_A")
        s_kexp, s_kend, s_S = sem("s_kexp"), sem("s_kend"), sem("s_S")
        s_o, s_osq, s_ors, s_mixH = sem("s_o"), sem("s_osq"), sem("s_ors"), sem("s_mixH")
        s_vm, s_vrow, s_vzero = sem("s_vm"), sem("s_vrow"), sem("s_vzero")
        s_pmeta, s_nmax, s_exp, s_pT, s_pmT = sem("s_pmeta"), sem("s_nmax"), sem("s_exp"), sem("s_pT"), sem("s_pmT")
        s_asq, s_ars, s_mixA = sem("s_asq"), sem("s_ars"), sem("s_mixA")
        s_mhi, s_mlo = sem("s_mhi"), sem("s_mlo")
        s_xres = [sem(f"s_xres{t}") for t in range(TILES)]
        s_fb = sem("s_fb")
        s_y, s_ysq, s_yrs, s_fin = sem("s_y"), sem("s_ysq"), sem("s_yrs"), sem("s_fin")
        s_out = sem("s_out")
        s_a, s_v, s_p = sem("s_a"), sem("s_v"), sem("s_p")

        full = {n: sem(f"{n}_full") for n in ("pj", "tr", "sd", "mi")}
        free = {n: {b: sem(f"{n}_free{b}") for b in bs}
                for n, bs in (("pj", (0, 1)), ("tr", (2, 3)), ("sd", (4, 5)), ("mi", (6, 7)))}

        def of(*kinds):
            return [s for s in SCHEDULE if s[0] in kinds]

        pj = Banks(full["pj"], free["pj"], [(u, i % 2) for i, u in enumerate(units())])
        tr_keys = of("hT", "kT", "ikT", "kiT", "ropeT", "probT", "metaT", "mixT")
        tr = Banks(full["tr"], free["tr"], [(k, 2 + i % 2) for i, k in enumerate(tr_keys)])
        sd_turns = []
        for s in SCHEDULE:
            if s[0] in ("index", "score"):
                sd_turns.append((s, 4 + s[2] % 2))
            if s[0] == "decay":
                sd_turns += [(s + (i,), 4 + i) for i in range(2)]
        sd = Banks(full["sd"], free["sd"], sd_turns)
        mi_turns = []
        for s in SCHEDULE:
            if s[0] == "piece":
                mi_turns.append((s, 6 + s[3] % 2))
            if s[0] in ("suffix", "meta"):
                mi_turns.append((s, 6))
            if s[0] == "state":
                mi_turns.append((s, 6))
            if s[0] in ("out", "attn"):
                mi_turns.append((s, 7))
        mi = Banks(full["mi"], free["mi"], mi_turns)

        quarters = Order([s[1:] for s in of("weights")])

        def lo_on_pool(n):
            g, q = quarters.keys[n]
            return q == 1 if g == "hf" else q % 2 == 0 if g in ("ikw", "iq") else True

        lo_pool = Order([k for i, k in enumerate(quarters.keys) if lo_on_pool(i)])
        lo_dve = Order([k for i, k in enumerate(quarters.keys) if not lo_on_pool(i)])
        used = Order([k for k in quarters.keys if k[1] != QUARTERS - 1])

        def wait_lo(eng, key):
            if key in lo_pool.n:
                eng.wait_ge(s_wlo_pool, lo_pool.at(key))
            else:
                eng.wait_ge(s_wlo_dve, lo_dve.at(key))

        def wait_slot_used(eng, n):
            if n >= RING:
                g, q = quarters.keys[n - RING]
                if q == QUARTERS - 1:
                    pj.wait_full(eng, (g, GROUPS[g][2][-1]))
                else:
                    eng.wait_ge(s_wused, used.at((g, q)))

        norms = Order([s[1] for s in of("norm")])
        hTs = Order(of("hT"))
        ropes = Order([u for u in units() if u[0] in ("iq", "ak", "aq")])
        ropeTs = Order([s[1:] for s in of("ropeT")])
        silus = Order([u for u in units() if u[0] in ("hq", "hg", "ag")])
        evacs = Order([u for u in units() if u[0] not in ("o0", "o1")])
        hfs = Order(GROUPS["hf"][2])
        temps = Order([u for u in units() if u[0] in ("hf", "hq", "hg", "ag")])
        rels = Order([s[1:] for s in of("index")])
        pairs = Order([s[1:3] for s in of("piece") if s[3] == 0])
        gates = Order([s[1:] for s in of("gate")])
        suffixes = Order([s[1] for s in of("suffix")])
        states = Order([s[1] for s in of("state")])
        outs = Order([s[1] for s in of("out")])
        mixHs = Order([s[1] for s in of("mixH")])
        kTs = Order([s[1] for s in of("kT")])
        pmetas = Order([s[1] for s in of("pmeta")])
        scores = Order([s[1:] for s in of("score")])
        probTs = Order([s[1:] for s in of("probT")])
        attns = Order([s[1] for s in of("attn")])
        mixTs = Order([s[1:] for s in of("mixT")])
        finals = Order([s[1] for s in of("final")])
        yunits = Order([u for u in units() if u[0] in ("o0", "o1")])

        def rows_of(t):
            return NMETA if t == META else P

        def cols_of(t):
            return slice(SEQ, SEQ + NMETA) if t == META else slice(t * P, (t + 1) * P)

        def temp_of(u):
            return temp[0:(rows_of(u[1]) if u[0] == "hf" else P), temps.n[u] % 2, :]

        def f_of(t):
            if t == META:
                return k_end[0:NMETA, :]
            return E[:, :, :, :].rearrange("p l h t -> p (l h t)")[:, t * 512:(t + 1) * 512]

        def wait_temp(eng, u):
            n = temps.n[u]
            if n < 2:
                return
            old = temps.keys[n - 2]
            if old[0] == "hf":
                eng.wait_ge(s_fk, hfs.at(old[1]))
            else:
                pj.wait_freed(eng, old)

        def heads_of(ap, n=HEADS):
            return ap.rearrange("p (h d) -> p h d", h=n)

        block = ctx.enter_context(nc.Block())

        @block.sync
        def _(sp):
            def load_x(t):
                r = rows_of(t)
                n = norms.n[t]
                if n >= 3:
                    tr.wait_full(sp, ("hT", norms.keys[n - 3], 1))
                src = meta_tokens if t == META else x[0, t * P:(t + 1) * P, :]
                sp.dma_start(x_t[0:r, n % 3, :], src).then_inc(s_xin[t], 16)

            def load_w(n):
                g, q = quarters.keys[n]
                c0, width, _ = GROUPS[g]
                w = w_out[0] if g in ("o0", "o1") else w_in[0]
                k0 = row_chunk(g, q * KQ)
                src = w[k0 * P:(k0 + KQ) * P, c0:c0 + width]
                if n >= RAW:
                    wait_lo(sp, quarters.keys[n - RAW])
                sp.dma_start(w_raw[:, n % RAW, :, 0:width], src.rearrange("(k p) c -> p k c", p=P))\
                    .then_inc(s_raw[n % RAW], 16)

            def load_tables():
                sp.dma_start(staged[:, 0:1024], t_sums).then_inc(s_staged, 16)
                sp.dma_start(staged[:, 1024:1152], t_after).then_inc(s_staged, 16)
                sp.dma_start(staged[:, 1152:1152 + 6 * P], t_kept.rearrange("p j t -> p (j t)")).then_inc(s_staged, 16)
                sp.dma_start(cos[:], t_cos).then_inc(s_rot, 16)
                sp.dma_start(sin[:], t_sin).then_inc(s_rot, 16)
                sp.dma_start(bias[0][:], t_causal).then_inc(s_causal, 16)

            load_x(0)
            load_w(0)
            load_w(1)
            load_x(1)
            load_w(2)
            load_x(2)
            sp.dma_start(logits, lb_logits.rearrange("(o a) c -> o a c", o=1).broadcast_to([P, 2, 512]))\
                .then_inc(s_logits, 16)
            load_w(3)
            load_x(3)
            load_tables()
            load_w(4)
            load_x(META)
            for n in range(5, len(quarters.keys)):
                load_w(n)
                if quarters.keys[n] == ("o0", 0):
                    pj.wait_freed(sp, ("av", META))
                    sp.wait_ge(s_vzero, 2)
                    for h in range(HEADS):
                        sp.dma_start(V_meta[h * NMETA:(h + 1) * NMETA, h * HD:(h + 1) * HD],
                                     v_row[:, h * HD:(h + 1) * HD]).then_inc(s_vm, 16)
                    sp.dma_start(fb[:], final_g.rearrange("(o c) -> o c", o=1).broadcast_to([P, D])).then_inc(s_fb, 16)
                if quarters.keys[n] == ("hg", 1):
                    sp.wait_ge(s_acc, rels.at((3, 7)))
                    sp.dma_start(gain_a[:], attn_g[0:1, :].broadcast_to([P, 512])).then_inc(s_gains, 16)
                    sp.dma_start(gain_h[:], hgrn_g[0:1, :].broadcast_to([P, GK])).then_inc(s_gains, 16)
                if quarters.keys[n] == ("ikw", 3):
                    tr.wait_full(sp, ("hT", META, 1))
                    sp.dma_start(idx_gb[:, 0, :], idx_g[0:1, :].broadcast_to([P, 64])).then_inc(s_idxg, 16)
                    sp.dma_start(idx_gb[:, 1, :], idx_b[0:1, :].broadcast_to([P, 64])).then_inc(s_idxg, 16)
                if quarters.keys[n] == ("o0", 3):
                    sp.wait_ge(s_mixH, 4)
                    for t in range(TILES):
                        sp.dma_start(y[:, t, :], x[0, t * P:(t + 1) * P, :]).then_inc(s_xres[t], 16)
            for t in range(TILES):
                sp.wait_ge(s_fin, t + 1)
                sp.dma_start(out[0, t * P:(t + 1) * P, :], y[:, t, :]).then_inc(s_out, 16)
            sp.wait_ge(s_out, 16 * TILES)

        @block.gpsimd
        def _(pool):
            steps = [0]

            def link(ins):
                steps[0] += 1
                ins.then_inc(s_p, 1)
                pool.wait_ge(s_p, steps[0])

            def rstd(dst, src, scale, done, r=P, eps=EPS):
                link(pool.tensor_scalar(dst, src, scale, eps, ALU.mult, ALU.add))
                pool.tensor_tensor(dst, dst, mhalf[0:r, 0:dst.shape[1]], ALU.pow).then_inc(done, 1)

            link(pool.memset(mhalf, -0.5))
            pool.memset(A[:, :, :], 0.0).then_inc(s_azero, 1)
            for step in SCHEDULE:
                kind = step[0]
                if kind == "log":
                    t = step[1]
                    r = rows_of(t)
                    pool.wait_ge(s_ghi, hfs.at(t))
                    pool.tensor_tensor(g_lo[0:r, t, :], f_of(t), g_hi[0:r, t, :].bitcast(F32),
                                       ALU.subtract).then_inc(s_glo, 1)
                if kind == "norm":
                    t = step[1]
                    r = rows_of(t)
                    pool.wait_ge(s_sq, norms.at(t))
                    rstd(rs_x[0:r, t:t + 1], sq_x[0:r, t:t + 1], 1.0 / D, s_rstd, r)
                elif kind == "weights" and step[1:] in lo_pool.n:
                    n = quarters.n[step[1:]]
                    width = GROUPS[step[1]][1]
                    pool.wait_ge(s_whi, n + 1)
                    pool.tensor_tensor(w_lo[:, n % RING, :, 0:width], w_raw[:, n % RAW, :, 0:width],
                                       w_hi[:, n % RING, :, 0:width].bitcast(F32), ALU.subtract)\
                        .then_inc(s_wlo_pool, 1)
                elif kind == "silu":
                    pj.wait_freed(pool, step[1:])
                    pool.wait_ge(s_gains, 32)
                    if step[1] == "hg":
                        gate = mixH[:, step[2], :].rearrange("p (h v) -> p h v", h=GH)
                        gain = gain_h[:, :].rearrange("p (o v) -> p o v", o=1).broadcast_to([P, GH, GK])
                    else:
                        gate, gain = mixA[:, step[2], :], gain_a[:, :]
                    pool.tensor_tensor(gate, gate, gain, ALU.mult).then_inc(s_gate, 1)
                elif kind == "ikT":
                    pool.wait_ge(s_ikvar, 1)
                    rstd(ik_rs, ik_var, 1.0 / 64, s_ikrs)
                elif kind == "out":
                    if outs.n[step[1]]:
                        pool.wait_ge(s_mixH, outs.n[step[1]])
                    pool.wait_ge(s_osq, outs.at(step[1]))
                    rstd(rs_h, ms_h, 1.0 / GK, s_ors)
                elif kind == "proj" and step[1:] == ("ak", META):
                    sd.wait_full(pool, ("decay", 3, 1, 0, 1))
                    pool.memset(kmT[:, :, :], 0.0).then_inc(s_vzero, 1)
                    tr.wait_full(pool, ("kT", 3))
                    pool.wait_ge(s_X, gates.at((3, 1, INF_LEVEL)))
                    pool.wait_ge(s_kend, suffixes.at(2))
                    mi.wait_full(pool, ("out", 3))
                    pool.memset(V_meta[:, :], 0.0).then_inc(s_vzero, 1)
                elif kind == "attn":
                    pool.wait_ge(s_asq, attns.at(step[1]))
                    rstd(rs_a, ms_a, 4.0 / AW, s_ars, eps=4.0 * EPS)
                elif kind == "final":
                    t = step[1]
                    pool.wait_ge(s_ysq, finals.at(t))
                    rstd(rs_f[:, t:t + 1], ms_f[:, t:t + 1], 1.0 / D, s_yrs)

        @block.scalar
        def _(act):
            steps = [0]

            def link(ins):
                steps[0] += 1
                ins.then_inc(s_a, 1)
                act.wait_ge(s_a, steps[0])

            act.dma_start(gb[:], mix_norm[0:1, :].broadcast_to([P, D])).then_inc(s_gb, 16)
            act.dma_start(ident[:], t_ident).then_inc(s_ident, 16)

            def weights_hi(g, q):
                n = quarters.n[(g, q)]
                width = GROUPS[g][1]
                wait_slot_used(act, n)
                act.wait_ge(s_raw[n % RAW], 16 * (n // RAW + 1))
                ins = act.activation(w_hi[:, n % RING, :, 0:width], w_raw[:, n % RAW, :, 0:width], ACT.Copy)
                ins.then_inc(s_whi, 1)

            def unit(g, t):
                u = (g, t)
                src = bank[pj.bank[u]]
                r = P if g == "hq" else rows_of(t)
                if g in ("o0", "o1"):
                    return
                if g in ("hf", "hq", "hg", "ag"):
                    wait_temp(act, u)
                    pj.wait_full(act, u)
                    ins = act.activation(temp_of(u), src[0:r, :], ACT.Tanh, scale=0.5)
                    ins.then_inc(pj.freed(u) if g == "hf" else s_tanh, 1)
                elif g == "hi":
                    pj.wait_full(act, u)
                    act.activation(hv[0:r, t, :], src[0:r, :], ACT.Copy).then_inc(pj.freed(u), 1)
                elif g == "av":
                    pj.wait_full(act, u)
                    act.wait_ge(s_mixH, 4)
                    dst = v_row[:, :] if t == META else V[:, t, :]
                    act.activation(dst, src[0:r, :], ACT.Copy).then_inc(pj.freed(u), 1)
                elif g == "ikw":
                    pj.wait_full(act, u)
                    act.activation(ikT[0:IKW, :], src[0:IKW, :], ACT.Copy).then_inc(pj.freed(u), 1)
                else:
                    n = ropes.n[u]
                    if n >= 2:
                        tr.wait_full(act, ("ropeT",) + ropes.keys[n - 2])
                    pj.wait_full(act, u)
                    act.activation(rows[0:r, n % 2, :], src[0:r, :], ACT.Copy).then_inc(pj.freed(u), 1)

            for step in SCHEDULE:
                kind = step[0]
                if kind == "norm":
                    t = step[1]
                    r = rows_of(t)
                    act.wait_ge(s_xin[t], 16)
                    if norms.n[t]:
                        act.wait_ge(s_sq, norms.n[t])
                    act.activation(rows[0:r, :, :].rearrange("p a b -> p (a b)"), x_t[0:r, norms.n[t] % 3, :],
                                   ACT.Square, accum_out=sq_x[0:r, t:t + 1]).then_inc(s_sq, 1)
                elif kind == "floor" and step[1] == 1:
                    act.wait_ge(s_lbexp, 1)
                    act.activation(logits, logits, ACT.Exp).then_inc(s_lb, 1)
                elif kind == "hT":
                    _, t, half = step
                    r = rows_of(t)
                    b = bank[tr.bank[step]]
                    tr.wait_full(act, step)
                    act.activation(hT_hi[:, 4 * half:4 * half + 4, cols_of(t)],
                                   b[:, :].rearrange("p (k t) -> p k t", k=4)[:, :, 0:r], ACT.Copy).then_inc(s_hhi, 1)
                elif kind == "weights":
                    weights_hi(*step[1:])
                elif kind == "proj":
                    unit(*step[1:])
                elif kind == "log":
                    t = step[1]
                    r = rows_of(t)
                    if hfs.n[t] == 0:
                        act.wait_ge(s_staged, 48)
                        act.activation(sums[:, :, :].rearrange("p l t -> p (l t)"), staged[:, 0:1024], ACT.Copy)
                        act.activation(after[:], staged[:, 1024:1152], ACT.Copy)
                    act.wait_ge(s_fk, hfs.at(t))
                    link(act.activation(f_of(t), f_of(t), ACT.Ln))
                    act.activation(g_hi[0:r, t, :], f_of(t), ACT.Copy).then_inc(s_ghi, 1)
                elif kind == "ikT":
                    tr.wait_full(act, step)
                    act.activation(ik_row[:, :, :], bank[tr.bank[step]][:, 0:TILES * IKW]
                                   .rearrange("p (t c) -> p t c", t=TILES), ACT.Copy).then_inc(tr.freed(step), 1)
                elif kind == "kiT":
                    tr.wait_full(act, step)
                    act.activation(kiT[:, :], bank[tr.bank[step]][:, :], ACT.Copy).then_inc(tr.freed(step), 1)
                elif kind == "ropeT":
                    _, g, t = step
                    b4 = bank[tr.bank[step]][:, :].rearrange("p (j t) -> p j t", j=4)
                    tr.wait_full(act, step)
                    if g == "iq":
                        ins = act.activation(qiT[:, :, (t - 1) * P:t * P], b4, ACT.Copy)
                    elif g == "aq":
                        ins = act.activation(qT[:, :, t * P:(t + 1) * P], b4, ACT.Copy)
                    elif t == META:
                        act.wait_ge(s_vzero, 2)
                        act.activation(kmT[0:HD, :, 0:NMETA], b4[0:HD, :, 0:NMETA], ACT.Copy)
                        ins = act.activation(kmT[HD:P, :, NMETA:2 * NMETA], b4[HD:P, :, 0:NMETA], ACT.Copy)
                    else:
                        ins = act.activation(kT[:, :, t * P:(t + 1) * P], b4, ACT.Copy)
                    ins.then_inc(tr.freed(step), 1)
                elif kind == "index":
                    _, b, h = step
                    n = rels.n[(b, h)]
                    if n >= 2:
                        act.wait_ge(s_acc, n - 1)
                    sd.wait_full(act, step)
                    w = (b + 1) * P
                    act.activation(rel[:, n % 2, 0:w], bank[sd.bank[step]][:, 0:w], ACT.Relu)\
                        .then_inc(sd.freed(step), 1)
                elif kind == "kT":
                    t = step[1]
                    tr.wait_full(act, step)
                    if kTs.n[t]:
                        mi.wait_full(act, ("piece", t - 1, 1, 0))
                        act.wait_ge(s_X, gates.at((t - 1, 1, INF_LEVEL)))
                    act.activation(hkT[:, :, :], bank[tr.bank[step]][:, :].rearrange("p (h t) -> p h t", h=GH),
                                   ACT.Copy).then_inc(tr.freed(step), 1)
                elif kind == "decay":
                    _, t, hp, half = step
                    n = pairs.n[(t, hp)]
                    if n:
                        mi.wait_full(act, ("piece",) + pairs.keys[n - 1] + (2 if half else PIECES - 1,))
                        act.wait_ge(s_X, gates.at(pairs.keys[n - 1] + (INF_LEVEL,)))
                    for i in range(2):
                        key = step + (i,)
                        sd.wait_full(act, key)
                        act.activation(E[:, 4 * half:4 * half + 4, i, :],
                                       bank[sd.bank[key]][:, :].rearrange("p (l t) -> p l t", l=4), ACT.Exp)\
                            .then_inc(sd.freed(key), 1)
                elif kind == "piece" and step[3] == 1:
                    _, t, hp, j = step
                    pair = slice(2 * hp, 2 * hp + 2)
                    src = bank[mi.bank[step]][:, 0:2 * P].rearrange("p (h t) -> p h t", h=2)
                    mi.wait_full(act, step)
                    mi.wait_freed(act, ("piece", t, hp, 0))
                    for s0, s1, t0, t1 in BLOCKS:
                        ins = act.activation(A[s0:s1, pair, t0:t1], src[s0:s1, :, t0:t1], ACT.Copy)
                    ins.then_inc(mi.freed(step), 1)
                elif kind == "suffix":
                    t = step[1]
                    r = rows_of(t)
                    mi.wait_full(act, step)
                    if suffixes.n[t]:
                        mi.wait_full(act, ("state", suffixes.keys[suffixes.n[t] - 1]))
                    act.activation(k_end[0:r, :], bank[6][0:r, :], ACT.Exp).then_inc(mi.freed(step), 1)
                elif kind == "out":
                    t = step[1]
                    mi.wait_full(act, step)
                    if outs.n[t]:
                        act.wait_ge(s_mixH, mixHs.at(outs.keys[outs.n[t] - 1]))
                    act.activation(o_row[:, :], bank[7][:, :], ACT.Copy, scale=0.5).then_inc(mi.freed(step), 1)
                    mi.wait_freed(act, step)
                    for h in range(GH):
                        link(act.activation(junk[:, :], o_row[:, h * GK:(h + 1) * GK], ACT.Square,
                                            accum_out=ms_h[:, h:h + 1])) if h < GH - 1 else \
                            act.activation(junk[:, :], o_row[:, h * GK:(h + 1) * GK], ACT.Square,
                                           accum_out=ms_h[:, h:h + 1]).then_inc(s_osq, 1)
                elif kind == "meta":
                    b = step[1]
                    mi.wait_full(act, step)
                    if b >= 2:
                        tr.wait_full(act, ("metaT", b - 2))
                    else:
                        act.wait_ge(s_mixH, 4)
                    act.activation(pm[:, b % 2, :], bank[6][:, 0:P], ACT.Copy).then_inc(mi.freed(step), 1)
                elif kind == "pmeta":
                    act.wait_ge(s_pmsub, pmetas.at(step[1]))
                    half = pm[:, step[1] % 2, :]
                    act.activation(half, half, ACT.Exp, scale=ATTN_SCALE).then_inc(s_pmexp, 1)
                elif kind == "score":
                    _, b, h = step
                    w = (b + 1) * P
                    act.wait_ge(s_nmax, scores.at((b, h)))
                    act.activation(prob[:, h % PROBS, 0:w], prob[:, h % PROBS, 0:w], ACT.Exp, bias=nmax[b % 2][:, h:h + 1],
                                   scale=ATTN_SCALE, accum_out=psums[b % 2][:, h:h + 1]).then_inc(s_exp, 1)
                elif kind == "probT":
                    _, b, h = step
                    n = probTs.n[(b, h)]
                    w = (b + 1) * P
                    tr.wait_full(act, step)
                    if n >= 2:
                        act.wait_ge(s_pv, n - 1)
                    act.activation(probT[:, n % 2, 0:w], bank[tr.bank[step]][:, 0:w], ACT.Copy)\
                        .then_inc(tr.freed(step), 1)
                elif kind == "metaT":
                    tr.wait_full(act, step)
                    if step[1]:
                        mi.wait_full(act, ("attn", step[1] - 1))
                    act.activation(pmT[:, :], bank[tr.bank[step]][:, 0:P], ACT.Copy).then_inc(tr.freed(step), 1)
                elif kind == "attn":
                    mi.wait_freed(act, step)
                    act.activation(attn_squares, attn_row, ACT.Square, accum_out=ms_a).then_inc(s_asq, 1)
                elif kind == "mixT":
                    _, t, half = step
                    tr.wait_full(act, step)
                    act.activation(hT_hi[:, 4 * half:4 * half + 4, cols_of(t)],
                                   bank[tr.bank[step]][:, :].rearrange("p (k t) -> p k t", k=4), ACT.Copy)\
                        .then_inc(s_mhi, 1)
                elif kind == "final":
                    t = step[1]
                    pj.wait_freed(act, ("o1", t))
                    if finals.n[t]:
                        act.wait_ge(s_ysq, finals.n[t])
                    act.activation(rows[:, :, :].rearrange("p a b -> p (a b)"), y[:, t, :], ACT.Square,
                                   accum_out=ms_f[:, t:t + 1]).then_inc(s_ysq, 1)

        @block.vector
        def _(dve):
            steps = [0]

            def mark(ins):
                steps[0] += 1
                ins.then_inc(s_v, 1)
                return steps[0]

            def link(ins):
                dve.wait_ge(s_v, mark(ins))

            def over_heads(ap, n=HEADS, d=HD):
                return ap.rearrange("p (h o) -> p h o", o=1).broadcast_to([P, n, d])

            def rope(rot, rot_swapped, c, sn, tmp):
                mark(dve.tensor_tensor(tmp, rot_swapped, sn, ALU.mult))
                dve.wait_ge(s_v, steps[0])
                link(dve.tensor_tensor(rot, rot, c, ALU.mult))
                return dve.tensor_tensor(rot, rot, tmp, ALU.add)

            def silu(u, dst):
                z = temp_of(u)
                dve.wait_ge(s_tanh, silus.at(u))
                dve.scalar_tensor_tensor(out=dst, in0=z, scalar=1.0, in1=bank[pj.bank[u]][:, :], op0=ALU.add,
                                         op1=ALU.mult).then_inc(pj.freed(u), 1)

            last_round = {}
            for step in SCHEDULE:
                kind = step[0]
                if kind == "norm":
                    t = step[1]
                    r = rows_of(t)
                    xt = x_t[0:r, norms.n[t] % 3, :]
                    if norms.n[t] == 0:
                        dve.wait_ge(s_gb, 16)
                    dve.wait_ge(s_rstd, norms.at(t))
                    dve.scalar_tensor_tensor(out=xt, in0=xt, scalar=rs_x[0:r, t:t + 1], in1=gb[0:r, :],
                                             op0=ALU.mult, op1=ALU.mult).then_inc(s_xn, 1)
                elif kind == "floor" and step[1] == 0:
                    dve.wait_ge(s_logits, 16)
                    link(dve.tensor_tensor(lb, logits[:, 0, :], logits[:, 1, :], ALU.max))
                    link(dve.tensor_tensor(logits[:, 0, :], logits[:, 0, :], lb, ALU.subtract))
                    dve.tensor_tensor(logits[:, 1, :], logits[:, 1, :], lb, ALU.subtract).then_inc(s_lbexp, 1)
                elif kind == "floor":
                    dve.wait_ge(s_lb, 1)
                    link(dve.tensor_tensor(half_span, logits[:, 0, :], logits[:, 1, :], ALU.add))
                    link(dve.reciprocal(half_span, half_span))
                    link(dve.tensor_tensor(lb, logits[:, 0, :], half_span, ALU.mult))
                    link(dve.tensor_scalar(half_span, lb, -0.5, 0.5, ALU.mult, ALU.add))
                    link(dve.tensor_tensor(middle, lb, half_span, ALU.add))
                elif kind == "hT" or kind == "mixT":
                    _, t, half = step
                    r = rows_of(t)
                    if kind == "hT":
                        dve.wait_ge(s_hhi, hTs.at(step))
                    else:
                        dve.wait_ge(s_mhi, mixTs.at(step[1:]))
                    at = (slice(None), slice(4 * half, 4 * half + 4), cols_of(t))
                    dve.tensor_tensor(hT_lo[at], bank[tr.bank[step]][:, :].rearrange("p (k t) -> p k t", k=4)[:, :, 0:r],
                                      hT_hi[at].bitcast(F32), ALU.subtract).then_inc(tr.freed(step), 1)
                elif kind == "weights" and step[1:] in lo_dve.n:
                    g, q = step[1:]
                    n = quarters.n[(g, q)]
                    dve.wait_ge(s_whi, n + 1)
                    width = GROUPS[g][1]
                    for j in range(KQ):
                        slot = (slice(None), n % RING, j, slice(0, width))
                        raw, hi = w_raw[:, n % RAW, j, 0:width], w_hi[slot].bitcast(F32)
                        ins = dve.tensor_tensor(w_lo[slot], raw, hi, ALU.subtract)
                    ins.then_inc(s_wlo_dve, 1)
                elif kind == "proj":
                    g, t = u = step[1:]
                    if g == "hq":
                        silu(u, hqT[:, t, :])
                    elif g in ("iq", "ak", "aq"):
                        r = rows_of(t)
                        pj.wait_freed(dve, u)
                        v = rows[0:r, ropes.n[u] % 2, :].rearrange("p (h a two k) -> p h a two k", h=HEADS, a=4, two=2)
                        rot, rev = v[:, :, 0, :, :], v[:, :, 0, ::-1, :]
                        shape = [r, HEADS, 2, 8]
                        c = cos[0:r, t, :].rearrange("p (o two k) -> p o two k", o=1, two=2).broadcast_to(shape)
                        sn = sin[0:r, t, :].rearrange("p (o two k) -> p o two k", o=1, two=2).broadcast_to(shape)
                        if ropes.n[u]:
                            dve.wait_ge(s_rope, ropes.n[u])
                        tmp = swapped[0:r, :].rearrange("p (h two k) -> p h two k", h=HEADS, two=2)
                        rope(rot, rev, c, sn, tmp).then_inc(s_rope, 1)
                    elif g in ("o0", "o1"):
                        half = int(g == "o1")
                        pj.wait_full(dve, u)
                        if not half:
                            dve.wait_ge(s_xres[t], 16)
                        yt = y[:, t, half * 512:(half + 1) * 512]
                        dve.tensor_tensor(yt, yt, bank[pj.bank[u]][:, :], ALU.add).then_inc(pj.freed(u), 1)
                elif kind == "silu":
                    _, g, t = step
                    silu((g, t), (mixH if g == "hg" else mixA)[:, t, :])
                elif kind == "gate f":
                    t = step[1]
                    r = rows_of(t)
                    z = temp_of(("hf", t))
                    pj.wait_freed(dve, ("hf", t))
                    link(dve.tensor_tensor(z, z, half_span[0:r, :], ALU.mult))
                    link(dve.tensor_tensor(f_of(t), z, middle[0:r, :], ALU.add))
                    dve.tensor_scalar(hk[0:r, t, :], f_of(t), -1.0, 1.0, ALU.mult, ALU.add).then_inc(s_fk, 1)
                elif kind == "ikT":
                    dve.wait_ge(s_staged, 48)
                    dve.tensor_copy(kept[:, :, :].rearrange("p j t -> p (j t)"), staged[:, 1152:1152 + 6 * P])\
                        .then_inc(s_kept, 1)
                    dve.wait_ge(s_rot, 32)
                    dve.wait_ge(s_causal, 16)
                    tr.wait_freed(dve, step)
                    key, two, sq = ik_row[:, :, 0:64], ik_two[:, :, 0, :], ik_two[:, :, 1, :]
                    per_tile = [P, TILES, 64]
                    link(dve.tensor_reduce(ik_mean, key, AX.X, ALU.add))
                    link(dve.tensor_scalar(ik_mean, ik_mean, 1.0 / 64, None, ALU.mult))
                    link(dve.tensor_tensor(two, key, over_heads(ik_mean, TILES, 64), ALU.subtract))
                    link(dve.tensor_tensor(sq, two, two, ALU.mult))
                    dve.tensor_reduce(ik_var, sq, AX.X, ALU.add).then_inc(s_ikvar, 1)
                    link(dve.tensor_scalar(idxw[:, :, :], ik_row[:, :, 64:72], IDX_SCALE, None, ALU.mult))
                    dve.wait_ge(s_ikrs, 1)
                    dve.wait_ge(s_idxg, 32)
                    gain = idx_gb[:, 0:1, :].broadcast_to(per_tile)
                    shift = idx_gb[:, 1:2, :].broadcast_to(per_tile)
                    link(dve.tensor_tensor(two, two, over_heads(ik_rs, TILES, 64), ALU.mult))
                    link(dve.tensor_tensor(two, two, gain, ALU.mult))
                    link(dve.tensor_tensor(two, two, shift, ALU.add))
                    v = two.rearrange("p t (a two k) -> p t a two k", a=4, two=2)
                    as_pairs = lambda ap: ap.rearrange("p t (two k) -> p t two k", two=2)
                    link(rope(v[:, :, 0, :, :], v[:, :, 0, ::-1, :], as_pairs(cos[:, 0:TILES, :]),
                              as_pairs(sin[:, 0:TILES, :]),
                              swapped[:, 0:64].rearrange("p (t two k) -> p t two k", t=TILES, two=2)))
                    dve.tensor_copy(sq, two).then_inc(s_iktwo, 1)
                elif kind == "index":
                    _, b, h = step
                    n = rels.n[(b, h)]
                    w = (b + 1) * P
                    wgt = idxw[:, b, h:h + 1]
                    sd.wait_freed(dve, step)
                    if h == 0:
                        dve.tensor_scalar(bias[b][:, :], rel[:, n % 2, 0:w], wgt, None, ALU.mult).then_inc(s_acc, 1)
                    else:
                        dve.wait_ge(s_acc, n)
                        dve.scalar_tensor_tensor(out=bias[b][:, :], in0=rel[:, n % 2, 0:w], scalar=wgt, in1=bias[b][:, :],
                                                 op0=ALU.mult, op1=ALU.add).then_inc(s_acc, 1)
                    if h == 7:
                        dve.wait_ge(s_acc, n + 1)
                        diag = bias[b][:, b * P:w]
                        last_round[b] = mark(dve.tensor_tensor(diag, diag, bias[0][:, :], ALU.add))
                elif kind == "find":
                    b = step[2]
                    dve.wait_ge(s_v, last_round[b])
                    last_round[b] = mark(dve.max(top8[:, b, :], bias[b][:, :]))
                elif kind == "take":
                    b = step[2]
                    dve.wait_ge(s_v, last_round[b])
                    last_round[b] = mark(dve.match_replace(bias[b][:, :], top8[:, b, :], bias[b][:, :], TAKEN))
                elif kind == "biases":
                    for b in range(1, TILES):
                        dve.wait_ge(s_v, last_round[b])
                        last_round[b] = mark(dve.tensor_scalar(bias[b][:, :], bias[b][:, :], 0.5 * TAKEN, NEG,
                                                               ALU.is_gt, ALU.mult))
                elif kind == "gate":
                    _, t, hp, l = step
                    for i in range(2):
                        sd.wait_freed(dve, ("decay", t, hp, int(l >= 4), i))
                    tr.wait_freed(dve, ("kT", t))
                    pair = slice(2 * hp, 2 * hp + 2)
                    keys, queries = hkT[:, pair, :], hqT[:, pair, t * P:(t + 1) * P]
                    if l == INF_LEVEL:
                        if hp == 0 and t:
                            mi.wait_full(dve, ("out", t - 1))
                        dve.tensor_copy(decay_end[:, t % 2, pair], E[:, INF_LEVEL, :, P - 1])
                        dve.tensor_tensor(q_inf[:, pair, :], E[:, INF_LEVEL, :, :], queries, ALU.mult).then_inc(s_X, 1)
                    else:
                        def halves(ap):
                            return ap.rearrange("p h (b two m) -> p h b two m", two=2, m=1 << l)
                        e = halves(E[:, l, :, :])
                        for side, z in ((0, keys), (1, queries)):
                            ins = dve.tensor_tensor(e[:, :, :, side, :], e[:, :, :, side, :],
                                                    halves(z)[:, :, :, side, :], ALU.mult)
                        ins.then_inc(s_X, 1)
                elif kind == "piece" and step[3] != 1:
                    _, t, hp, j = step
                    pair = slice(2 * hp, 2 * hp + 2)
                    if (t, hp, j) == (0, 0, 0):
                        dve.wait_ge(s_azero, 1)
                        dve.wait_ge(s_kept, 1)
                    if j == 0 and hp == 0 and t:
                        mi.wait_full(dve, ("out", t - 1))
                    src = bank[mi.bank[step]][:, 0:2 * P].rearrange("p (h t) -> p h t", h=2)
                    mi.wait_full(dve, step)
                    if j:
                        mi.wait_freed(dve, ("piece", t, hp, j - 1))
                    dve.copy_predicated(A[:, pair, :], kept[:, max(j - 1, 0):max(j, 1), :].broadcast_to([P, 2, P]),
                                        src).then_inc(mi.freed(step), 1)
                elif kind == "suffix":
                    t = step[1]
                    r = rows_of(t)
                    mi.wait_freed(dve, step)
                    dve.tensor_tensor(k_end[0:r, :], k_end[0:r, :], hk[0:r, t, :], ALU.mult).then_inc(s_kend, 1)
                elif kind == "state":
                    t = step[1]
                    mi.wait_full(dve, step)
                    if t == META:
                        dve.tensor_copy(S[:, :, :], bank[6][:, :].rearrange("p (h v) -> p h v", h=GH))\
                            .then_inc(mi.freed(step), 1)
                    else:
                        mi.wait_full(dve, ("out", t))
                        for h in range(GH):
                            ins = dve.scalar_tensor_tensor(out=S[:, h, :], in0=S[:, h, :],
                                                           scalar=decay_end[:, t % 2, h:h + 1],
                                                           in1=bank[6][:, h * GK:(h + 1) * GK],
                                                           op0=ALU.mult, op1=ALU.add)
                        ins.then_inc(mi.freed(step), 1)
                elif kind == "mixH":
                    t = step[1]
                    dve.wait_ge(s_ors, mixHs.at(t))
                    o4 = o_row[:, :].rearrange("p (h v) -> p h v", h=GH)
                    link(dve.tensor_tensor(o4, o4, over_heads(rs_h, GH, GK), ALU.mult))
                    dve.wait_ge(s_gate, t + 1)
                    dve.scalar_tensor_tensor(out=mixH[:, t, :], in0=mixH[:, t, :], scalar=0.5, in1=o_row[:, :],
                                             op0=ALU.mult, op1=ALU.mult).then_inc(s_mixH, 1)
                elif kind == "meta":
                    b = step[1]
                    mi.wait_freed(dve, step)
                    link(dve.tensor_reduce(mmax[b % 2], pm[:, b % 2, :].rearrange("p (h m) -> p h m", h=HEADS), AX.X, ALU.max))
                elif kind == "score":
                    _, b, h = step
                    w = (b + 1) * P
                    sd.wait_full(dve, step)
                    if scores.n[(b, h)] >= PROBS:
                        tr.wait_full(dve, ("probT",) + scores.keys[scores.n[(b, h)] - PROBS])
                    dve.tensor_tensor_reduce(prob[:, h % PROBS, 0:w], bank[sd.bank[step]][:, 0:w], bias[b][:, :], 1.0,
                                             mmax[b % 2][:, h:h + 1], ALU.add, ALU.max, pmax[b % 2][:, h:h + 1])\
                        .then_inc(sd.freed(step), 1)
                    sd.wait_freed(dve, step)
                    dve.tensor_scalar(nmax[b % 2][:, h:h + 1], pmax[b % 2][:, h:h + 1], -ATTN_SCALE, None, ALU.mult)\
                        .then_inc(s_nmax, 1)
                elif kind == "pmeta":
                    half = step[1] % 2
                    pm3 = pm[:, half, :].rearrange("p (h m) -> p h m", h=HEADS)
                    dve.tensor_tensor(pm3, pm3, over_heads(pmax[half], HEADS, NMETA), ALU.subtract).then_inc(s_pmsub, 1)
                elif kind == "metaT":
                    b = step[1]
                    dve.wait_ge(s_pmexp, pmetas.at(b))
                    dve.wait_ge(s_exp, scores.at((b, HEADS - 1)))
                    link(dve.tensor_reduce(msum, pm[:, b % 2, :].rearrange("p (h m) -> p h m", h=HEADS), AX.X, ALU.add))
                    link(dve.tensor_tensor(msum, msum, psums[b % 2], ALU.add))
                    link(dve.reciprocal(prec, msum))
                elif kind == "attn":
                    b = step[1]
                    mi.wait_full(dve, step)
                    dve.tensor_tensor(attn_row.rearrange("p (h d) -> p h d", h=HEADS),
                                      bank[7][:, :].rearrange("p (h d) -> p h d", h=HEADS), over_heads(prec), ALU.mult)\
                        .then_inc(mi.freed(step), 1)
                elif kind == "mixA":
                    b = step[1]
                    dve.wait_ge(s_ars, attns.at(b))
                    dve.wait_ge(s_gate, TILES + b + 1)
                    dve.scalar_tensor_tensor(out=mixA[:, b, :], in0=attn_row, scalar=rs_a, in1=mixA[:, b, :],
                                             op0=ALU.mult, op1=ALU.mult).then_inc(s_mixA, 1)
                elif kind == "final":
                    t = step[1]
                    dve.wait_ge(s_yrs, finals.at(t))
                    dve.wait_ge(s_fb, 16)
                    dve.scalar_tensor_tensor(out=y[:, t, :], in0=y[:, t, :], scalar=rs_f[:, t:t + 1], in1=fb[:, :],
                                             op0=ALU.mult, op1=ALU.mult).then_inc(s_fin, 1)

        @block.tensor
        def _(pe):
            pe.wait_ge(s_ident, 16)
            ready = set()

            def transposes(step, sources, width=P):
                b = bank[tr.bank[step]]
                tr.wait_free(pe, step)
                for i, src in enumerate(sources):
                    r, c = src.shape
                    ins = pe.transpose(b[0:c, width * i:width * i + r], src, ident[0:r, 0:r])
                ins.then_inc(full["tr"], 1)

            def project(u, k):
                g, t = u
                r = P if g == "hq" else rows_of(t)
                width = GROUPS[g][1]
                n0 = quarters.n[(g, 0)]
                cols = slice(0, SEQ) if g in ("hq", "ikw") else cols_of(t)
                b = bank[pj.bank[u]]
                if k == 0:
                    if g in ("o0", "o1"):
                        tr.wait_freed(pe, ("mixT", t, 1))
                    else:
                        for tt in ([0, 1, 2, 3] if g in ("hq", "ikw") else [t]):
                            tr.wait_freed(pe, ("hT", tt, 0))
                    pj.wait_free(pe, u)
                last_unit = u[1] == GROUPS[g][2][-1]
                if k == KC // 2 and g in ("o0", "o1"):
                    tr.wait_freed(pe, ("mixT", t, 0))
                elif k == KC // 2:
                    for tt in ([0, 1, 2, 3] if g in ("hq", "ikw") else [t]):
                        tr.wait_freed(pe, ("hT", tt, 1))
                q, j = divmod(k, KQ)
                slot = (n0 + q) % RING
                if (g, q) not in ready:
                    wait_lo(pe, (g, q))
                    ready.add((g, q))
                row = row_chunk(g, k)
                h_hi, h_lo = hT_hi[:, row, cols], hT_lo[:, row, cols]
                m_hi, m_lo = w_hi[:, slot, j, 0:width], w_lo[:, slot, j, 0:width]
                if g == "hq":
                    c = slice(t * P, (t + 1) * P)
                    pairs = [(m_hi[:, c], h_hi), (m_hi[:, c], h_lo), (m_lo[:, c], h_hi)]
                elif g == "ikw":
                    pairs = [(m_hi, h_hi), (m_hi, h_lo), (m_lo, h_hi)]
                else:
                    pairs = [(h_hi, m_hi), (h_hi, m_lo), (h_lo, m_hi)]
                dst = b[0:IKW, :] if g == "ikw" else b[0:r, 0:512]
                for i, (a, m) in enumerate(pairs):
                    ins = pe.matmul(dst, a, m, start=(k == 0 and i == 0), stop=(k == KC - 1 and i == 2))
                if k == KC - 1:
                    ins.then_inc(full["pj"], 1)
                elif last_unit and j == KQ - 1:
                    ins.then_inc(s_wused, 1)

            for step, part in TENSOR_ORDER:
                kind = step[0]
                if kind == "hT":
                    _, t, half = step
                    r = rows_of(t)
                    pe.wait_ge(s_xn, norms.at(t))
                    transposes(step, [x_t[0:r, norms.n[t] % 3, k * P:(k + 1) * P] for k in range(4 * half, 4 * half + 4)])
                elif kind == "proj":
                    project(step[1:], part)
                elif kind == "ikT":
                    pj.wait_freed(pe, ("ikw", 0))
                    transposes(step, [ikT[0:IKW, t * P:(t + 1) * P] for t in range(TILES)], IKW)
                elif kind == "kiT":
                    pe.wait_ge(s_iktwo, 1)
                    transposes(step, [ik_two[:, t, :, :].rearrange("p two d -> p (two d)") for t in range(TILES)])
                elif kind == "ropeT":
                    _, g, t = step
                    r = rows_of(t)
                    pe.wait_ge(s_rope, ropes.at((g, t)))
                    transposes(step, [rows[0:r, ropes.n[(g, t)] % 2, j * P:(j + 1) * P] for j in range(4)])
                elif kind == "kT":
                    t = step[1]
                    pe.wait_ge(s_fk, hfs.at(t))
                    transposes(step, [hk[:, t, j * P:(j + 1) * P] for j in range(4)])
                elif kind == "index":
                    _, b, h = step
                    sd.wait_free(pe, step)
                    tr.wait_freed(pe, ("ropeT", "iq", b))
                    tr.wait_freed(pe, ("kiT",))
                    lanes = slice(64 * (h % 2), 64 * (h % 2) + 64)
                    w = (b + 1) * P
                    pe.matmul(bank[sd.bank[step]][:, 0:w], qiT[lanes, h // 2, (b - 1) * P:b * P], kiT[lanes, 0:w],
                              start=True, stop=True).then_inc(full["sd"], 1)
                elif kind == "decay":
                    _, t, hp, half = step
                    pe.wait_ge(s_glo, hfs.at(t))
                    m = sums[:, 4 * half:4 * half + 4, :].rearrange("p l t -> p (l t)")
                    for i in range(2):
                        key = step + (i,)
                        c = slice((2 * hp + i) * GK, (2 * hp + i + 1) * GK)
                        sd.wait_free(pe, key)
                        b = bank[sd.bank[key]]
                        pe.matmul(b[:, :], g_hi[:, t, c], m, start=True, stop=False)
                        pe.matmul(b[:, :], g_lo[:, t, c], m, start=False, stop=True).then_inc(full["sd"], 1)
                elif kind == "suffix":
                    t = step[1]
                    r = rows_of(t)
                    pe.wait_ge(s_glo, hfs.at(t))
                    mi.wait_free(pe, step)
                    pe.matmul(bank[6][0:r, :], after[0:r, 0:r], g_hi[0:r, t, :], start=True, stop=False)
                    pe.matmul(bank[6][0:r, :], after[0:r, 0:r], g_lo[0:r, t, :], start=False, stop=True)\
                        .then_inc(full["mi"], 1)
                elif kind == "state":
                    t = step[1]
                    r = rows_of(t)
                    pe.wait_ge(s_kend, suffixes.at(t))
                    pj.wait_freed(pe, ("hi", t))
                    mi.wait_free(pe, step)
                    for h in range(GH):
                        c = slice(h * GK, (h + 1) * GK)
                        ins = pe.matmul(bank[6][:, c], k_end[0:r, c], hv[0:r, t, c], start=True, stop=True)
                    ins.then_inc(full["mi"], 1)
                elif kind == "piece":
                    _, t, hp, j = step
                    b = bank[mi.bank[step]]
                    mi.wait_free(pe, step)
                    if j == 0:
                        tr.wait_freed(pe, ("kT", t))
                        for h in (2 * hp, 2 * hp + 1):
                            pj.wait_freed(pe, ("hq", h))
                    else:
                        pe.wait_ge(s_X, gates.at((t, hp, 5 if j == 1 else 6 - j)))
                    for i in range(2):
                        h = 2 * hp + i
                        if j == 0:
                            ins = pe.matmul(b[:, i * P:(i + 1) * P], hkT[:, h, :], hqT[:, h, t * P:(t + 1) * P],
                                            start=True, stop=True)
                        elif j == 1:
                            for s0, s1, t0, t1 in BLOCKS:
                                e = E[:, 6 if s1 == 64 else 5, i, :]
                                ins = pe.matmul(b[s0:s1, i * P + t0:i * P + t1], e[:, s0:s1], e[:, t0:t1],
                                                start=True, stop=True)
                        else:
                            e = E[:, 6 - j, i, :]
                            ins = pe.matmul(b[:, i * P:(i + 1) * P], e, e, start=True, stop=True)
                    ins.then_inc(full["mi"], 1)
                elif kind == "out":
                    t = step[1]
                    pe.wait_ge(s_X, gates.at((t, 1, INF_LEVEL)))
                    mi.wait_freed(pe, ("piece", t, 1, PIECES - 1))
                    prev = states.keys[outs.n[t]]
                    mi.wait_freed(pe, ("state", prev))
                    mi.wait_free(pe, step)
                    for h in range(GH):
                        c = slice(h * GK, (h + 1) * GK)
                        pe.matmul(bank[7][:, c], A[:, h, :], hv[:, t, c], start=True, stop=False)
                        ins = pe.matmul(bank[7][:, c], q_inf[:, h, :], S[:, h, :], start=False, stop=True)
                    ins.then_inc(full["mi"], 1)
                elif kind == "meta":
                    b = step[1]
                    tr.wait_freed(pe, ("ropeT", "ak", META))
                    tr.wait_freed(pe, ("ropeT", "aq", b))
                    mi.wait_free(pe, step)
                    for j in range(4):
                        ins = pe.matmul(bank[6][:, 32 * j:32 * j + 32], qT[:, j, b * P:(b + 1) * P], kmT[:, j, :],
                                        start=True, stop=True)
                    ins.then_inc(full["mi"], 1)
                elif kind == "score":
                    _, b, h = step
                    tr.wait_freed(pe, ("ropeT", "ak", b))
                    sd.wait_free(pe, step)
                    lanes = slice(64 * (h % 2), 64 * (h % 2) + 64)
                    w = (b + 1) * P
                    pe.matmul(bank[sd.bank[step]][:, 0:w], qT[lanes, h // 2, b * P:(b + 1) * P], kT[lanes, h // 2, 0:w],
                              start=True, stop=True).then_inc(full["sd"], 1)
                elif kind == "probT":
                    _, b, h = step
                    pe.wait_ge(s_exp, scores.at((b, h)))
                    transposes(step, [prob[:, h % PROBS, j * P:(j + 1) * P] for j in range(b + 1)])
                elif kind == "pv":
                    _, b, h = step
                    n = probTs.n[(b, h)]
                    tr.wait_freed(pe, ("probT", b, h))
                    if h == 0:
                        mi.wait_free(pe, ("attn", b))
                        for t in range(b + 1):
                            pj.wait_freed(pe, ("av", t))
                    c = slice(h * HD, (h + 1) * HD)
                    for j in range(b + 1):
                        ins = pe.matmul(bank[7][:, c], probT[:, n % 2, j * P:(j + 1) * P], V[:, j, c],
                                        start=(h == 0 and j == 0), stop=False, skip_group_check=True)
                    ins.then_inc(s_pv, 1)
                elif kind == "metaT":
                    b = step[1]
                    pe.wait_ge(s_pmexp, pmetas.at(b))
                    transposes(step, [pm[:, b % 2, :]])
                elif kind == "attn":
                    b = step[1]
                    tr.wait_freed(pe, ("metaT", b))
                    pe.wait_ge(s_vm, 16 * HEADS)
                    pe.matmul(bank[7][:, :], pmT[:, :], V_meta[:, :], start=False, stop=True, skip_group_check=True)\
                        .then_inc(full["mi"], 1)
                elif kind == "mixT":
                    _, t, half = step
                    if half == 0:
                        pe.wait_ge(s_mixA, attns.at(t))
                    else:
                        pe.wait_ge(s_mixH, mixHs.at(t))
                    src = mixH if half else mixA
                    transposes(step, [src[:, t, j * P:(j + 1) * P] for j in range(4)])


def program(nc, arrays, out_shape):
    aps = []
    for name, a in arrays.items():
        aps.append(nc.dram_tensor(name, a.shape, mybir.dt.from_np(a.dtype), kind="ExternalInput").ap())
    aps.append(nc.dram_tensor("out_0_dram", out_shape, F32, kind="ExternalOutput").ap())
    hymba_layer(nc, *aps)


_INS = ["x", "meta_tokens", "mix_norm", "w_in", "idx_k_norm_g", "idx_k_norm_b", "attn_out_norm",
        "hgrn_lb_logits", "hgrn_out_norm", "w_out", "final_norm"]


def kernel(**inputs):
    import concourse.bacc as bacc
    from concourse.bass_utils import run_bass_kernel_spmd

    nc = bacc.Bacc("TRN2", target_bir_lowering=False, num_devices=1)
    arrays = {f"in_{n}": np.ascontiguousarray(inputs[n]) for n in _INS}
    sums, after, kept = level_tables()
    cos, sin = rope_tables()
    causal = np.where(np.arange(P)[None, :] <= np.arange(P)[:, None], 0.0, NEG).astype(np.float32)
    arrays |= {"t_ident": np.eye(P, dtype=np.float32), "t_cos": cos, "t_sin": sin,
               "t_sums": sums.reshape(P, -1), "t_after": after, "t_kept": kept, "t_causal": causal}
    program(nc, arrays, inputs["x"].shape)
    r = run_bass_kernel_spmd(nc, [arrays], core_ids=[0])
    return r.results[0]["out_0_dram"]
```

```python
from contextlib import ExitStack

import numpy as np

import concourse.bass as bass
from concourse import mybir

ACT = mybir.ActivationFunctionType
ALU = mybir.AluOpType
AX = mybir.AxisListType
F32 = mybir.dt.float32
F32R = mybir.dt.float32r
U8 = mybir.dt.uint8

P = 128
SEQ, D, NMETA = 512, 1024, 16
HEADS, HD = 8, 64
AW = HEADS * HD
GH, GK = 4, 128
TILES = SEQ // P
META = TILES
KC = D // P
QUARTERS = 4
KQ = KC // QUARTERS
TOPK = min(256, SEQ // 4)
RAW, RING, PROBS = 3, 6, 4
META_LO = 32
LEVELS = 7
TOP_OPS = 7
LAG = 5
CUTS = (0, 7, 13, 18, 22, 26, 30, 33)
INF_LEVEL = LEVELS
EPS = 1e-6
ATTN_SCALE = HD ** -0.5
IDX_SCALE = (8 ** -0.5) * (64 ** -0.5)
NEG = -1.0e30
TAKEN = -3.0e38
IKW = 72

GROUPS = {
    "hf": (3144, 512, [0, 1, 2, 3, META]),
    "ikw": (2560, IKW, [0]),
    "iq": (2048, 512, [1, 2, 3]),
    "hi": (3656, 512, [META, 0, 1, 2, 3]),
    "hq": (2632, 512, [0, 1, 2, 3]),
    "hg": (4168, 512, [0, 1, 2, 3]),
    "ag": (1536, 512, [0, 1, 2, 3]),
    "ak": (512, 512, [META, 0, 1, 2, 3]),
    "aq": (0, 512, [0, 1, 2, 3]),
    "av": (1024, 512, [META, 0, 1, 2, 3]),
    "o0": (0, 512, [0, 1, 2, 3]),
    "o1": (512, 512, [0, 1, 2, 3]),
}
ORDER = list(GROUPS)


def row_chunk(g, k):
    return (k + KC // 2) % KC if g in ("o0", "o1") else k


def level_tables():
    u, p = np.meshgrid(np.arange(P), np.arange(P), indexing="ij")
    sums = np.zeros((P, LEVELS + 1, P), np.float32)
    for l in range(LEVELS):
        m = 1 << l
        mid = (p // (2 * m)) * 2 * m + m
        key = p < mid
        sums[:, l] = np.where(key, (u > p) & (u < mid), (u >= mid) & (u <= p))
    sums[:, INF_LEVEL] = u <= p
    after = (u > p).astype(np.float32)
    s, t = u, p
    level = np.full((P, P), -1)
    for l in range(LEVELS):
        m = 1 << l
        mid = (s // (2 * m)) * 2 * m + m
        level[(s // (2 * m) == t // (2 * m)) & (s < mid) & (t >= mid)] = l
    pieces = [s == t] + [level == l for l in (4, 3, 2, 1, 0)]
    kept = np.stack(pieces, 1).astype(np.float32)
    return sums, after, kept


PIECES = 7
BLOCKS = [(0, 64, 64, 128), (0, 32, 32, 64), (64, 96, 96, 128)]


def rope_tables():
    half = HD // 4 // 2
    inv = np.float32(500000.0) ** (-np.arange(half, dtype=np.float32) * np.float32(2.0) / np.float32(2 * half))
    pos = np.zeros((P, TILES + 1), np.float32)
    for t in range(TILES):
        pos[:, t] = NMETA + t * P + np.arange(P)
    pos[:NMETA, META] = np.arange(NMETA)
    ang = (pos[:, :, None] * inv.astype(np.float32)).astype(np.float32)
    cos, sin = np.cos(ang.astype(np.float64)), np.sin(ang.astype(np.float64))
    return (np.concatenate([cos, cos], 2).astype(np.float32), np.concatenate([-sin, sin], 2).astype(np.float32))


def schedule():
    s = []

    def proj(g, i):
        s.append(("proj", g, GROUPS[g][2][i]))

    def weights(g, *qs):
        s.extend(("weights", g, q) for q in qs)

    def group(g, between=None):
        units = GROUPS[g][2]
        nxt = ORDER[ORDER.index(g) + 1] if g != ORDER[-1] else None
        between, last = between or {}, len(s)
        for i in range(len(units)):
            early = [q for q in range(2) if nxt and i == max(0, min(q + 1, len(units) - 2))]
            if len(units) == 1:
                weights(nxt, *early)
            if i == len(units) - 1 and nxt:
                n = len(s) - last
                s.insert(last + (n // 2 if i else n), ("weights", nxt, 2))
                s.insert(len(s) - (s[-1][0] == "ropeT"), ("weights", nxt, 3))
            proj(g, i)
            if len(units) > 1:
                weights(nxt, *early)
            last = len(s)
            s.extend(between.get(i, []))

    def gates(t, hp, levels):
        return [("gate", t, hp, l) for l in levels]

    def turn(t, hp):
        last = (t, hp) == (TILES - 1, 1)
        nt, nhp = (t, 1) if hp == 0 else (t + 1, 0)
        out = [("piece", t, hp, j) for j in range(3)]
        if hp == 0 and t:
            out += [("state", t - 1)]
        out += gates(t, hp, [3, 2, 1, 0, INF_LEVEL])
        if last:
            return out + [("piece", t, hp, j) for j in range(3, PIECES)] + [("out", t), ("mixH", t)]
        if hp == 1:
            out += [("suffix", t), ("kT", nt)]
        out += [("decay", nt, nhp, 1)]
        for j in range(3, PIECES):
            out += [("piece", t, hp, j)]
            if j < PIECES - 1:
                out += gates(nt, nhp, [LEVELS + 2 - j])
        out += [("decay", nt, nhp, 0)]
        if hp == 0 and t:
            out += [("mixH", t - 1)]
        if hp == 1:
            out += [("out", t)]
        return out

    def with_gate(g, t, steps):
        i = next(i for i, s in enumerate(steps) if s[0] == "gate" and s[3] == INF_LEVEL)
        return steps[:i + 1] + [("silu", g, t)] + steps[i + 1:]

    def index(b):
        return [("index", b, h) for h in range(8)]

    def attend(first, last):
        out = []
        for n in range(first, last):
            b, h = divmod(n, HEADS)
            if b < TILES:
                out.append(("probT", b, h))
            ahead, ah = divmod(n + 3, HEADS)
            if ahead < TILES:
                if ah == 0:
                    out.append(("meta", ahead))
                out.append(("score", ahead, ah))
                if ah == HEADS - 1:
                    out.append(("pmeta", ahead))
            if n:
                pb, ph = divmod(n - 1, HEADS)
                if pb < TILES:
                    out.append(("pv", pb, ph))
                if ph == HEADS - 3:
                    out.append(("metaT", pb))
                if ph == HEADS - 1:
                    out.append(("attn", pb))
                if ph == 1 and pb:
                    out.append(("mixA", pb - 1))
                if ph == 2 and pb:
                    out.append(("mixT", pb - 1, 0))
        return out

    rounds = [(kind, r, b) for r in range(TOPK // 8) for kind in ("find", "take") for b in range(1, TILES)]

    def top(n, steps=()):
        out, steps, n = [], list(steps), min(n, len(rounds))
        for i in range(n):
            out.append(rounds.pop(0))
            out += steps[len(steps) * i // n:len(steps) * (i + 1) // n]
        return out + (steps if n == 0 else [])

    s += [("norm", 0)]
    weights("hf", 0)
    s += [("hT", 0, 0), ("hT", 0, 1)]
    s += [("norm", 1)]
    weights("hf", 1, 2)
    s += [("hT", 1, 0), ("hT", 1, 1), ("norm", 2)]
    weights("hf", 3)
    s += [("floor", 0)]
    group("hf", {0: [("hT", 2, 0), ("hT", 2, 1), ("norm", 3), ("floor", 1)],
                 1: [("hT", 3, 0), ("hT", 3, 1), ("norm", META), ("gate f", 0)],
                 2: [("gate f", 1), ("hT", META, 0), ("hT", META, 1)], 3: [("gate f", 2), ("gate f", 3)],
                 4: []})
    group("ikw", {0: [("gate f", META), ("ikT",)]})
    logs = [("log", t) for t in GROUPS["hf"][2]]
    group("iq", {0: [logs[0]],
                 1: [("ropeT", "iq", 1), ("kiT",), logs[1], ("ropeT", "iq", 2)] + index(1),
                 2: [logs[2], ("ropeT", "iq", 3)] + index(2)[0:4]})
    T = TOP_OPS
    group("hi", {0: [logs[3]] + index(2)[4:], 1: [logs[4]] + index(3)[0:4], 2: index(3)[4:], 3: top(T), 4: top(T)})
    group("hq", {0: top(T, [("suffix", META), ("kT", 0)]), 1: top(T, [("state", META)]),
                 2: top(T, [("decay", 0, 0, 1), ("decay", 0, 0, 0)]),
                 3: top(T, gates(0, 0, [6, 5, 4]))})
    group("hg", {t: with_gate("hg", t, turn(t // 2, t % 2)) for t in range(TILES)})
    group("ag", {t: with_gate("ag", t, turn(2 + t // 2, t % 2)) for t in range(TILES)})
    group("ak", {0: top(T), 1: top(T) + [("ropeT", "ak", META), ("ropeT", "ak", 0)],
                 2: top(T) + [("ropeT", "ak", 1)], 3: top(T) + [("ropeT", "ak", 2)], 4: top(T)})
    group("aq", {0: top(T) + [("ropeT", "ak", 3)], 1: top(T) + [("ropeT", "aq", 0)],
                 2: top(len(rounds)) + [("biases",), ("ropeT", "aq", 1)], 3: [("ropeT", "aq", 2)]})
    group("av", {0: [("ropeT", "aq", 3), ("meta", 0), ("score", 0, 0), ("score", 0, 1), ("score", 0, 2)],
                 1: attend(*CUTS[0:2]), 2: attend(*CUTS[1:3]) + [("mixT", 0, 1)],
                 3: attend(*CUTS[2:4]) + [("mixT", 1, 1)], 4: [("mixT", 2, 1)] + attend(*CUTS[3:5])})
    group("o0", {0: [("mixT", 3, 1)] + attend(*CUTS[4:6]), 1: attend(*CUTS[5:7]),
                 2: attend(*CUTS[6:8]) + [("mixA", 3), ("mixT", 3, 0)]})
    group("o1", {0: [("half", 0), ("half", 1)], 1: [("half", 2), ("half", 3), ("final", 0), ("final", 1)],
                 2: [("final", 2)], 3: [("final", 3)]})
    return s


SCHEDULE = schedule()

FILL = {"meta": 1.6, "kiT": 4, "ropeT": 7, "out": 1.4, "decay": 0.5, "state": 1, "index": 1, "score": 2.3,
        "probT": 0.5, "pv": 8, "metaT": 1, "attn": 1.5, "mixT": 0.5, "ikT": 1, "suffix": 1,
        "pieces": (0.6, 0.6, 1.2, 2, 1, 1.6, 1.3)}


def fill_before(step):
    return FILL["pieces"][step[3]] if step[0] == "piece" else FILL.get(step[0], 0)


def tensor_order():
    order, between = [], []
    for step in SCHEDULE:
        if step[0] == "proj":
            _, g, t = step
            needs = {}
            for i, (s, _) in enumerate(between):
                if s[0] == "hT" and (s[1] == t or g in ("hq", "ikw")) or g in ("o0", "o1") and s == ("mixT", t, 1):
                    needs[0] = i + 1
                if g in ("o0", "o1") and s == ("mixT", t, 0):
                    needs[KC // 2] = min(i + 1 + LAG, len(between))
            first = needs.get(0, 0)
            order += between[:first]
            between = between[first:]
            want = np.cumsum([fill_before(s) for s, _ in between])
            done = 0
            for k in range(KC):
                while k and done < needs.get(k, 0) - first:
                    order.append(between[done])
                    done += 1
                order.append((step, k))
                while done < len(between) and (k == KC - 1 or want[done] * (KC - 1) <= (k + 1) * want[-1]):
                    order.append(between[done])
                    done += 1
            between = []
        else:
            between.append((step, None))
    early = [(("proj", "o1", 0), k) for k in range(KC - 2)]
    order = [o for o in order if o not in early]
    wait = order.index((("mixT", TILES - 1, 0), None))
    return order[:wait] + early + order[wait:] + between


TENSOR_ORDER = tensor_order()


class Order:

    def __init__(self, keys):
        self.keys = list(keys)
        self.n = {k: i for i, k in enumerate(self.keys)}
        assert len(self.n) == len(self.keys), [k for k in self.keys if self.keys.count(k) > 1][:5]

    def at(self, key):
        return self.n[key] + 1


class Banks:

    def __init__(self, full, free, turns):
        self.full, self.free = full, free
        self.order = Order([k for k, _ in turns])
        self.bank = dict(turns)
        seen = {}
        self.turn = {}
        for k, b in turns:
            self.turn[k] = seen.get(b, 0)
            seen[b] = self.turn[k] + 1

    def wait_free(self, eng, key):
        if self.turn[key]:
            eng.wait_ge(self.free[self.bank[key]], self.turn[key])

    def wait_full(self, eng, key):
        eng.wait_ge(self.full, self.order.at(key))

    def wait_freed(self, eng, key):
        eng.wait_ge(self.free[self.bank[key]], self.turn[key] + 1)

    def freed(self, key):
        return self.free[self.bank[key]]


def units():
    return [s[1:] for s in SCHEDULE if s[0] == "proj"]


def hymba_layer(nc, x, meta_tokens, mix_norm, w_in, idx_g, idx_b, attn_g, lb_logits, hgrn_g, w_out,
                final_g, t_ident, t_cos, t_sin, t_sums, t_after, t_kept, t_causal, out):
    with ExitStack() as ctx:
        def sb(name, shape, dt=F32, where=ctx):
            return where.enter_context(nc.sbuf_tensor(name, shape, dt))

        def sem(name):
            return ctx.enter_context(nc.semaphore(name))

        hT_hi = sb("hT_hi", [P, KC, SEQ], F32R)
        hT_lo = sb("hT_lo", [P, KC, SEQ], F32R)
        hT_meta = sb("hT_meta", [P, KC, META_LO + NMETA], F32R)
        w_raw = sb("w_raw", [P, RAW, KQ, 512])
        w_hi = sb("w_hi", [P, RING, KQ, 512], F32R)
        w_lo = sb("w_lo", [P, RING, KQ, 512], F32R)
        ident = sb("ident", [P, P])
        cos = sb("cos", [P, TILES + 1, 16])
        sin = sb("sin", [P, TILES + 1, 16])
        sums = sb("sums", [P, LEVELS + 1, P], F32R)
        after = sb("after", [P, P], F32R)
        kept = sb("kept", [P, PIECES - 1, P], U8)
        bias = [sb(f"bias{b}", [P, (b + 1) * P]) for b in range(TILES)]
        rows = sb("rows", [P, 2, 512])
        temp = sb("temp", [P, 2, 512])
        mixH = sb("mixH", [P, TILES, 512])
        small = sb("small", [P, 136])
        idxw = sb("idxw", [P, TILES, 8])
        mhalf = small[:, 0:8]
        sq_x, rs_x = small[:, 8:13], small[:, 13:18]
        ik_mean, ik_var, ik_rs = small[:, 18:22], small[:, 22:26], small[:, 26:30]
        ms_h, rs_h = small[:, 30:34], small[:, 34:38]
        mmax, pmax, nmax, psums = ([small[:, c + 8 * i:c + 8 * i + 8] for i in range(2)] for c in (38, 54, 88, 104))
        prec, msum = small[:, 70:78], small[:, 120:128]
        ms_a, rs_a = small[:, 78:79], small[:, 79:80]
        ms_f, rs_f = small[:, 128:136].rearrange("p (h t) -> p h t", h=2), small[:, 84:88]
        top8 = sb("top8", [P, TILES, 8])
        decay_end = sb("decay_end", [P, 2, GH])
        swapped = sb("swapped", [P, P])

        with ExitStack() as r1:
            x_t = sb("x_t", [P, 3, D], where=r1)
            gb = sb("gb", [P, D], where=r1)
        with ExitStack() as r1:
            qi_even = sb("qi_even", [P, 4, 3 * P], F32R, where=r1)
            ki_hi = sb("ki_hi", [P, SEQ], F32R, where=r1)
            rel = sb("rel", [P, 2, SEQ], where=r1)
            ik_row = sb("ik_row", [P, TILES, IKW], where=r1)
            ik_two = sb("ik_two", [P, TILES, 2, 64], where=r1)
            idx_gb = sb("idx_gb", [P, 2, 64], where=r1)
            ikT = rel[:, 0, :]
        with ExitStack() as r1:
            mixA = sb("mixA", [P, TILES, 512], where=r1)
            gain_a = sb("gain_a", [P, 512], where=r1)
            gain_h = sb("gain_h", [P, GK], where=r1)
            v_row = sb("v_row", [NMETA, 512], where=r1)
            o_row = sb("o_row", [P, 512], where=r1)
            junk = sb("junk", [P, P], where=r1)
        sb("region1", [P, 16 * 1024 // 4])

        with ExitStack() as r2:
            g_hi = sb("g_hi", [P, TILES + 1, 512], F32R, where=r2)
            g_lo = sb("g_lo", [P, TILES + 1, 512], F32R, where=r2)
            hk = sb("hk", [P, TILES + 1, 512], where=r2)
            hv = sb("hv", [P, TILES + 1, 512], where=r2)
            hqT = sb("hqT", [P, GH, SEQ], where=r2)
            E = sb("E", [P, LEVELS + 1, 2, P], where=r2)
            A = sb("A", [P, GH, P], where=r2)
            k_end = sb("k_end", [P, 512], where=r2)
            with ExitStack() as r3:
                qi_odd = sb("qi_odd", [P, 4, 3 * P], F32R, where=r3)
            q_inf = sb("q_inf", [P, GH, P], where=r2)
            S = sb("S", [P, GH, GK], where=r2)
            hkT = sb("hkT", [P, GH, P], where=r2)
            ki_lo = sb("ki_lo", [P, SEQ], F32R, where=r2)
        with ExitStack() as r2:
            k_two = sb("k_two", [P, 4, 2, SEQ], F32R, where=r2)
            k_lo = sb("k_lo", [P, 4, SEQ], F32R, where=r2)
            km_two = sb("km_two", [P, 4, 2, NMETA], where=r2)
            V = sb("V", [P, TILES, 512], where=r2)
            V_meta = sb("V_meta", [P, 512], where=r2)
            q_two = sb("q_two", [P, 4, 2, SEQ], F32R, where=r2)
            prob = sb("prob", [P, PROBS, SEQ], where=r2)
            pm = sb("pm", [P, 2, P], where=r2)
            probT = sb("probT", [P, 2, SEQ], where=r2)
            fb = sb("fb", [P, D], where=r2)
            pmT = sb("pmT", [P, P], where=r2)
        sb("region2", [P, 68 * 1024 // 4])

        lb, half_span, logits = mixH[:, 0, :], mixH[:, 1, :], mixH[:, 2:4, :]
        middle = lb
        qi_pair = (qi_even, qi_odd)
        y = (mixH, mixA)
        staged = hqT[:, :, :].rearrange("p h t -> p (h t)")
        attn_row, attn_squares = temp[:, 0, :], temp[:, 1, :]

        bank = [ctx.enter_context(nc.psum_tensor(f"bank{i}", [P, 512], F32)) for i in range(8)]

        s_ident, s_staged, s_rot, s_causal = sem("s_ident"), sem("s_staged"), sem("s_rot"), sem("s_causal")
        s_xin = [sem(f"s_xin{t}") for t in range(TILES + 1)]
        s_xres = [[sem(f"s_xres{half}_{t}") for t in range(TILES)] for half in range(2)]
        s_raw = [sem(f"s_raw{i}") for i in range(RAW)]
        s_gb, s_logits, s_idxg, s_gains, s_fb = (sem(n) for n in ("s_gb", "s_logits", "s_idxg", "s_gains", "s_fb"))
        s_vmeta, s_out = sem("s_vmeta"), sem("s_out")
        s_whi, s_wlo_dve, s_wlo_pool, s_wused = sem("s_whi"), sem("s_wlo_dve"), sem("s_wlo_pool"), sem("s_wused")
        s_kept, s_azero, s_vzero = sem("s_kept"), sem("s_azero"), sem("s_vzero")
        s_sq, s_rstd, s_xn, s_hhi = sem("s_sq"), sem("s_rstd"), sem("s_xn"), sem("s_hhi")
        s_lbexp, s_lb = sem("s_lbexp"), sem("s_lb")
        s_tanh, s_gate, s_mlow, s_mtanh = sem("s_tanh"), sem("s_gate"), sem("s_mlow"), sem("s_mtanh")
        s_fk, s_ghi, s_glo = sem("s_fk"), sem("s_ghi"), sem("s_glo")
        s_turned = sem("s_turned")
        s_rope, s_ikvar, s_ikrs, s_iktwo, s_acc = (sem(n) for n in ("s_rope", "s_ikvar", "s_ikrs", "s_iktwo", "s_acc"))
        s_gated, s_kend, s_osq, s_ors, s_mixH = (sem(n) for n in ("s_gated", "s_kend", "s_osq", "s_ors", "s_mixH"))
        s_nmax, s_exp, s_pmsub, s_pmexp, s_pv = (sem(n) for n in ("s_nmax", "s_exp", "s_pmsub", "s_pmexp", "s_pv"))
        s_asq, s_ars, s_mixA, s_mhi = sem("s_asq"), sem("s_ars"), sem("s_mixA"), sem("s_mhi")
        s_half, s_halfg, s_ysq, s_yrs = sem("s_half"), sem("s_halfg"), sem("s_ysq"), sem("s_yrs")
        s_first, s_second = sem("s_first"), sem("s_second")
        s_a, s_v, s_p = sem("s_a"), sem("s_v"), sem("s_p")

        full = {n: sem(f"{n}_full") for n in ("pj", "tr", "sd", "mi")}
        free = {n: {b: sem(f"{n}_free{b}") for b in bs}
                for n, bs in (("pj", (0, 1)), ("tr", (2, 3)), ("sd", (4, 5)), ("mi", (6, 7)))}

        def of(*kinds):
            return [s for s in SCHEDULE if s[0] in kinds]

        pj = Banks(full["pj"], free["pj"], [(u, i % 2) for i, u in enumerate(units())])
        tr_keys = of("hT", "kT", "ikT", "kiT", "ropeT", "probT", "metaT", "mixT")
        tr = Banks(full["tr"], free["tr"], [(k, 2 + i % 2) for i, k in enumerate(tr_keys)])
        sd_turns = []
        for s in SCHEDULE:
            if s[0] in ("index", "score"):
                sd_turns.append((s, 4 + s[2] % 2))
            if s[0] == "decay":
                sd_turns += [(s + (i,), 4 + i) for i in range(2)]
        sd = Banks(full["sd"], free["sd"], sd_turns)
        mi_turns = []
        for s in SCHEDULE:
            if s[0] == "piece":
                mi_turns.append((s, 6 + s[3] % 2))
            if s[0] in ("suffix", "state", "meta"):
                mi_turns.append((s, 6))
            if s[0] in ("out", "attn"):
                mi_turns.append((s, 7))
        mi = Banks(full["mi"], free["mi"], mi_turns)

        quarters = Order([s[1:] for s in of("weights")])

        def lo_on_pool(n):
            g, q = quarters.keys[n]
            return q in {"hf": (1,), "ikw": (0, 2), "iq": (2,)}.get(g, range(QUARTERS))

        lo_pool = Order([k for i, k in enumerate(quarters.keys) if lo_on_pool(i)])
        lo_dve = Order([k for i, k in enumerate(quarters.keys) if not lo_on_pool(i)])
        used = Order([k for k in quarters.keys if k[1] != QUARTERS - 1])

        def wait_lo(eng, key):
            if key in lo_pool.n:
                eng.wait_ge(s_wlo_pool, lo_pool.at(key))
            else:
                eng.wait_ge(s_wlo_dve, lo_dve.at(key))

        def wait_slot_used(eng, n):
            if n >= RING:
                g, q = quarters.keys[n - RING]
                if q == QUARTERS - 1:
                    pj.wait_full(eng, (g, GROUPS[g][2][-1]))
                else:
                    eng.wait_ge(s_wused, used.at((g, q)))

        norms = Order([s[1] for s in of("norm")])
        hTs = Order(of("hT"))
        turned = Order([s for s in of("kiT", "ropeT") if s[-1] != META])
        ropes = Order([u for u in units() if u[0] in ("iq", "ak", "aq")])
        silus = Order([u for u in units() if u[0] in ("hq", "hg", "ag")])
        hfs = Order(GROUPS["hf"][2])
        temps = Order([u for u in units() if u[0] in ("hf", "hq", "hg", "ag")])
        rels = Order([s[1:] for s in of("index")])
        pairs = Order([s[1:3] for s in of("piece") if s[3] == 0])
        gates = Order([s[1:] for s in of("gate")])
        suffixes = Order([s[1] for s in of("suffix")])
        states = Order([s[1] for s in of("state")])
        outs = Order([s[1] for s in of("out")])
        mixHs = Order([s[1] for s in of("mixH")])
        kTs = Order([s[1] for s in of("kT")])
        metas = Order([g for g, t in units() if t == META])
        pmetas = Order([s[1] for s in of("pmeta")])
        scores = Order([s[1:] for s in of("score")])
        probTs = Order([s[1:] for s in of("probT")])
        attns = Order([s[1] for s in of("attn")])
        mixTs = Order([s[1:] for s in of("mixT")])
        finals = Order([s[1] for s in of("final")])

        SIDES = [(0, slice(0, HD), slice(HD, P)), (1, slice(HD, P), slice(0, HD))]

        def rows_of(t):
            return NMETA if t == META else P

        def cols_of(t):
            return slice(t * P, (t + 1) * P)

        def meta_of(g):
            return {"hf": temp_of(("hf", META)), "hi": hv[0:NMETA, META, :], "av": v_row[:, :],
                    "ak": rows[0:NMETA, ropes.n[("ak", META)] % 2, :]}[g]

        def temp_of(u):
            return temp[0:(rows_of(u[1]) if u[0] == "hf" else P), temps.n[u] % 2, :]

        def f_of(t):
            if t == META:
                return k_end[0:NMETA, :]
            return E[:, :, :, :].rearrange("p l h t -> p (l h t)")[:, t * 512:(t + 1) * 512]

        def wait_temp(eng, u):
            n = temps.n[u]
            if n < 2:
                return
            old = temps.keys[n - 2]
            if old[0] == "hf":
                eng.wait_ge(s_fk, hfs.at(old[1]))
            else:
                pj.wait_freed(eng, old)

        block = ctx.enter_context(nc.Block())

        @block.sync
        def _(sp):
            def load_x(t):
                r = rows_of(t)
                n = norms.n[t]
                if n >= 3:
                    tr.wait_full(sp, ("hT", norms.keys[n - 3], 1))
                src = meta_tokens if t == META else x[0, t * P:(t + 1) * P, :]
                sp.dma_start(x_t[0:r, n % 3, :], src).then_inc(s_xin[t], 16)

            def load_w(n):
                g, q = quarters.keys[n]
                c0, width, _ = GROUPS[g]
                w = w_out[0] if g in ("o0", "o1") else w_in[0]
                k0 = row_chunk(g, q * KQ)
                src = w[k0 * P:(k0 + KQ) * P, c0:c0 + width]
                if n >= RAW:
                    wait_lo(sp, quarters.keys[n - RAW])
                sp.dma_start(w_raw[:, n % RAW, :, 0:width], src.rearrange("(k p) c -> p k c", p=P))\
                    .then_inc(s_raw[n % RAW], 16)

            def load_tables():
                sp.dma_start(staged[:, 0:1024], t_sums).then_inc(s_staged, 16)
                sp.dma_start(staged[:, 1024:1152], t_after).then_inc(s_staged, 16)
                sp.dma_start(staged[:, 1152:1152 + 6 * P], t_kept.rearrange("p j t -> p (j t)")).then_inc(s_staged, 16)
                sp.dma_start(cos[:], t_cos).then_inc(s_rot, 16)
                sp.dma_start(sin[:], t_sin).then_inc(s_rot, 16)
                sp.dma_start(bias[0][:], t_causal).then_inc(s_causal, 16)

            load_x(0)
            load_w(0)
            load_w(1)
            load_x(1)
            load_w(2)
            load_x(2)
            sp.dma_start(logits, lb_logits.rearrange("(o a) c -> o a c", o=1).broadcast_to([P, 2, 512]))\
                .then_inc(s_logits, 16)
            load_w(3)
            load_x(3)
            load_tables()
            load_w(4)
            load_x(META)
            for n in range(5, len(quarters.keys)):
                load_w(n)
                if quarters.keys[n] == ("o0", 0):
                    pj.wait_freed(sp, ("av", META))
                    sp.wait_ge(s_vzero, 1)
                    for h in range(HEADS):
                        sp.dma_start(V_meta[h * NMETA:(h + 1) * NMETA, h * HD:(h + 1) * HD],
                                     v_row[:, h * HD:(h + 1) * HD]).then_inc(s_vmeta, 16)
                    sp.dma_start(fb[:], final_g.rearrange("(o c) -> o c", o=1).broadcast_to([P, D])).then_inc(s_fb, 16)
                if quarters.keys[n] == ("hg", 1):
                    sp.wait_ge(s_acc, rels.at((3, 7)))
                    sp.dma_start(gain_a[:], attn_g[0:1, :].broadcast_to([P, 512])).then_inc(s_gains, 16)
                    sp.dma_start(gain_h[:], hgrn_g[0:1, :].broadcast_to([P, GK])).then_inc(s_gains, 16)
                if quarters.keys[n] == ("ikw", 3):
                    tr.wait_full(sp, ("hT", META, 1))
                    sp.dma_start(idx_gb[:, 0, :], idx_g[0:1, :].broadcast_to([P, 64])).then_inc(s_idxg, 16)
                    sp.dma_start(idx_gb[:, 1, :], idx_b[0:1, :].broadcast_to([P, 64])).then_inc(s_idxg, 16)
                for t, half in {("o0", 3): [(0, 0), (1, 0)], ("o1", 0): [(2, 0)], ("o1", 1): [(3, 0)],
                                ("o1", 3): [(t, 1) for t in range(TILES)]}.get(quarters.keys[n], []):
                    tr.wait_full(sp, ("mixT", t, 1 - half))
                    sp.dma_start(y[half][:, t, :], x[0, t * P:(t + 1) * P, 512 * half:512 * half + 512])\
                        .then_inc(s_xres[half][t], 16)
            for t in range(TILES):
                for half, done in ((0, s_first), (1, s_second)):
                    c = slice(512 * half, 512 * half + 512)
                    sp.wait_ge(done, t + 1)
                    sp.dma_start(out[0, t * P:(t + 1) * P, c], y[half][:, t, :]).then_inc(s_out, 16)
            sp.wait_ge(s_out, 2 * 16 * TILES)

        @block.gpsimd
        def _(pool):
            steps = [0]

            def link(ins):
                steps[0] += 1
                ins.then_inc(s_p, 1)
                pool.wait_ge(s_p, steps[0])

            def rstd(dst, src, scale, done, r=P, eps=EPS):
                link(pool.tensor_scalar(dst, src, scale, eps, ALU.mult, ALU.add))
                pool.tensor_tensor(dst, dst, mhalf[0:r, 0:dst.shape[1]], ALU.pow).then_inc(done, 1)

            link(pool.memset(mhalf, -0.5))
            pool.memset(A[:, :, :], 0.0).then_inc(s_azero, 1)
            for step in SCHEDULE:
                kind = step[0]
                if kind == "log":
                    t = step[1]
                    r = rows_of(t)
                    pool.wait_ge(s_ghi, hfs.at(t))
                    pool.tensor_tensor(g_lo[0:r, t, :], f_of(t), g_hi[0:r, t, :].bitcast(F32),
                                       ALU.subtract).then_inc(s_glo, 1)
                elif kind == "norm":
                    t = step[1]
                    r = rows_of(t)
                    pool.wait_ge(s_sq, norms.at(t))
                    rstd(rs_x[0:r, t:t + 1], sq_x[0:r, t:t + 1], 1.0 / D, s_rstd, r)
                elif kind == "weights" and step[1:] in lo_pool.n:
                    n = quarters.n[step[1:]]
                    width = GROUPS[step[1]][1]
                    pool.wait_ge(s_whi, n + 1)
                    pool.tensor_tensor(w_lo[:, n % RING, :, 0:width], w_raw[:, n % RAW, :, 0:width],
                                       w_hi[:, n % RING, :, 0:width].bitcast(F32), ALU.subtract)\
                        .then_inc(s_wlo_pool, 1)
                elif kind == "silu":
                    pj.wait_freed(pool, step[1:])
                    pool.wait_ge(s_gains, 32)
                    if step[1] == "hg":
                        gate = mixH[:, step[2], :].rearrange("p (h v) -> p h v", h=GH)
                        gain = gain_h[:, :].rearrange("p (o v) -> p o v", o=1).broadcast_to([P, GH, GK])
                    else:
                        gate, gain = mixA[:, step[2], :], gain_a[:, :]
                    pool.tensor_tensor(gate, gate, gain, ALU.mult).then_inc(s_gate, 1)
                elif kind == "ikT":
                    pool.wait_ge(s_ikvar, 1)
                    rstd(ik_rs, ik_var, 1.0 / 64, s_ikrs)
                elif kind == "out":
                    if outs.n[step[1]]:
                        pool.wait_ge(s_mixH, outs.n[step[1]])
                    pool.wait_ge(s_osq, outs.at(step[1]))
                    rstd(rs_h, ms_h, 1.0 / GK, s_ors)
                elif step == ("ropeT", "ak", META):
                    pool.wait_ge(s_mixH, 4)
                    pool.memset(V_meta[:, :], 0.0).then_inc(s_vzero, 1)
                elif kind == "attn":
                    pool.wait_ge(s_asq, attns.at(step[1]))
                    rstd(rs_a, ms_a, 4.0 / AW, s_ars, eps=4.0 * EPS)
                elif kind == "final":
                    t = step[1]
                    pool.wait_ge(s_ysq, finals.at(t))
                    rstd(rs_f[:, t:t + 1], ms_f[:, 1, t:t + 1], 1.0 / D, s_yrs)
                elif kind == "half":
                    t = step[1]
                    pool.wait_ge(s_fb, 16)
                    pool.wait_ge(s_half, t + 1)
                    pool.tensor_tensor(y[0][:, t, :], y[0][:, t, :], fb[:, 0:512], ALU.mult).then_inc(s_halfg, 1)

        @block.scalar
        def _(act):
            steps = [0]

            def link(ins):
                steps[0] += 1
                ins.then_inc(s_a, 1)
                act.wait_ge(s_a, steps[0])

            act.dma_start(gb[:], mix_norm[0:1, :].broadcast_to([P, D])).then_inc(s_gb, 16)
            act.dma_start(ident[:], t_ident).then_inc(s_ident, 16)

            def weights_hi(g, q):
                n = quarters.n[(g, q)]
                width = GROUPS[g][1]
                wait_slot_used(act, n)
                act.wait_ge(s_raw[n % RAW], 16 * (n // RAW + 1))
                ins = act.activation(w_hi[:, n % RING, :, 0:width], w_raw[:, n % RAW, :, 0:width], ACT.Copy)
                ins.then_inc(s_whi, 1)

            def unit(g, t):
                u = (g, t)
                src = bank[pj.bank[u]]
                r = P if g == "hq" else rows_of(t)
                if g in ("o0", "o1"):
                    return
                if t == META:
                    if g == "hf":
                        wait_temp(act, u)
                    if g == "ak":
                        tr.wait_full(act, ("ropeT",) + ropes.keys[ropes.n[u] - 2])
                    if g == "av":
                        act.wait_ge(s_mixH, 4)
                    pj.wait_full(act, u)
                    act.activation(meta_of(g), src[META_LO:META_LO + NMETA, :], ACT.Copy).then_inc(s_mlow, 1)
                    if g == "hf":
                        pj.wait_freed(act, u)
                        act.activation(meta_of(g), meta_of(g), ACT.Tanh, scale=0.5).then_inc(s_mtanh, 1)
                    return
                if g in ("hf", "hq", "hg", "ag"):
                    wait_temp(act, u)
                    pj.wait_full(act, u)
                    ins = act.activation(temp_of(u), src[0:r, :], ACT.Tanh, scale=0.5)
                    ins.then_inc(pj.freed(u) if g == "hf" else s_tanh, 1)
                elif g == "hi":
                    pj.wait_full(act, u)
                    act.activation(hv[0:r, t, :], src[0:r, :], ACT.Copy).then_inc(pj.freed(u), 1)
                elif g == "av":
                    pj.wait_full(act, u)
                    act.wait_ge(s_mixH, 4)
                    dst = v_row[:, :] if t == META else V[:, t, :]
                    act.activation(dst, src[0:r, :], ACT.Copy).then_inc(pj.freed(u), 1)
                elif g == "ikw":
                    pj.wait_full(act, u)
                    act.activation(ikT[0:IKW, :], src[0:IKW, :], ACT.Copy).then_inc(pj.freed(u), 1)
                else:
                    n = ropes.n[u]
                    if n >= 2:
                        tr.wait_full(act, ("ropeT",) + ropes.keys[n - 2])
                    pj.wait_full(act, u)
                    act.activation(rows[0:r, n % 2, :], src[0:r, :], ACT.Copy).then_inc(pj.freed(u), 1)

            for step in SCHEDULE:
                kind = step[0]
                if kind == "norm":
                    t = step[1]
                    r = rows_of(t)
                    act.wait_ge(s_xin[t], 16)
                    if norms.n[t]:
                        act.wait_ge(s_sq, norms.n[t])
                    act.activation(rows[0:r, :, :].rearrange("p a b -> p (a b)"), x_t[0:r, norms.n[t] % 3, :],
                                   ACT.Square, accum_out=sq_x[0:r, t:t + 1]).then_inc(s_sq, 1)
                elif kind == "floor" and step[1] == 1:
                    act.wait_ge(s_lbexp, 1)
                    act.activation(logits, logits, ACT.Exp).then_inc(s_lb, 1)
                elif kind == "hT":
                    _, t, half = step
                    src = bank[tr.bank[step]][:, :].rearrange("p (k t) -> p k t", k=4)
                    ks = slice(4 * half, 4 * half + 4)
                    tr.wait_full(act, step)
                    if t == META:
                        act.activation(hT_meta[:, ks, 0:NMETA], src[:, :, 0:NMETA], ACT.Copy).then_inc(s_hhi, 1)
                    else:
                        act.activation(hT_hi[:, ks, cols_of(t)], src, ACT.Copy).then_inc(s_hhi, 1)
                elif kind == "weights":
                    weights_hi(*step[1:])
                elif kind == "proj":
                    unit(*step[1:])
                elif kind == "log":
                    t = step[1]
                    r = rows_of(t)
                    if hfs.n[t] == 0:
                        act.wait_ge(s_staged, 48)
                        act.activation(sums[:, :, :].rearrange("p l t -> p (l t)"), staged[:, 0:1024], ACT.Copy)
                        act.activation(after[:], staged[:, 1024:1152], ACT.Copy)
                    act.wait_ge(s_fk, hfs.at(t))
                    link(act.activation(f_of(t), f_of(t), ACT.Ln))
                    act.activation(g_hi[0:r, t, :], f_of(t), ACT.Copy).then_inc(s_ghi, 1)
                elif kind == "ikT":
                    tr.wait_full(act, step)
                    act.activation(ik_row[:, :, :], bank[tr.bank[step]][:, 0:TILES * IKW]
                                   .rearrange("p (t c) -> p t c", t=TILES), ACT.Copy).then_inc(tr.freed(step), 1)
                elif kind == "kiT":
                    tr.wait_full(act, step)
                    act.activation(ki_hi[:, :], bank[tr.bank[step]][:, :], ACT.Copy).then_inc(s_turned, 1)
                elif kind == "ropeT":
                    _, g, t = step
                    b4 = bank[tr.bank[step]][:, :].rearrange("p (j t) -> p j t", j=4)
                    tr.wait_full(act, step)
                    if t == META:
                        act.wait_ge(s_mixH, 4)
                        for e, own, other in SIDES:
                            for lanes in (own, other):
                                ins = act.activation(km_two[lanes, :, e, :], b4[own, :, 0:NMETA], ACT.Copy)
                        ins.then_inc(tr.freed(step), 1)
                        continue
                    for e, own, other in SIDES:
                        if g == "iq":
                            ins = act.activation(qi_pair[e][own, :, (t - 1) * P:t * P], b4[own, :, :], ACT.Copy)
                        elif g == "aq":
                            ins = act.activation(q_two[own, :, e, cols_of(t)], b4[own, :, :], ACT.Copy)
                        else:
                            for lanes in (own, other):
                                ins = act.activation(k_two[lanes, :, e, cols_of(t)], b4[own, :, :], ACT.Copy)
                    ins.then_inc(s_turned, 1)
                elif kind == "index":
                    _, b, h = step
                    n = rels.n[(b, h)]
                    if n >= 2:
                        act.wait_ge(s_acc, n - 1)
                    sd.wait_full(act, step)
                    w = (b + 1) * P
                    act.activation(rel[:, n % 2, 0:w], bank[sd.bank[step]][:, 0:w], ACT.Relu)\
                        .then_inc(sd.freed(step), 1)
                elif kind == "kT":
                    t = step[1]
                    tr.wait_full(act, step)
                    if kTs.n[t]:
                        mi.wait_full(act, ("piece", t - 1, 1, 0))
                        act.wait_ge(s_gated, gates.at((t - 1, 1, INF_LEVEL)))
                    act.activation(hkT[:, :, :], bank[tr.bank[step]][:, :].rearrange("p (h t) -> p h t", h=GH),
                                   ACT.Copy).then_inc(tr.freed(step), 1)
                elif kind == "decay":
                    _, t, hp, half = step
                    n = pairs.n[(t, hp)]
                    if n:
                        mi.wait_full(act, ("piece",) + pairs.keys[n - 1] + (2 if half else PIECES - 1,))
                        act.wait_ge(s_gated, gates.at(pairs.keys[n - 1] + (INF_LEVEL,)))
                    for i in range(2):
                        key = step + (i,)
                        sd.wait_full(act, key)
                        act.activation(E[:, 4 * half:4 * half + 4, i, :],
                                       bank[sd.bank[key]][:, :].rearrange("p (l t) -> p l t", l=4), ACT.Exp)\
                            .then_inc(sd.freed(key), 1)
                elif kind == "piece" and step[3] == 1:
                    _, t, hp, j = step
                    pair = slice(2 * hp, 2 * hp + 2)
                    src = bank[mi.bank[step]][:, 0:2 * P].rearrange("p (h t) -> p h t", h=2)
                    mi.wait_full(act, step)
                    mi.wait_freed(act, ("piece", t, hp, 0))
                    for s0, s1, t0, t1 in BLOCKS:
                        ins = act.activation(A[s0:s1, pair, t0:t1], src[s0:s1, :, t0:t1], ACT.Copy)
                    ins.then_inc(mi.freed(step), 1)
                elif kind == "suffix":
                    t = step[1]
                    r = rows_of(t)
                    mi.wait_full(act, step)
                    if suffixes.n[t]:
                        mi.wait_full(act, ("state", suffixes.keys[suffixes.n[t] - 1]))
                    act.activation(k_end[0:r, :], bank[6][0:r, :], ACT.Exp).then_inc(mi.freed(step), 1)
                elif kind == "out":
                    t = step[1]
                    mi.wait_full(act, step)
                    if outs.n[t]:
                        act.wait_ge(s_mixH, mixHs.at(outs.keys[outs.n[t] - 1]))
                    act.activation(o_row[:, :], bank[7][:, :], ACT.Copy, scale=0.5).then_inc(mi.freed(step), 1)
                    mi.wait_freed(act, step)
                    for h in range(GH):
                        ins = act.activation(junk[:, :], o_row[:, h * GK:(h + 1) * GK], ACT.Square,
                                             accum_out=ms_h[:, h:h + 1])
                        if h < GH - 1:
                            link(ins)
                    ins.then_inc(s_osq, 1)
                elif kind == "meta":
                    b = step[1]
                    mi.wait_full(act, step)
                    if b >= 2:
                        tr.wait_full(act, ("metaT", b - 2))
                    else:
                        act.wait_ge(s_mixH, 4)
                    act.activation(pm[:, b % 2, :], bank[6][:, 0:P], ACT.Copy).then_inc(mi.freed(step), 1)
                elif kind == "pmeta":
                    act.wait_ge(s_pmsub, pmetas.at(step[1]))
                    half = pm[:, step[1] % 2, :]
                    act.activation(half, half, ACT.Exp, scale=ATTN_SCALE).then_inc(s_pmexp, 1)
                elif kind == "score":
                    _, b, h = step
                    w = (b + 1) * P
                    act.wait_ge(s_nmax, scores.at((b, h)))
                    act.activation(prob[:, h % PROBS, 0:w], prob[:, h % PROBS, 0:w], ACT.Exp, bias=nmax[b % 2][:, h:h + 1],
                                   scale=ATTN_SCALE, accum_out=psums[b % 2][:, h:h + 1]).then_inc(s_exp, 1)
                elif kind == "probT":
                    _, b, h = step
                    n = probTs.n[(b, h)]
                    w = (b + 1) * P
                    tr.wait_full(act, step)
                    if n >= 2:
                        act.wait_ge(s_pv, n - 1)
                    act.activation(probT[:, n % 2, 0:w], bank[tr.bank[step]][:, 0:w], ACT.Copy)\
                        .then_inc(tr.freed(step), 1)
                elif kind == "metaT":
                    tr.wait_full(act, step)
                    if step[1]:
                        mi.wait_full(act, ("attn", step[1] - 1))
                    act.activation(pmT[:, :], bank[tr.bank[step]][:, 0:P], ACT.Copy).then_inc(tr.freed(step), 1)
                elif kind == "attn":
                    mi.wait_freed(act, step)
                    act.activation(attn_squares, attn_row, ACT.Square, accum_out=ms_a).then_inc(s_asq, 1)
                elif kind == "mixT":
                    _, t, half = step
                    tr.wait_full(act, step)
                    act.activation(hT_hi[:, 4 * half:4 * half + 4, cols_of(t)],
                                   bank[tr.bank[step]][:, :].rearrange("p (k t) -> p k t", k=4), ACT.Copy)\
                        .then_inc(s_mhi, 1)
                elif kind == "half":
                    t = step[1]
                    pj.wait_freed(act, ("o0", t))
                    if t:
                        act.wait_ge(s_half, t)
                    act.activation(rows[:, 0, :], y[0][:, t, :], ACT.Square, accum_out=ms_f[:, 0, t:t + 1])\
                        .then_inc(s_half, 1)
                elif kind == "final":
                    t = step[1]
                    act.wait_ge(s_halfg, t + 1)
                    act.wait_ge(s_yrs, finals.at(t))
                    act.activation(y[0][:, t, :], y[0][:, t, :], ACT.Copy, scale=rs_f[:, t:t + 1]).then_inc(s_first, 1)

        @block.vector
        def _(dve):
            steps = [0]

            def mark(ins):
                steps[0] += 1
                ins.then_inc(s_v, 1)
                return steps[0]

            def link(ins):
                dve.wait_ge(s_v, mark(ins))

            def over_heads(ap, n=HEADS, d=HD):
                return ap.rearrange("p (h o) -> p h o", o=1).broadcast_to([P, n, d])

            def rope(rot, rot_swapped, c, sn, tmp):
                link(dve.tensor_tensor(tmp, rot_swapped, sn, ALU.mult))
                link(dve.tensor_tensor(rot, rot, c, ALU.mult))
                return dve.tensor_tensor(rot, rot, tmp, ALU.add)

            def silu(u, dst):
                z = temp_of(u)
                dve.wait_ge(s_tanh, silus.at(u))
                dve.scalar_tensor_tensor(out=dst, in0=z, scalar=1.0, in1=bank[pj.bank[u]][:, :], op0=ALU.add,
                                         op1=ALU.mult).then_inc(pj.freed(u), 1)

            last_round = {}
            for step in SCHEDULE:
                kind = step[0]
                if kind == "norm":
                    t = step[1]
                    r = rows_of(t)
                    xt = x_t[0:r, norms.n[t] % 3, :]
                    if norms.n[t] == 0:
                        dve.wait_ge(s_gb, 16)
                    dve.wait_ge(s_rstd, norms.at(t))
                    dve.scalar_tensor_tensor(out=xt, in0=xt, scalar=rs_x[0:r, t:t + 1], in1=gb[0:r, :],
                                             op0=ALU.mult, op1=ALU.mult).then_inc(s_xn, 1)
                elif kind == "floor" and step[1] == 0:
                    dve.wait_ge(s_logits, 16)
                    link(dve.tensor_tensor(lb, logits[:, 0, :], logits[:, 1, :], ALU.max))
                    link(dve.tensor_tensor(logits[:, 0, :], logits[:, 0, :], lb, ALU.subtract))
                    dve.tensor_tensor(logits[:, 1, :], logits[:, 1, :], lb, ALU.subtract).then_inc(s_lbexp, 1)
                elif kind == "floor":
                    dve.wait_ge(s_lb, 1)
                    link(dve.tensor_tensor(half_span, logits[:, 0, :], logits[:, 1, :], ALU.add))
                    link(dve.reciprocal(half_span, half_span))
                    link(dve.tensor_tensor(lb, logits[:, 0, :], half_span, ALU.mult))
                    link(dve.tensor_scalar(half_span, lb, -0.5, 0.5, ALU.mult, ALU.add))
                    link(dve.tensor_tensor(middle, lb, half_span, ALU.add))
                elif kind == "hT" or kind == "mixT":
                    _, t, half = step
                    if kind == "hT":
                        dve.wait_ge(s_hhi, hTs.at(step))
                    else:
                        dve.wait_ge(s_mhi, mixTs.at(step[1:]))
                    src = bank[tr.bank[step]][:, :].rearrange("p (k t) -> p k t", k=4)
                    ks = slice(4 * half, 4 * half + 4)
                    if t == META:
                        shape = [P, 4, 2, NMETA]
                        low = hT_meta[:, ks, NMETA:].rearrange("p k (two t) -> p k two t", two=2)
                        src = src[:, :, 0:NMETA].rearrange("p k (o t) -> p k o t", o=1).broadcast_to(shape)
                        high = hT_meta[:, ks, 0:NMETA].rearrange("p k (o t) -> p k o t", o=1).broadcast_to(shape)
                        ins = dve.tensor_tensor(low, src, high.bitcast(F32), ALU.subtract)
                    else:
                        at = (slice(None), ks, cols_of(t))
                        ins = dve.tensor_tensor(hT_lo[at], src, hT_hi[at].bitcast(F32), ALU.subtract)
                    ins.then_inc(tr.freed(step), 1)
                elif kind == "weights" and step[1:] in lo_dve.n:
                    g, q = step[1:]
                    n = quarters.n[(g, q)]
                    dve.wait_ge(s_whi, n + 1)
                    width = GROUPS[g][1]
                    for j in range(KQ):
                        slot = (slice(None), n % RING, j, slice(0, width))
                        raw, hi = w_raw[:, n % RAW, j, 0:width], w_hi[slot].bitcast(F32)
                        ins = dve.tensor_tensor(w_lo[slot], raw, hi, ALU.subtract)
                    ins.then_inc(s_wlo_dve, 1)
                elif kind == "proj":
                    g, t = u = step[1:]
                    if t == META:
                        dve.wait_ge(s_mlow, metas.at(g))
                        dve.tensor_tensor(meta_of(g), meta_of(g), bank[pj.bank[u]][0:NMETA, :], ALU.add)\
                            .then_inc(pj.freed(u), 1)
                    if g == "hq":
                        silu(u, hqT[:, t, :])
                    elif g in ("iq", "ak", "aq"):
                        r = rows_of(t)
                        pj.wait_freed(dve, u)
                        v = rows[0:r, ropes.n[u] % 2, :].rearrange("p (h a two k) -> p h a two k", h=HEADS, a=4, two=2)
                        rot, rev = v[:, :, 0, :, :], v[:, :, 0, ::-1, :]
                        shape = [r, HEADS, 2, 8]
                        c = cos[0:r, t, :].rearrange("p (o two k) -> p o two k", o=1, two=2).broadcast_to(shape)
                        sn = sin[0:r, t, :].rearrange("p (o two k) -> p o two k", o=1, two=2).broadcast_to(shape)
                        if ropes.n[u]:
                            dve.wait_ge(s_rope, ropes.n[u])
                        tmp = swapped[0:r, :].rearrange("p (h two k) -> p h two k", h=HEADS, two=2)
                        rope(rot, rev, c, sn, tmp).then_inc(s_rope, 1)
                    elif g in ("o0", "o1"):
                        half = int(g == "o1")
                        pj.wait_full(dve, u)
                        dve.wait_ge(s_xres[half][t], 16)
                        yt = y[half][:, t, :]
                        dve.tensor_tensor(yt, yt, bank[pj.bank[u]][:, :], ALU.add).then_inc(pj.freed(u), 1)
                elif kind == "silu":
                    _, g, t = step
                    silu((g, t), (mixH if g == "hg" else mixA)[:, t, :])
                elif kind == "gate f":
                    t = step[1]
                    r = rows_of(t)
                    z = temp_of(("hf", t))
                    if t == META:
                        dve.wait_ge(s_mtanh, 1)
                    else:
                        pj.wait_freed(dve, ("hf", t))
                    link(dve.tensor_tensor(z, z, half_span[0:r, :], ALU.mult))
                    link(dve.tensor_tensor(f_of(t), z, middle[0:r, :], ALU.add))
                    dve.tensor_scalar(hk[0:r, t, :], f_of(t), -1.0, 1.0, ALU.mult, ALU.add).then_inc(s_fk, 1)
                elif kind == "ikT":
                    dve.wait_ge(s_staged, 48)
                    dve.tensor_copy(kept[:, :, :].rearrange("p j t -> p (j t)"), staged[:, 1152:1152 + 6 * P])\
                        .then_inc(s_kept, 1)
                    dve.wait_ge(s_rot, 32)
                    dve.wait_ge(s_causal, 16)
                    tr.wait_freed(dve, step)
                    key, two, sq = ik_row[:, :, 0:64], ik_two[:, :, 0, :], ik_two[:, :, 1, :]
                    per_tile = [P, TILES, 64]
                    link(dve.tensor_reduce(ik_mean, key, AX.X, ALU.add))
                    link(dve.tensor_scalar(ik_mean, ik_mean, 1.0 / 64, None, ALU.mult))
                    link(dve.tensor_tensor(two, key, over_heads(ik_mean, TILES, 64), ALU.subtract))
                    link(dve.tensor_tensor(sq, two, two, ALU.mult))
                    dve.tensor_reduce(ik_var, sq, AX.X, ALU.add).then_inc(s_ikvar, 1)
                    link(dve.tensor_scalar(idxw[:, :, :], ik_row[:, :, 64:72], IDX_SCALE, None, ALU.mult))
                    dve.wait_ge(s_ikrs, 1)
                    dve.wait_ge(s_idxg, 32)
                    gain = idx_gb[:, 0:1, :].broadcast_to(per_tile)
                    shift = idx_gb[:, 1:2, :].broadcast_to(per_tile)
                    link(dve.tensor_tensor(two, two, over_heads(ik_rs, TILES, 64), ALU.mult))
                    link(dve.tensor_tensor(two, two, gain, ALU.mult))
                    link(dve.tensor_tensor(two, two, shift, ALU.add))
                    v = two.rearrange("p t (a two k) -> p t a two k", a=4, two=2)
                    as_pairs = lambda ap: ap.rearrange("p t (two k) -> p t two k", two=2)
                    link(rope(v[:, :, 0, :, :], v[:, :, 0, ::-1, :], as_pairs(cos[:, 0:TILES, :]),
                              as_pairs(sin[:, 0:TILES, :]),
                              swapped[:, 0:64].rearrange("p (t two k) -> p t two k", t=TILES, two=2)))
                    dve.tensor_copy(sq, two).then_inc(s_iktwo, 1)
                elif kind == "kiT":
                    dve.wait_ge(s_turned, turned.at(step))
                    dve.tensor_tensor(ki_lo[:, :], bank[tr.bank[step]][:, :], ki_hi[:, :].bitcast(F32), ALU.subtract)\
                        .then_inc(tr.freed(step), 1)
                elif kind == "ropeT" and step[2] != META:
                    _, g, t = step
                    b4 = bank[tr.bank[step]][:, :].rearrange("p (j t) -> p j t", j=4)
                    dve.wait_ge(s_turned, turned.at(step))
                    for e, own, other in SIDES:
                        if g == "iq":
                            at = (slice(None), slice((t - 1) * P, t * P))
                            low, high = qi_pair[e][(other,) + at], qi_pair[e][(own,) + at]
                        elif g == "aq":
                            low, high = q_two[other, :, e, cols_of(t)], q_two[own, :, e, cols_of(t)]
                        else:
                            low, high = k_lo[own, :, cols_of(t)], k_two[own, :, e, cols_of(t)]
                        ins = dve.tensor_tensor(low, b4[own, :, :], high.bitcast(F32), ALU.subtract)
                    ins.then_inc(tr.freed(step), 1)
                elif kind == "index":
                    _, b, h = step
                    n = rels.n[(b, h)]
                    w = (b + 1) * P
                    wgt = idxw[:, b, h:h + 1]
                    sd.wait_freed(dve, step)
                    if h == 0:
                        dve.tensor_scalar(bias[b][:, :], rel[:, n % 2, 0:w], wgt, None, ALU.mult).then_inc(s_acc, 1)
                    else:
                        dve.wait_ge(s_acc, n)
                        dve.scalar_tensor_tensor(out=bias[b][:, :], in0=rel[:, n % 2, 0:w], scalar=wgt, in1=bias[b][:, :],
                                                 op0=ALU.mult, op1=ALU.add).then_inc(s_acc, 1)
                    if h == 7:
                        dve.wait_ge(s_acc, n + 1)
                        diag = bias[b][:, b * P:w]
                        last_round[b] = mark(dve.tensor_tensor(diag, diag, bias[0][:, :], ALU.add))
                elif kind == "find":
                    b = step[2]
                    dve.wait_ge(s_v, last_round[b])
                    last_round[b] = mark(dve.max(top8[:, b, :], bias[b][:, :]))
                elif kind == "take":
                    b = step[2]
                    dve.wait_ge(s_v, last_round[b])
                    last_round[b] = mark(dve.match_replace(bias[b][:, :], top8[:, b, :], bias[b][:, :], TAKEN))
                elif kind == "biases":
                    for b in range(1, TILES):
                        dve.wait_ge(s_v, last_round[b])
                        last_round[b] = mark(dve.tensor_scalar(bias[b][:, :], bias[b][:, :], 0.5 * TAKEN, NEG,
                                                               ALU.is_gt, ALU.mult))
                elif kind == "gate":
                    _, t, hp, l = step
                    for i in range(2):
                        sd.wait_freed(dve, ("decay", t, hp, int(l >= 4), i))
                    tr.wait_freed(dve, ("kT", t))
                    pair = slice(2 * hp, 2 * hp + 2)
                    keys, queries = hkT[:, pair, :], hqT[:, pair, t * P:(t + 1) * P]
                    if l == INF_LEVEL:
                        if hp == 0 and t:
                            mi.wait_full(dve, ("out", t - 1))
                        dve.tensor_copy(decay_end[:, t % 2, pair], E[:, INF_LEVEL, :, P - 1])
                        dve.tensor_tensor(q_inf[:, pair, :], E[:, INF_LEVEL, :, :], queries, ALU.mult).then_inc(s_gated, 1)
                    else:
                        def halves(ap):
                            return ap.rearrange("p h (b two m) -> p h b two m", two=2, m=1 << l)
                        e = halves(E[:, l, :, :])
                        for side, z in ((0, keys), (1, queries)):
                            ins = dve.tensor_tensor(e[:, :, :, side, :], e[:, :, :, side, :],
                                                    halves(z)[:, :, :, side, :], ALU.mult)
                        ins.then_inc(s_gated, 1)
                elif kind == "piece" and step[3] != 1:
                    _, t, hp, j = step
                    pair = slice(2 * hp, 2 * hp + 2)
                    if (t, hp, j) == (0, 0, 0):
                        dve.wait_ge(s_azero, 1)
                        dve.wait_ge(s_kept, 1)
                    if j == 0 and hp == 0 and t:
                        mi.wait_full(dve, ("out", t - 1))
                    src = bank[mi.bank[step]][:, 0:2 * P].rearrange("p (h t) -> p h t", h=2)
                    mi.wait_full(dve, step)
                    if j:
                        mi.wait_freed(dve, ("piece", t, hp, j - 1))
                    dve.copy_predicated(A[:, pair, :], kept[:, max(j - 1, 0):max(j, 1), :].broadcast_to([P, 2, P]),
                                        src).then_inc(mi.freed(step), 1)
                elif kind == "suffix":
                    t = step[1]
                    r = rows_of(t)
                    mi.wait_freed(dve, step)
                    dve.tensor_tensor(k_end[0:r, :], k_end[0:r, :], hk[0:r, t, :], ALU.mult).then_inc(s_kend, 1)
                elif kind == "state":
                    t = step[1]
                    mi.wait_full(dve, step)
                    if t == META:
                        dve.tensor_copy(S[:, :, :], bank[6][:, :].rearrange("p (h v) -> p h v", h=GH))\
                            .then_inc(mi.freed(step), 1)
                    else:
                        mi.wait_full(dve, ("out", t))
                        for h in range(GH):
                            ins = dve.scalar_tensor_tensor(out=S[:, h, :], in0=S[:, h, :],
                                                           scalar=decay_end[:, t % 2, h:h + 1],
                                                           in1=bank[6][:, h * GK:(h + 1) * GK],
                                                           op0=ALU.mult, op1=ALU.add)
                        ins.then_inc(mi.freed(step), 1)
                elif kind == "mixH":
                    t = step[1]
                    dve.wait_ge(s_ors, mixHs.at(t))
                    o4 = o_row[:, :].rearrange("p (h v) -> p h v", h=GH)
                    link(dve.tensor_tensor(o4, o4, over_heads(rs_h, GH, GK), ALU.mult))
                    dve.wait_ge(s_gate, t + 1)
                    dve.scalar_tensor_tensor(out=mixH[:, t, :], in0=mixH[:, t, :], scalar=0.5, in1=o_row[:, :],
                                             op0=ALU.mult, op1=ALU.mult).then_inc(s_mixH, 1)
                elif kind == "meta":
                    b = step[1]
                    mi.wait_freed(dve, step)
                    link(dve.tensor_reduce(mmax[b % 2], pm[:, b % 2, :].rearrange("p (h m) -> p h m", h=HEADS), AX.X, ALU.max))
                elif kind == "score":
                    _, b, h = step
                    w = (b + 1) * P
                    sd.wait_full(dve, step)
                    if scores.n[(b, h)] >= PROBS:
                        tr.wait_full(dve, ("probT",) + scores.keys[scores.n[(b, h)] - PROBS])
                    dve.tensor_tensor_reduce(prob[:, h % PROBS, 0:w], bank[sd.bank[step]][:, 0:w], bias[b][:, :], 1.0,
                                             mmax[b % 2][:, h:h + 1], ALU.add, ALU.max, pmax[b % 2][:, h:h + 1])\
                        .then_inc(sd.freed(step), 1)
                    sd.wait_freed(dve, step)
                    dve.tensor_scalar(nmax[b % 2][:, h:h + 1], pmax[b % 2][:, h:h + 1], -ATTN_SCALE, None, ALU.mult)\
                        .then_inc(s_nmax, 1)
                elif kind == "pmeta":
                    half = step[1] % 2
                    pm3 = pm[:, half, :].rearrange("p (h m) -> p h m", h=HEADS)
                    dve.tensor_tensor(pm3, pm3, over_heads(pmax[half], HEADS, NMETA), ALU.subtract).then_inc(s_pmsub, 1)
                elif kind == "metaT":
                    b = step[1]
                    dve.wait_ge(s_pmexp, pmetas.at(b))
                    dve.wait_ge(s_exp, scores.at((b, HEADS - 1)))
                    link(dve.tensor_reduce(msum, pm[:, b % 2, :].rearrange("p (h m) -> p h m", h=HEADS), AX.X, ALU.add))
                    link(dve.tensor_tensor(msum, msum, psums[b % 2], ALU.add))
                    link(dve.reciprocal(prec, msum))
                elif kind == "attn":
                    b = step[1]
                    mi.wait_full(dve, step)
                    dve.tensor_tensor(attn_row.rearrange("p (h d) -> p h d", h=HEADS),
                                      bank[7][:, :].rearrange("p (h d) -> p h d", h=HEADS), over_heads(prec), ALU.mult)\
                        .then_inc(mi.freed(step), 1)
                elif kind == "mixA":
                    b = step[1]
                    dve.wait_ge(s_ars, attns.at(b))
                    dve.wait_ge(s_gate, TILES + b + 1)
                    dve.scalar_tensor_tensor(out=mixA[:, b, :], in0=attn_row, scalar=rs_a, in1=mixA[:, b, :],
                                             op0=ALU.mult, op1=ALU.mult).then_inc(s_mixA, 1)
                elif kind == "final":
                    t = step[1]
                    second = y[1][:, t, :]
                    dve.wait_ge(s_half, t + 1)
                    pj.wait_freed(dve, ("o1", t))
                    if finals.n[t]:
                        dve.wait_ge(s_ysq, finals.n[t])
                    dve.tensor_tensor_reduce(rows[:, 1, :], second, second, 1.0, ms_f[:, 0, t:t + 1], ALU.mult, ALU.add,
                                             ms_f[:, 1, t:t + 1]).then_inc(s_ysq, 1)
                    dve.wait_ge(s_yrs, finals.at(t))
                    dve.wait_ge(s_fb, 16)
                    dve.scalar_tensor_tensor(out=second, in0=second, scalar=rs_f[:, t:t + 1], in1=fb[:, 512:D],
                                             op0=ALU.mult, op1=ALU.mult).then_inc(s_second, 1)

        @block.tensor
        def _(pe):
            pe.wait_ge(s_ident, 16)
            ready = set()

            def transposes(step, sources, width=P):
                b = bank[tr.bank[step]]
                tr.wait_free(pe, step)
                for i, src in enumerate(sources):
                    r, c = src.shape
                    ins = pe.transpose(b[0:c, width * i:width * i + r], src, ident[0:r, 0:r])
                ins.then_inc(full["tr"], 1)

            def project(u, k):
                g, t = u
                r = P if g == "hq" else rows_of(t)
                width = GROUPS[g][1]
                n0 = quarters.n[(g, 0)]
                cols = slice(0, SEQ) if g in ("hq", "ikw") else cols_of(t)
                b = bank[pj.bank[u]]
                if k == 0:
                    if g in ("o0", "o1"):
                        tr.wait_freed(pe, ("mixT", t, 1))
                    else:
                        for tt in ([0, 1, 2, 3] if g in ("hq", "ikw") else [t]):
                            tr.wait_freed(pe, ("hT", tt, 0))
                    pj.wait_free(pe, u)
                last_unit = u[1] == GROUPS[g][2][-1]
                if k == KC // 2 and g in ("o0", "o1"):
                    tr.wait_freed(pe, ("mixT", t, 0))
                elif k == KC // 2:
                    for tt in ([0, 1, 2, 3] if g in ("hq", "ikw") else [t]):
                        tr.wait_freed(pe, ("hT", tt, 1))
                q, j = divmod(k, KQ)
                slot = (n0 + q) % RING
                if (g, q) not in ready:
                    wait_lo(pe, (g, q))
                    ready.add((g, q))
                row = row_chunk(g, k)
                m_hi, m_lo = w_hi[:, slot, j, 0:width], w_lo[:, slot, j, 0:width]
                if t == META:
                    wide = (b[0:META_LO + NMETA, 0:512], hT_meta[:, k, :], m_hi)
                    narrow = (b[0:NMETA, 0:512], hT_meta[:, k, 0:NMETA], m_lo)
                    for i, (dst, a, m) in enumerate([narrow, wide] if k else [wide, narrow]):
                        ins = pe.matmul(dst, a, m, start=(k == 0 and i == 0), stop=(k == KC - 1 and i == 1))
                else:
                    h_hi, h_lo = hT_hi[:, row, cols], hT_lo[:, row, cols]
                    if g == "hq":
                        c = slice(t * P, (t + 1) * P)
                        pairs = [(m_hi[:, c], h_hi), (m_hi[:, c], h_lo), (m_lo[:, c], h_hi)]
                    elif g == "ikw":
                        pairs = [(m_hi, h_hi), (m_hi, h_lo), (m_lo, h_hi)]
                    else:
                        pairs = [(h_hi, m_hi), (h_hi, m_lo), (h_lo, m_hi)]
                    dst = b[0:IKW, :] if g == "ikw" else b[0:r, 0:512]
                    for i, (a, m) in enumerate(pairs):
                        ins = pe.matmul(dst, a, m, start=(k == 0 and i == 0), stop=(k == KC - 1 and i == 2))
                if k == KC - 1:
                    ins.then_inc(full["pj"], 1)
                elif last_unit and j == KQ - 1:
                    ins.then_inc(s_wused, 1)

            def head_scores(step, q_both, q_high, k_high, k_low):
                dst = bank[sd.bank[step]][:, 0:k_high.shape[1]]
                pe.matmul(dst, q_both, k_high, start=True, stop=False)
                pe.matmul(dst, q_high, k_low, start=False, stop=True).then_inc(full["sd"], 1)

            for step, part in TENSOR_ORDER:
                kind = step[0]
                if kind == "hT":
                    _, t, half = step
                    r = rows_of(t)
                    pe.wait_ge(s_xn, norms.at(t))
                    transposes(step, [x_t[0:r, norms.n[t] % 3, k * P:(k + 1) * P] for k in range(4 * half, 4 * half + 4)])
                elif kind == "proj":
                    project(step[1:], part)
                elif kind == "ikT":
                    pj.wait_freed(pe, ("ikw", 0))
                    transposes(step, [ikT[0:IKW, t * P:(t + 1) * P] for t in range(TILES)], IKW)
                elif kind == "kiT":
                    pe.wait_ge(s_iktwo, 1)
                    transposes(step, [ik_two[:, t, :, :].rearrange("p two d -> p (two d)") for t in range(TILES)])
                elif kind == "ropeT":
                    _, g, t = step
                    r = rows_of(t)
                    pe.wait_ge(s_rope, ropes.at((g, t)))
                    transposes(step, [rows[0:r, ropes.n[(g, t)] % 2, j * P:(j + 1) * P] for j in range(4)])
                elif kind == "kT":
                    t = step[1]
                    pe.wait_ge(s_fk, hfs.at(t))
                    transposes(step, [hk[:, t, j * P:(j + 1) * P] for j in range(4)])
                elif kind == "index":
                    _, b, h = step
                    sd.wait_free(pe, step)
                    tr.wait_freed(pe, ("ropeT", "iq", b))
                    tr.wait_freed(pe, ("kiT",))
                    w = (b + 1) * P
                    e, own, _ = SIDES[h % 2]
                    q = qi_pair[e][:, h // 2, (b - 1) * P:b * P]
                    head_scores(step, q, q[own, :], ki_hi[:, 0:w], ki_lo[own, 0:w])
                elif kind == "decay":
                    _, t, hp, half = step
                    pe.wait_ge(s_glo, hfs.at(t))
                    m = sums[:, 4 * half:4 * half + 4, :].rearrange("p l t -> p (l t)")
                    for i in range(2):
                        key = step + (i,)
                        c = slice((2 * hp + i) * GK, (2 * hp + i + 1) * GK)
                        sd.wait_free(pe, key)
                        b = bank[sd.bank[key]]
                        pe.matmul(b[:, :], g_hi[:, t, c], m, start=True, stop=False)
                        pe.matmul(b[:, :], g_lo[:, t, c], m, start=False, stop=True).then_inc(full["sd"], 1)
                elif kind == "suffix":
                    t = step[1]
                    r = rows_of(t)
                    pe.wait_ge(s_glo, hfs.at(t))
                    mi.wait_free(pe, step)
                    pe.matmul(bank[6][0:r, :], after[0:r, 0:r], g_hi[0:r, t, :], start=True, stop=False)
                    pe.matmul(bank[6][0:r, :], after[0:r, 0:r], g_lo[0:r, t, :], start=False, stop=True)\
                        .then_inc(full["mi"], 1)
                elif kind == "state":
                    t = step[1]
                    r = rows_of(t)
                    pe.wait_ge(s_kend, suffixes.at(t))
                    pj.wait_freed(pe, ("hi", t))
                    mi.wait_free(pe, step)
                    for h in range(GH):
                        c = slice(h * GK, (h + 1) * GK)
                        ins = pe.matmul(bank[6][:, c], k_end[0:r, c], hv[0:r, t, c], start=True, stop=True)
                    ins.then_inc(full["mi"], 1)
                elif kind == "piece":
                    _, t, hp, j = step
                    b = bank[mi.bank[step]]
                    mi.wait_free(pe, step)
                    if j == 0:
                        tr.wait_freed(pe, ("kT", t))
                        for h in (2 * hp, 2 * hp + 1):
                            pj.wait_freed(pe, ("hq", h))
                    else:
                        pe.wait_ge(s_gated, gates.at((t, hp, 5 if j == 1 else 6 - j)))
                    for i in range(2):
                        h = 2 * hp + i
                        if j == 0:
                            ins = pe.matmul(b[:, i * P:(i + 1) * P], hkT[:, h, :], hqT[:, h, t * P:(t + 1) * P],
                                            start=True, stop=True)
                        elif j == 1:
                            for s0, s1, t0, t1 in BLOCKS:
                                e = E[:, 6 if s1 == 64 else 5, i, :]
                                ins = pe.matmul(b[s0:s1, i * P + t0:i * P + t1], e[:, s0:s1], e[:, t0:t1],
                                                start=True, stop=True)
                        else:
                            e = E[:, 6 - j, i, :]
                            ins = pe.matmul(b[:, i * P:(i + 1) * P], e, e, start=True, stop=True)
                    ins.then_inc(full["mi"], 1)
                elif kind == "out":
                    t = step[1]
                    pe.wait_ge(s_gated, gates.at((t, 1, INF_LEVEL)))
                    mi.wait_freed(pe, ("piece", t, 1, PIECES - 1))
                    prev = states.keys[outs.n[t]]
                    mi.wait_freed(pe, ("state", prev))
                    mi.wait_free(pe, step)
                    for h in range(GH):
                        c = slice(h * GK, (h + 1) * GK)
                        pe.matmul(bank[7][:, c], A[:, h, :], hv[:, t, c], start=True, stop=False)
                        ins = pe.matmul(bank[7][:, c], q_inf[:, h, :], S[:, h, :], start=False, stop=True)
                    ins.then_inc(full["mi"], 1)
                elif kind == "meta":
                    b = step[1]
                    tr.wait_freed(pe, ("ropeT", "ak", META))
                    tr.wait_freed(pe, ("ropeT", "aq", b))
                    mi.wait_free(pe, step)
                    for h in range(HEADS):
                        q = q_two[:, h // 2, h % 2, cols_of(b)].bitcast(F32)
                        ins = pe.matmul(bank[6][:, NMETA * h:NMETA * (h + 1)], q, km_two[:, h // 2, h % 2, :],
                                        start=True, stop=True)
                    ins.then_inc(full["mi"], 1)
                elif kind == "score":
                    _, b, h = step
                    sd.wait_free(pe, step)
                    w = max(b + 1, 2) * P
                    tr.wait_freed(pe, ("ropeT", "ak", max(b, 1)))
                    e, own, _ = SIDES[h % 2]
                    q = q_two[:, h // 2, e, cols_of(b)]
                    head_scores(step, q, q[own, :], k_two[:, h // 2, e, 0:w], k_lo[own, h // 2, 0:w])
                elif kind == "probT":
                    _, b, h = step
                    pe.wait_ge(s_exp, scores.at((b, h)))
                    transposes(step, [prob[:, h % PROBS, j * P:(j + 1) * P] for j in range(b + 1)])
                elif kind == "pv":
                    _, b, h = step
                    n = probTs.n[(b, h)]
                    tr.wait_freed(pe, ("probT", b, h))
                    if h == 0:
                        mi.wait_free(pe, ("attn", b))
                        for t in range(b + 1):
                            pj.wait_freed(pe, ("av", t))
                    c = slice(h * HD, (h + 1) * HD)
                    for j in range(b + 1):
                        ins = pe.matmul(bank[7][:, c], probT[:, n % 2, j * P:(j + 1) * P], V[:, j, c],
                                        start=(h == 0 and j == 0), stop=False, skip_group_check=True)
                    ins.then_inc(s_pv, 1)
                elif kind == "metaT":
                    b = step[1]
                    pe.wait_ge(s_pmexp, pmetas.at(b))
                    transposes(step, [pm[:, b % 2, :]])
                elif kind == "attn":
                    b = step[1]
                    tr.wait_freed(pe, ("metaT", b))
                    pe.wait_ge(s_vmeta, 16 * HEADS)
                    pe.matmul(bank[7][:, :], pmT[:, :], V_meta[:, :], start=False, stop=True, skip_group_check=True)\
                        .then_inc(full["mi"], 1)
                elif kind == "mixT":
                    _, t, half = step
                    if half == 0:
                        pe.wait_ge(s_mixA, attns.at(t))
                    else:
                        pe.wait_ge(s_mixH, mixHs.at(t))
                    src = mixH if half else mixA
                    transposes(step, [src[:, t, j * P:(j + 1) * P] for j in range(4)])


def program(nc, arrays, out_shape):
    aps = []
    for name, a in arrays.items():
        aps.append(nc.dram_tensor(name, a.shape, mybir.dt.from_np(a.dtype), kind="ExternalInput").ap())
    aps.append(nc.dram_tensor("out_0_dram", out_shape, F32, kind="ExternalOutput").ap())
    hymba_layer(nc, *aps)


_INS = ["x", "meta_tokens", "mix_norm", "w_in", "idx_k_norm_g", "idx_k_norm_b", "attn_out_norm",
        "hgrn_lb_logits", "hgrn_out_norm", "w_out", "final_norm"]


def kernel(**inputs):
    import concourse.bacc as bacc
    from concourse.bass_utils import run_bass_kernel_spmd

    nc = bacc.Bacc("TRN2", target_bir_lowering=False, num_devices=1)
    arrays = {f"in_{n}": np.ascontiguousarray(inputs[n]) for n in _INS}
    sums, after, kept = level_tables()
    cos, sin = rope_tables()
    causal = np.where(np.arange(P)[None, :] <= np.arange(P)[:, None], 0.0, NEG).astype(np.float32)
    arrays |= {"t_ident": np.eye(P, dtype=np.float32), "t_cos": cos, "t_sin": sin,
               "t_sums": sums.reshape(P, -1), "t_after": after, "t_kept": kept, "t_causal": causal}
    program(nc, arrays, inputs["x"].shape)
    r = run_bass_kernel_spmd(nc, [arrays], core_ids=[0])
    return r.results[0]["out_0_dram"]
```
